# Optimizing a Trainium2 kernel written in Bass

```python
import math
import jax, jax.numpy as jnp
from jax import lax
import numpy as np

D_MODEL = 1024
BATCH = 1
SEQ = 256
DEPTH = 2

MLA_HEADS = 8
MLA_NOPE = 64
MLA_ROPE = 32
MLA_QK = MLA_NOPE + MLA_ROPE
MLA_V = 64
Q_LORA = 384
KV_LORA = 256
ROPE_THETA = 10000.0
Q_BLOCK = 128
MLA_WIDTH = MLA_HEADS * MLA_V

HG_HEADS = 4
HG_DK = 128
HG_DV = 128
HG_CHUNK = 32
HG_KW = HG_HEADS * HG_DK
HG_WIDTH = HG_HEADS * HG_DV

D_FF = -(-8 * D_MODEL // (3 * 256)) * 256

NORM_EPS = 1e-6

IN_SPLITS = (Q_LORA, KV_LORA, MLA_ROPE, HG_KW, HG_KW, HG_WIDTH, HG_WIDTH, D_MODEL, D_MODEL)
D_IN = sum(IN_SPLITS)


def rms_norm(x, g):
    xf = x.astype(jnp.float32)
    y = xf * lax.rsqrt(jnp.mean(xf * xf, axis=-1, keepdims=True) + NORM_EPS)
    return (y * g.astype(jnp.float32)).astype(x.dtype)

def rope_tables(seq):
    pos = jnp.arange(seq, dtype=jnp.float32)
    inv_freq = 1.0 / (ROPE_THETA ** (jnp.arange(0, MLA_ROPE, 2, dtype=jnp.float32) / MLA_ROPE))
    ang = pos[:, None] * inv_freq[None, :]
    return jnp.cos(ang), jnp.sin(ang)

def apply_rope(x, cos, sin):
    half = x.shape[-1] // 2
    xf = x.astype(jnp.float32)
    x1, x2 = xf[..., :half], xf[..., half:]
    return jnp.concatenate([x1 * cos - x2 * sin, x1 * sin + x2 * cos], axis=-1).astype(x.dtype)

def mla_mixer(c_q, c_kv, k_pe, norm_cq, w_uq, norm_ckv, w_ukv, q_norm, k_norm, cos, sin):
    B, T, _ = c_q.shape
    q = (rms_norm(c_q, norm_cq) @ w_uq).reshape(B, T, MLA_HEADS, MLA_QK)
    kv = (rms_norm(c_kv, norm_ckv) @ w_ukv).reshape(B, T, MLA_HEADS, MLA_NOPE + MLA_V)
    k_nope, v = kv[..., :MLA_NOPE], kv[..., MLA_NOPE:]
    k = jnp.concatenate([k_nope, jnp.broadcast_to(k_pe[:, :, None, :], (B, T, MLA_HEADS, MLA_ROPE))], axis=-1)
    q = rms_norm(q, q_norm)
    k = rms_norm(k, k_norm)
    c, s = cos[:, None, :], sin[:, None, :]
    q = jnp.concatenate([q[..., :MLA_NOPE], apply_rope(q[..., MLA_NOPE:], c, s)], axis=-1)
    k = jnp.concatenate([k[..., :MLA_NOPE], apply_rope(k[..., MLA_NOPE:], c, s)], axis=-1)
    scale = MLA_QK ** -0.5
    outs = []
    for blk in range(T // Q_BLOCK):
        s0 = blk * Q_BLOCK
        s1 = s0 + Q_BLOCK
        qb, kb, vb = q[:, s0:s1], k[:, :s1], v[:, :s1]
        logits = jnp.einsum('bqhd,bkhd->bhqk', qb, kb).astype(jnp.float32) * scale
        mask = (s0 + jnp.arange(Q_BLOCK))[:, None] >= jnp.arange(s1)[None, :]
        logits = jnp.where(mask, logits, -jnp.inf)
        p = jax.nn.softmax(logits, axis=-1).astype(v.dtype)
        outs.append(jnp.einsum('bhqk,bkhd->bqhd', p, vb))
    return jnp.concatenate(outs, axis=1).reshape(B, T, MLA_WIDTH)

def hgrn2_mixer(q, f_logit, i, g, lb, out_norm):
    B, T, _ = q.shape
    N, C = T // HG_CHUNK, HG_CHUNK
    lbf = lb.astype(jnp.float32)
    log_f = jnp.logaddexp(jnp.log(lbf), jnp.log1p(-lbf) + jax.nn.log_sigmoid(f_logit.astype(jnp.float32)))
    k = -jnp.expm1(log_f)

    def to_chunks(a, d):
        return a.astype(jnp.float32).reshape(B, N, C, HG_HEADS, d).transpose(1, 0, 3, 2, 4)

    qc = to_chunks(q, HG_DK)
    kc = to_chunks(k, HG_DK)
    vc = to_chunks(i, HG_DV)
    bc = jnp.cumsum(to_chunks(log_f, HG_DK), axis=3)
    causal = jnp.arange(C)[:, None] >= jnp.arange(C)[None, :]

    def step(S, inp):
        qx, kx, vx, bx = inp
        b_last = bx[:, :, -1:, :]
        o_inter = jnp.einsum('bhck,bhkv->bhcv', qx * jnp.exp(bx), S)
        diff = bx[:, :, :, None, :] - bx[:, :, None, :, :]
        decay = jnp.exp(jnp.where(causal[:, :, None], diff, -jnp.inf))
        A = jnp.einsum('bhtk,bhsk,bhtsk->bhts', qx, kx, decay)
        o_intra = jnp.einsum('bhts,bhsv->bhtv', A, vx)
        S_new = jnp.exp(b_last[:, :, 0, :])[..., None] * S + jnp.einsum('bhsk,bhsv->bhkv', kx * jnp.exp(b_last - bx), vx)
        return S_new, o_inter + o_intra

    S0 = jnp.zeros((B, HG_HEADS, HG_DK, HG_DV), jnp.float32)
    _, o = lax.scan(step, S0, (qc, kc, vc, bc))
    o = o.transpose(1, 0, 3, 2, 4).reshape(B, T, HG_HEADS, HG_DV).astype(q.dtype)
    o = rms_norm(o, out_norm) * jax.nn.silu(g.reshape(B, T, HG_HEADS, HG_DV))
    return o.reshape(B, T, HG_WIDTH)

def first_inputs(seed: int = 0) -> dict:
    key = jax.random.key(seed)
    ks = jax.random.split(key, 20)

    def w(k, shape, fan_in):
        return jax.random.normal(k, shape, jnp.float32) * fan_in ** -0.5

    def gain(k, shape):
        return 1.0 + 0.02 * jax.random.normal(k, shape, jnp.float32)

    L = DEPTH
    return {
        "x": jax.random.normal(ks[0], (BATCH, SEQ, D_MODEL), jnp.float32),
        "norm_mix": gain(ks[1], (L, D_MODEL)),
        "w_in": w(ks[2], (L, D_MODEL, D_IN), D_MODEL),
        "mla_norm_cq": gain(ks[3], (L, Q_LORA)),
        "mla_w_uq": w(ks[4], (L, Q_LORA, MLA_HEADS * MLA_QK), Q_LORA),
        "mla_norm_ckv": gain(ks[5], (L, KV_LORA)),
        "mla_w_ukv": w(ks[6], (L, KV_LORA, MLA_HEADS * (MLA_NOPE + MLA_V)), KV_LORA),
        "mla_q_norm": gain(ks[7], (L, MLA_QK)),
        "mla_k_norm": gain(ks[8], (L, MLA_QK)),
        "hg_lb_logits": 0.5 * jax.random.normal(ks[9], (L, HG_KW), jnp.float32),
        "hg_out_norm": gain(ks[10], (L, HG_DV)),
        "w_proj_a": w(ks[11], (L, MLA_WIDTH, D_MODEL), MLA_WIDTH),
        "w_proj_b": w(ks[12], (L, HG_WIDTH, D_MODEL), HG_WIDTH),
        "w_out": w(ks[13], (L, D_MODEL, D_MODEL), D_MODEL),
        "norm_ffn": gain(ks[14], (L, D_MODEL)),
        "w_gate": w(ks[15], (L, D_MODEL, D_FF), D_MODEL),
        "w_up": w(ks[16], (L, D_MODEL, D_FF), D_MODEL),
        "w_down": w(ks[17], (L, D_FF, D_MODEL), D_FF),
    }

def first_block(x, norm_mix, w_in, mla_norm_cq, mla_w_uq, mla_norm_ckv, mla_w_ukv, mla_q_norm, mla_k_norm,
              hg_lb_logits, hg_out_norm, w_proj_a, w_proj_b, w_out, norm_ffn, w_gate, w_up, w_down):
    T = x.shape[1]
    cos, sin = rope_tables(T)
    p = jax.nn.softmax(hg_lb_logits.astype(jnp.float32), axis=0)
    lower_bounds = jnp.maximum(jnp.cumsum(p, axis=0) - p[0:1], 0.0)
    offsets = [int(o) for o in np.cumsum(IN_SPLITS)[:-1]]

    for l in range(DEPTH):
        h = rms_norm(x, norm_mix[l])
        z = h @ w_in[l]
        c_q, c_kv, k_pe, hq, hf, hi, hg, g_a, g_b = jnp.split(z, offsets, axis=-1)
        y_a = mla_mixer(c_q, c_kv, k_pe, mla_norm_cq[l], mla_w_uq[l], mla_norm_ckv[l], mla_w_ukv[l],
                        mla_q_norm[l], mla_k_norm[l], cos, sin) @ w_proj_a[l]
        y_b = hgrn2_mixer(hq, hf, hi, hg, lower_bounds[l], hg_out_norm[l]) @ w_proj_b[l]
        y = jax.nn.sigmoid(g_a) * y_a + jax.nn.sigmoid(g_b) * y_b
        x = x + y @ w_out[l]
        h = rms_norm(x, norm_ffn[l])
        x = x + (jax.nn.silu(h @ w_gate[l]) * (h @ w_up[l])) @ w_down[l]
    return x


HEAD_DIM = 64
N_ATTN_HEADS = 8
N_KV_HEADS = 2
GQA_GROUP = N_ATTN_HEADS // N_KV_HEADS
ATTN_WIDTH = N_ATTN_HEADS * HEAD_DIM
KV_WIDTH = N_KV_HEADS * HEAD_DIM
ROPE_DIM = HEAD_DIM // 4
ROPE_THETA_2 = 500000.0
DILATED_PATTERNS = ((128, 1), (512, 4), (2048, 16))
ATTN_BLOCK = 128

SSM_HEAD_DIM = 64
SSM_HEADS = 16
SSM_INNER = SSM_HEADS * SSM_HEAD_DIM
SSM_GROUPS = 2
D_STATE = 128
CONV_WIDTH = 4
CHUNK = 128
CONV_CH = SSM_INNER + 2 * SSM_GROUPS * D_STATE

MIX_WIDTH = ATTN_WIDTH + SSM_INNER
Q_END = ATTN_WIDTH
K_END = Q_END + KV_WIDTH
V_END = K_END + KV_WIDTH
Z_END = V_END + SSM_INNER
XBC_END = Z_END + CONV_CH
IN_PROJ = XBC_END + SSM_HEADS

FFN_HIDDEN = ((8 * D_MODEL + 3 * 256 - 1) // (3 * 256)) * 256
EPS = 1e-5


def rmsnorm(x, w):
    xf = x.astype(jnp.float32)
    y = xf * lax.rsqrt(jnp.mean(xf * xf, axis=-1, keepdims=True) + EPS)
    return (y * w.astype(jnp.float32)).astype(x.dtype)

def rotary_tables(positions, dtype):
    inv_freq = ROPE_THETA_2 ** (-jnp.arange(0, ROPE_DIM, 2, dtype=jnp.float32) / ROPE_DIM)
    ang = positions.astype(jnp.float32)[..., None] * inv_freq
    return jnp.cos(ang)[:, :, None, :].astype(dtype), jnp.sin(ang)[:, :, None, :].astype(dtype)

def partial_rotary(t, cos, sin):
    half = ROPE_DIM // 2
    t1, t2, rest = t[..., :half], t[..., half:ROPE_DIM], t[..., ROPE_DIM:]
    return jnp.concatenate([t1 * cos - t2 * sin, t2 * cos + t1 * sin, rest], axis=-1)

def dilated_window_branch(q, k, v, window, dilation):
    bsz, s = q.shape[0], q.shape[1]
    length = s // dilation
    w_d = window // dilation
    nb = -(-length // ATTN_BLOCK)
    lp = nb * ATTN_BLOCK
    qd = q.reshape((bsz, length, dilation) + q.shape[2:])
    kd = k.reshape((bsz, length, dilation) + k.shape[2:])
    vd = v.reshape((bsz, length, dilation) + v.shape[2:])
    qd = jnp.pad(qd, [(0, 0), (0, lp - length)] + [(0, 0)] * (qd.ndim - 2))
    kv_pad = [(0, 0), (ATTN_BLOCK, lp - length)] + [(0, 0)] * (kd.ndim - 2)
    kd = jnp.pad(kd, kv_pad)
    vd = jnp.pad(vd, kv_pad)
    qb = qd.reshape((bsz, nb, ATTN_BLOCK) + qd.shape[2:])
    kb = kd.reshape((bsz, nb + 1, ATTN_BLOCK) + kd.shape[2:])
    vb = vd.reshape((bsz, nb + 1, ATTN_BLOCK) + vd.shape[2:])
    kb = jnp.concatenate([kb[:, :-1], kb[:, 1:]], axis=2)
    vb = jnp.concatenate([vb[:, :-1], vb[:, 1:]], axis=2)
    scores = jnp.einsum('bnqrhgc,bnkrhc->bnrhgqk', qb, kb).astype(jnp.float32)
    qi = jnp.arange(ATTN_BLOCK)[:, None]
    ki = jnp.arange(2 * ATTN_BLOCK)[None, :]
    delta = qi + ATTN_BLOCK - ki
    kpos = jnp.arange(nb)[:, None, None] * ATTN_BLOCK - ATTN_BLOCK + ki[None]
    valid = (delta >= 0)[None] & (delta <= w_d)[None] & (kpos >= 0)
    scores = jnp.where(valid[None, :, None, None, None], scores, -jnp.inf)
    m = jnp.max(scores, axis=-1, keepdims=True)
    p = jnp.exp(scores - m)
    den = jnp.sum(p, axis=-1, keepdims=True)
    o = jnp.einsum('bnrhgqk,bnkrhc->bnrhgqc', p, vb.astype(jnp.float32)) / den
    lse = (m + jnp.log(den))[..., 0]
    o = jnp.transpose(o, (0, 1, 5, 2, 3, 4, 6)).reshape((bsz, lp, dilation) + q.shape[2:])
    lse = jnp.transpose(lse, (0, 1, 5, 2, 3, 4)).reshape((bsz, lp, dilation) + q.shape[2:4])
    o = o[:, :length].reshape(q.shape)
    lse = lse[:, :length].reshape(q.shape[:4])
    return o, lse

def dilated_attention(q, k, v):
    outs, lses = [], []
    for window, dilation in DILATED_PATTERNS:
        o, l = dilated_window_branch(q, k, v, window, dilation)
        outs.append(o)
        lses.append(l)
    wts = jax.nn.softmax(jnp.stack(lses, axis=0), axis=0)
    return jnp.einsum('ibshg,ibshgc->bshgc', wts, jnp.stack(outs, axis=0))

def causal_depthwise_conv(u, w, b):
    y = lax.conv_general_dilated(u, w[:, None, :], window_strides=(1,),
                                 padding=[(CONV_WIDTH - 1, 0)],
                                 dimension_numbers=('NWC', 'WIO', 'NWC'),
                                 feature_group_count=u.shape[-1])
    return y + b

def segsum_exp(a):
    cs = jnp.cumsum(a, axis=-1)
    diff = cs[..., :, None] - cs[..., None, :]
    t = a.shape[-1]
    mask = jnp.tril(jnp.ones((t, t), dtype=bool))
    return jnp.exp(jnp.where(mask, diff, -jnp.inf))

def ssd_chunked(xs, dt, a_neg, bm, cm):
    bsz, s, nh, hp = xs.shape
    nc = s // CHUNK
    e = nh // SSM_GROUPS
    xg = (xs.astype(jnp.float32) * dt[..., None]).reshape(bsz, nc, CHUNK, SSM_GROUPS, e, hp)
    a = jnp.transpose((dt * a_neg).reshape(bsz, nc, CHUNK, SSM_GROUPS, e), (0, 1, 3, 4, 2))
    bc = bm.astype(jnp.float32).reshape(bsz, nc, CHUNK, SSM_GROUPS, D_STATE)
    cc = cm.astype(jnp.float32).reshape(bsz, nc, CHUNK, SSM_GROUPS, D_STATE)
    a_cs = jnp.cumsum(a, axis=-1)
    cb = jnp.einsum('bclgn,bcsgn->bcgls', cc, bc)
    m_mat = cb[:, :, :, None] * segsum_exp(a)
    y_diag = jnp.einsum('bcgels,bcsgep->bclgep', m_mat, xg)
    decay_states = jnp.exp(a_cs[..., -1:] - a_cs)
    states = jnp.einsum('bclgn,bcgel,bclgep->bcgepn', bc, decay_states, xg)
    chunk_decay = jnp.exp(a_cs[..., -1])

    def step(h, inp):
        dec, st = inp
        return h * dec[..., None, None] + st, h

    h0 = jnp.zeros((bsz, SSM_GROUPS, e, hp, D_STATE), jnp.float32)
    _, prev = lax.scan(step, h0, (jnp.moveaxis(chunk_decay, 1, 0), jnp.moveaxis(states, 1, 0)))
    prev_states = jnp.moveaxis(prev, 0, 1)
    y_off = jnp.einsum('bclgn,bcgepn,bcgel->bclgep', cc, prev_states, jnp.exp(a_cs))
    return (y_diag + y_off).reshape(bsz, s, nh, hp)

def hybrid_mixer(h, w_in, conv_w, conv_b, dt_bias, a_log, d_skip, ssm_norm, w_out, cos, sin):
    bsz, s, _ = h.shape
    proj = h @ w_in
    q, k, v, z, xbc, dt = jnp.split(proj, [Q_END, K_END, V_END, Z_END, XBC_END], axis=-1)
    q = partial_rotary(q.reshape(bsz, s, N_ATTN_HEADS, HEAD_DIM), cos, sin)
    k = partial_rotary(k.reshape(bsz, s, N_KV_HEADS, HEAD_DIM), cos, sin)
    v = v.reshape(bsz, s, N_KV_HEADS, HEAD_DIM)
    q = (q * (HEAD_DIM ** -0.5)).reshape(bsz, s, N_KV_HEADS, GQA_GROUP, HEAD_DIM)
    attn = dilated_attention(q, k, v).reshape(bsz, s, ATTN_WIDTH).astype(h.dtype)
    xbc = jax.nn.silu(causal_depthwise_conv(xbc, conv_w, conv_b))
    xs, bm, cm = jnp.split(xbc, [SSM_INNER, SSM_INNER + SSM_GROUPS * D_STATE], axis=-1)
    xs = xs.reshape(bsz, s, SSM_HEADS, SSM_HEAD_DIM)
    bm = bm.reshape(bsz, s, SSM_GROUPS, D_STATE)
    cm = cm.reshape(bsz, s, SSM_GROUPS, D_STATE)
    dt = jax.nn.softplus(dt.astype(jnp.float32) + dt_bias.astype(jnp.float32))
    a_neg = -jnp.exp(a_log.astype(jnp.float32))
    y = ssd_chunked(xs, dt, a_neg, bm, cm) + d_skip.astype(jnp.float32)[:, None] * xs.astype(jnp.float32)
    y = y.reshape(bsz, s, SSM_INNER).astype(h.dtype) * jax.nn.silu(z)
    gsize = SSM_INNER // SSM_GROUPS
    y = rmsnorm(y.reshape(bsz, s, SSM_GROUPS, gsize), ssm_norm.reshape(SSM_GROUPS, gsize))
    y = y.reshape(bsz, s, SSM_INNER)
    return jnp.concatenate([attn, y], axis=-1) @ w_out

def swiglu(h, w_gate, w_up, w_down):
    return (jax.nn.silu(h @ w_gate) * (h @ w_up)) @ w_down

def second_inputs(seed: int = 0) -> dict:
    key = jax.random.key(seed)
    ks = jax.random.split(key, 16)
    f32 = jnp.float32
    x = jax.random.normal(ks[0], (BATCH, SEQ, D_MODEL), f32)
    positions = jnp.broadcast_to(jnp.arange(SEQ, dtype=jnp.int32), (BATCH, SEQ))
    norm_mix = 1.0 + 0.02 * jax.random.normal(ks[1], (DEPTH, D_MODEL), f32)
    w_in = jax.random.normal(ks[2], (DEPTH, D_MODEL, IN_PROJ), f32) * D_MODEL ** -0.5
    conv_w = jax.random.normal(ks[3], (DEPTH, CONV_WIDTH, CONV_CH), f32) * CONV_WIDTH ** -0.5
    conv_b = 0.01 * jax.random.normal(ks[4], (DEPTH, CONV_CH), f32)
    dt0 = jnp.exp(jax.random.uniform(ks[5], (DEPTH, SSM_HEADS), f32, np.log(1e-3), np.log(1e-1)))
    dt_bias = dt0 + jnp.log(-jnp.expm1(-dt0))
    a_log = jnp.log(jax.random.uniform(ks[6], (DEPTH, SSM_HEADS), f32, 1.0, 16.0))
    d_skip = 1.0 + 0.1 * jax.random.normal(ks[7], (DEPTH, SSM_HEADS), f32)
    ssm_norm = 1.0 + 0.02 * jax.random.normal(ks[8], (DEPTH, SSM_INNER), f32)
    w_out = jax.random.normal(ks[9], (DEPTH, MIX_WIDTH, D_MODEL), f32) * MIX_WIDTH ** -0.5
    norm_ffn = 1.0 + 0.02 * jax.random.normal(ks[10], (DEPTH, D_MODEL), f32)
    w_gate = jax.random.normal(ks[11], (DEPTH, D_MODEL, FFN_HIDDEN), f32) * D_MODEL ** -0.5
    w_up = jax.random.normal(ks[12], (DEPTH, D_MODEL, FFN_HIDDEN), f32) * D_MODEL ** -0.5
    w_down = jax.random.normal(ks[13], (DEPTH, FFN_HIDDEN, D_MODEL), f32) * FFN_HIDDEN ** -0.5
    final_norm = 1.0 + 0.02 * jax.random.normal(ks[14], (D_MODEL,), f32)
    return {"x": x, "positions": positions, "norm_mix": norm_mix, "w_in": w_in,
            "conv_w": conv_w, "conv_b": conv_b, "dt_bias": dt_bias, "a_log": a_log,
            "d_skip": d_skip, "ssm_norm": ssm_norm, "w_out": w_out, "norm_ffn": norm_ffn,
            "w_gate": w_gate, "w_up": w_up, "w_down": w_down, "final_norm": final_norm}

def second_block(x, positions, norm_mix, w_in, conv_w, conv_b, dt_bias, a_log, d_skip, ssm_norm,
              w_out, norm_ffn, w_gate, w_up, w_down, final_norm):
    cos, sin = rotary_tables(positions, x.dtype)
    h = x
    for layer in range(DEPTH):
        h = h + hybrid_mixer(rmsnorm(h, norm_mix[layer]), w_in[layer], conv_w[layer],
                             conv_b[layer], dt_bias[layer], a_log[layer], d_skip[layer],
                             ssm_norm[layer], w_out[layer], cos, sin)
        h = h + swiglu(rmsnorm(h, norm_ffn[layer]), w_gate[layer], w_up[layer], w_down[layer])
    return rmsnorm(h, final_norm)


def setup_inputs(seed=0):
    out = dict(first_inputs(seed))
    for name, value in second_inputs(seed + 1).items():
        if name != "x":
            out[name + "_2"] = value
    return out


def reference(
    x, norm_mix, w_in, mla_norm_cq, mla_w_uq, mla_norm_ckv, mla_w_ukv, mla_q_norm, mla_k_norm,
    hg_lb_logits, hg_out_norm, w_proj_a, w_proj_b, w_out, norm_ffn, w_gate, w_up, w_down,
    positions_2, norm_mix_2, w_in_2, conv_w_2, conv_b_2, dt_bias_2, a_log_2, d_skip_2,
    ssm_norm_2, w_out_2, norm_ffn_2, w_gate_2, w_up_2, w_down_2, final_norm_2,
):
    x = first_block(
        x, norm_mix, w_in, mla_norm_cq, mla_w_uq, mla_norm_ckv, mla_w_ukv, mla_q_norm,
        mla_k_norm, hg_lb_logits, hg_out_norm, w_proj_a, w_proj_b, w_out, norm_ffn, w_gate,
        w_up, w_down,
    )
    return second_block(
        x, positions_2, norm_mix_2, w_in_2, conv_w_2, conv_b_2, dt_bias_2, a_log_2, d_skip_2,
        ssm_norm_2, w_out_2, norm_ffn_2, w_gate_2, w_up_2, w_down_2, final_norm_2,
    )


_drawn_inputs = setup_inputs


def setup_inputs(seed=0):
    import zlib

    import numpy as np

    out = dict(_drawn_inputs(seed))
    spreads = {}
    factors = {'mla_norm_cq': 8.0,
     'mla_norm_ckv': 8.0,
     'mla_q_norm': 8.0,
     'mla_k_norm': 8.0,
     'hg_out_norm': 3.833,
     'conv_b_2': 5.426,
     'ssm_norm_2': 14.013,
     'norm_ffn_2': 3.865,
     'final_norm_2': 8.146}
    for name, (base, spread) in spreads.items():
        noise = np.random.default_rng([zlib.crc32(name.encode()), seed]).standard_normal(out[name].shape)
        drawn = base * np.exp(spread * noise) if base else spread * noise
        out[name] = __import__('jax').numpy.asarray(drawn.astype(out[name].dtype))
    for name, factor in factors.items():
        out[name] = (out[name] * factor).astype(out[name].dtype)
    return out
```

```python
import math
from contextlib import ExitStack

import numpy as np
import concourse.bass as bass
from concourse import mybir

F32 = mybir.dt.float32
F32R = mybir.dt.float32r
I32 = mybir.dt.int32
U8 = mybir.dt.uint8
ALU = mybir.AluOpType
ACT = mybir.ActivationFunctionType
AX = mybir.AxisListType

P = 128
T = 256
NT = T // P
D = 1024
KD = D // P
DEPTH = 2
FF = 2816
FW = 256
FSTEPS = FF // FW
RING = 4
SLOT = 1024

QL, KVL, RA = 384, 256, 32
HA, NOPE, DQK, DV = 8, 64, 96, 64
HG, DK = 4, 128
IN_A = 4768
EPS_A = 1e-6
HB, HKV, DB = 8, 2, 64
RB = 16
SH, SP, SI, SN = 16, 64, 1024, 128
XBC = 1536
TAPS = 4
IN_B = 3344
XD = XBC + SH
EPS_B = 1e-5

C_ID, C_TRI, C_BIASA, C_BIASB = 0, 128, 256, 640
C_COS, C_SIN, C_INV, C_END = 1024, 1056, 1088, 1096
G_CQ, G_CKV, G_QK, G_HG = 0, QL, QL + KVL, QL + KVL + 2 * DQK
G_SSM = 0
M_X, M_CQ, M_CKV, M_QK, M_HG, M_Y, M_H, RS = 0, 2, 4, 8, 40, 48, 50, 64


class Progress:

    def __init__(self, nc, ctx, name, table):
        self.sem = ctx.enter_context(nc.semaphore(name))
        self.table, self.old = table.setdefault(name, {}), dict(table.setdefault(name, {}))
        self.k, self.block, self.inner = 0, 0, None

    def per(self, block):
        return self.old.get((block, "layer"), 1)

    def body(self, block):
        return self.old.get((block, "loop"), 1)

    def seed(self):
        return self.per(0)

    def mark(self, name=None):
        self.k += 1
        if name is not None:
            self.table[self.block, name] = self.k
        return self.sem, 1

    def at(self, layer, name, j=None):
        block, l = layer
        turns = 0
        if name is None:
            k = self.k
        elif self.old:
            if name.endswith("@last"):
                name, turns = name[:-5], LOOP_TIMES - 1
            k = self.old[block, name] + turns * self.body(block)
        else:
            k = 1
        base = self.seed() + (DEPTH * self.per(0) if block else 0) + k
        value = l * self.per(block) + base
        return self.sem, value if j is None else value + j * self.body(block)

    def now(self, layer, j=None):
        return self.at(layer, None, j)

    def before(self, layer, name):
        block, l = layer
        left = [self.per(b) - self.old.get((b, name), 1) for b in (0, 1)]
        assert not self.old or left[0] == left[1], (name, left)
        return self.sem, l * self.per(block) + (self.seed() + (DEPTH * self.per(0) if block else 0) - left[0])

    def final(self, name):
        return self.sem, self.seed() + DEPTH * self.per(0) + (DEPTH - 1) * self.per(1) + self.old.get((1, name), 1)

    def loop(self, times):
        if times is None:
            self.inner = self.k
        else:
            body = self.k - self.inner
            self.table[self.block, "loop"] = body
            self.k = self.inner + times * body

    def end(self):
        self.table[self.block, "layer"] = self.k
        self.k = 0
        self.block += 1


class Chunk:

    def __init__(self, name, weight, rows, col, ncols, nk, ktiles, stat, tile0, wide=False):
        self.name, self.weight, self.rows, self.col, self.ncols = name, weight, rows, col, ncols
        self.ktiles, self.stat, self.tile0, self.wide = ktiles, stat, tile0, wide
        self.slots = [(k, min(nk, ktiles - k)) for k in range(0, ktiles, nk)]


def plan_a():
    ch = {}

    def add(*args, **kw):
        ch[args[0]] = Chunk(*args, **kw)

    for i in range(2):
        add(f"mla{i}", "w_in", D, 336 * i, 336, 2, KD, "h", 0)
    for i, n in enumerate(("hq", "hf", "hi", "hg")):
        add(n, "w_in", D, 672 + 512 * i, 512, 2, KD, "h", 0)
    for i in range(4):
        add(f"gate{i}", "w_in", D, 2720 + 512 * i, 512, 2, KD, "h", 0)
    for i in range(2):
        add(f"uq{i}", "mla_w_uq", QL, 384 * i, 384, 2, 3, "st", 0)
        add(f"ukv{i}", "mla_w_ukv", KVL, 512 * i, 512, 2, 2, "st", 3)
        add(f"pa{i}", "w_proj_a", 512, 512 * i, 512, 2, 4, "st", 0)
        add(f"pb{i}", "w_proj_b", 512, 512 * i, 512, 2, 4, "h", 0)
        add(f"wo{i}", "w_out", D, 512 * i, 512, 2, KD, "h", 0)

    def whole(n):
        return [("slot", n, i) for i in range(len(ch[n].slots))]

    plan = [("misc", f"nT{i}") for i in range(4)]
    plan += whole("mla0") + whole("mla1") + whole("hq") + whole("hf")
    plan += [("misc", f"cT{i}") for i in range(3)]
    plan += whole("hi")
    plan += [("misc", n) for n in ("hqT0", "hqT1", "hfT0", "hfT1")]
    plan += whole("hg") + whole("uq0") + whole("uq1") + whole("ukv0") + whole("ukv1")
    plan += whole("gate0") + whole("gate1")
    plan += [("misc", f"qkT{i}") for i in range(8)]
    spare = whole("gate2") + whole("gate3")
    for i in range(8):
        if 2 <= i < 8:
            plan.append(("misc", f"O{i - 2}"))
        if 1 <= i < 7:
            plan.append(("misc", f"PT{i - 1}"))
        if i == 0:
            plan += [("misc", "S0"), ("misc", "S1")]
        elif i < 5:
            plan.append(("misc", f"S{i + 1}"))
        plan += [("misc", f"G{i}_0"), ("misc", f"G{i}_1"), spare.pop(0)]
    plan += [("misc", "GX"), ("misc", "attT0"), ("misc", "attT1"), ("misc", "oH0"), ("misc", "oH1")]
    plan += whole("pa0") + whole("pa1") + [("misc", "hgT0"), ("misc", "hgT1")]
    plan += whole("pb0") + whole("pb1") + [("misc", f"yT{i}") for i in range(4)]
    last = whole("wo1")
    plan += whole("wo0") + last[:-1] + [("misc", "mT0"), ("misc", "mT1"), last[-1], ("misc", "mT2"), ("misc", "mT3")]
    return ch, plan


def plan_b():
    ch = {}

    def add(*args, **kw):
        ch[args[0]] = Chunk(*args, **kw)

    for i in range(3):
        add(f"qkv{i}", "w_in_2", D, 256 * i, 256, 4, KD, "h", 0)
    for i in range(4):
        add(f"xd{i}", "w_in_2", D, 1792 + 388 * i, 388, 2, KD, "h", 0)
    for i in range(2):
        add(f"z{i}", "w_in_2", D, 768 + 512 * i, 512, 2, KD, "h", 0)
    for i in range(2):
        add(f"wo{i}", "w_out_2", 1536, 512 * i, 512, 2, 12, "mix", 0)

    def whole(n):
        return [("slot", n, i) for i in range(len(ch[n].slots))]

    def shared(names):
        return [("misc", n) for n in names.split()]

    plan = shared("nT0 nT1 nT2 nT3 cvT0 cvT1")
    for n in ("qkv0", "qkv1", "qkv2", "xd0", "xd1", "xd2", "xd3"):
        plan += whole(n)
    spare = whole("z0") + whole("z1")
    for names in ("qkT0 qkT1 qkT2 qkT3 qkT4 S0 S1", "xT0 xT1", "PT0 S2 xT2 xT3", "O0 PT1 S3 xT4 xT5", "O1 PT2 S4",
                  "O2 PT3 S5", "O3 PT4"):
        plan += shared(names) + [spare.pop(0)]
    plan += shared("O4 PT5 O5 attT0 attT1 xsT0 xsT1 xsT2 xsT3 cb0 cb1 cs cr0") + spare
    for hp in range(1, SH // 2):
        plan += shared(f"cr{hp} y{hp - 1}")
    first, second = whole("wo0"), whole("wo1")
    plan += shared(f"y{SH // 2 - 1}") + first[:2] + second[:2] + shared("ssT0 ssT1 ssT2 ssT3")
    plan += first[2:] + second[2:-1] + shared("mT0 mT1") + [second[-1]] + shared("mT2 mT3")
    return ch, plan


class Order:

    def __init__(self, chunks, plan):
        self.chunks, self.plan = chunks, plan
        self.slot_no, self.turn, self.before, self.pair, self.pair_turn = {}, {}, {}, {}, {}
        self.slot_of = []
        n_pair = [0, 0]
        for item in plan:
            self.before[item] = len(self.slot_of)
            if item[0] == "slot":
                self.slot_no[item[1:]] = len(self.slot_of)
                self.slot_of.append(item[1:])
                if item[2] == 0:
                    c = chunks[item[1]]
                    self.pair[c.name] = 0 if c.wide else len(self.pair) % 2
                    for pr in ((0, 1) if c.wide else (self.pair[c.name],)):
                        self.pair_turn[c.name, pr] = n_pair[pr]
                        n_pair[pr] += 1
            else:
                self.turn[item[1]] = len(self.turn)
        self.ffn0 = len(self.slot_of)
        self.slots = self.ffn0 + 6 * FSTEPS
        self.turns = len(self.turn)
        self.pair_total = [n + 1 for n in n_pair]
        assert self.slots % RING == 0 and self.turns % 4 == 0, (self.slots, self.turns)

    def chunk_end(self, name):
        return self.slot_no[name, len(self.chunks[name].slots) - 1] + 1

    def words(self, s):
        if s >= self.ffn0:
            return SLOT
        name, i = self.slot_of[s]
        return self.chunks[name].slots[i][1] * self.chunks[name].ncols

    def is_gate_up(self, s):
        r = s - self.ffn0
        return r >= 0 and (r < 4 or (r < 64 and (r - 4) % 6 < 4))

    def loads(self, s):
        return sum(2 if self.is_gate_up(x) else 1 for x in range(s % RING, s + 1, RING))


CH_A, PLAN_A = plan_a()
CH_B, PLAN_B = plan_b()
ORD = (Order(CH_A, PLAN_A), Order(CH_B, PLAN_B))


READ_A = {"hq": ("act", "hq.t1"), "hf": ("act", "hf.t1"), "hi": ("act", "hi.t1"), "hg": ("act", "hg.t1")}
READ_A.update({f"{n}{i}": ("act", f"{n}{i}.t1") for n in ("mla", "uq", "ukv") for i in range(2)})
READ_A.update({f"gate{i}": ("act", f"gate{i}.t1") for i in range(4)})
READ_A.update({f"{n}{i}": ("dve", f"{n}{i}.t1") for n in ("pa", "pb", "wo") for i in range(2)})
READ_B = {f"qkv{i}": ("act", f"qkv{i}.t1") for i in range(3)}
READ_B.update({f"xd{i}": ("act", f"xd{i}.t1") for i in range(4)})
READ_B.update({f"z{i}": ("act", f"z{i}.t1") for i in range(2)})
READ_B.update({f"wo{i}": ("dve", f"wo{i}.t1") for i in range(2)})
ACT_READS = ("hqT", "hfT", "qkT", "PT", "GX", "xT", "cr")


def reader(block, name):
    if block == 0 and name.startswith("oH"):
        return "dve", name
    return ("act" if name.startswith(ACT_READS) else "dve"), name


OPERANDS = (
    {"cT0": ("st", 0, 2, 1.0), "cT1": ("st", 2, 2, 1.0), "cT2": ("st", 4, 1, 1.0),
     "attT0": ("st", 0, 2, 1.0), "attT1": ("st", 2, 2, 1.0),
     "hgT0": ("h", 0, 2, 0.5), "hgT1": ("h", 2, 2, 0.5),
     **{f"yT{i}": ("h", 2 * i, 2, 0.5) for i in range(4)}},
    {"attT0": ("st", 0, 2, 1.0), "attT1": ("st", 2, 2, 1.0),
     **{f"ssT{i}": ("h", 2 * i, 2, 1.0) for i in range(4)}},
)
NEEDS = (
    {**{("mla0", i): f"nT{i}" for i in range(4)}, ("uq0", 0): "cT1", ("ukv0", 0): "cT2", ("pa0", 0): "attT1",
     ("pb0", 0): "hgT1", ("wo0", 0): "yT3"},
    {("qkv0", 0): "nT1", ("qkv0", 1): "nT3", ("wo0", 0): "attT1", ("wo0", 2): "ssT3"},
)
LOOK = 3
LOOP_AT, LOOP_SLOTS, LOOP_TIMES = 10, 12, 4


def build(nc, A, out, table):
    ctx = ExitStack()
    with ctx:
        def sb(name, shape, dt=F32):
            return ctx.enter_context(nc.sbuf_tensor(name, shape, dt))

        def sem(name):
            return ctx.enter_context(nc.semaphore(name))

        x = sb("x", [P, NT, D])
        h_hi = sb("h_hi", [P, KD, T], F32R)
        h_lo = sb("h_lo", [P, KD, T], F32R)
        st_hi = sb("st_hi", [P, 5, T], F32R)
        st_lo = sb("st_lo", [P, 5, T], F32R)
        w_raw = sb("w_raw", [P, RING, SLOT])
        w_hi = sb("w_hi", [P, RING, SLOT], F32R)
        w_lo = sb("w_lo", [P, RING, SLOT], F32R)
        gains = sb("gains", [P, D])
        gcol = sb("gcol", [P, 2, KD])
        const = sb("const", [P, C_END])
        masks = sb("masks", [P, 8, P], U8)
        lbs = sb("lbs", [P, 2, HG])
        lbw = sb("lbw", [P, 16])
        lbc = sb("lbc", [P, 2, HG])
        small = sb("small", [P, 208])
        halves = sb("halves", [P, 2])
        epsilons = sb("epsilons", [P, 32])
        ssm = sb("ssm", [P, 352])
        rows = sb("rows", [P, P])
        conv = sb("conv", [P, 60])
        arena = sb("arena", [P, 26112])
        acc = [ctx.enter_context(nc.psum_tensor(f"acc{i}", [P, 512], F32)) for i in range(4)]
        misc = [ctx.enter_context(nc.psum_tensor(f"misc{i}", [P, 512], F32)) for i in range(4)]
        ident = const[:, C_ID:C_ID + P]
        tri = const[:, C_TRI:C_TRI + P]
        stat = {"h": (h_hi, h_lo), "st": (st_hi, st_lo)}

        def carve(at, *shape):
            v = arena[:, at:at + int(np.prod(shape))]
            names = "abcd"[:len(shape)]
            if len(shape) == 1:
                return v
            return v.rearrange(f"p ({' '.join(names)}) -> p {' '.join(names)}",
                               **{c: s for c, s in zip(names[1:], shape[1:])})

        hrow = carve(0, NT, D)
        f_silu = carve(4096, NT, FW)
        f_act = carve(4608, NT, FW)
        gate = carve(0, NT, 2048)
        zm = carve(4096, NT, 672)
        X = carve(4096, 2, 1024)
        zq = carve(6144, NT, 512)
        zf = carve(7168, NT, 512)
        vh = carve(8192, NT, 512)
        sg = carve(9216, NT, 512)
        QK = carve(10240, NT, 16, DQK)
        hQ, hK, hP, hR = (carve(18432 + 1024 * i, 1024) for i in range(4))
        AT = carve(22528, HG, 3, P)
        sq = carve(14336, 2, 16, DQK)
        hdump = carve(14336, NT, HG, DK)
        zqkv = carve(4096, NT, 768)
        xd = carve(5632, NT, XD)
        xs = carve(5632, NT, SI)
        zs = carve(8736, NT, SI)
        xc = carve(13344, 12, T + TAPS - 1)
        xdt = carve(13344, NT, SI)
        cv = carve(16452, 12, T)
        cbm = carve(19524, 2, 384)
        Ex = carve(20292, 2, 2, 384)
        ys = carve(2048, NT, SI)
        qkT = (carve(14336, 16, T), carve(10784, HB + HKV, T))
        va = (carve(13312, NT, HA, DV), zqkv[:, :, 640:768].rearrange("p t (h d) -> p t h d", h=HKV))
        Sx = (carve(24064, 2, 512), carve(22852, 2, 512))
        PTx = (carve(25088, 2, 512), carve(23876, 2, 512))
        att = (carve(6144, NT, 512), carve(21828, NT, 512))
        oh = carve(7168, NT, 512)
        rope = (carve(24064, 4, 16, 16), carve(24900, 4, NT * 10, 8))
        prm = ssm[:, 0:48]
        dt_u, dt_m, dt_v, dt_a = (ssm[:, 48 + 32 * i:80 + 32 * i] for i in range(4))
        ea = ssm[:, 176:192]
        cs = ssm[:, 192:240]
        ncx = ssm[:, 240:256]
        cosb, sinb, angs = ssm[:, 256:272], ssm[:, 272:288], ssm[:, 288:304]
        turns_, wrap = ssm[:, 304:320], ssm[:, 320:336]
        posf = ssm[:, 336:338]
        posi = sb("posi", [P, NT], I32)

        PE, AC, DV_, PO = (Progress(nc, ctx, n, table) for n in
                           ("tensor_steps", "scalar_steps", "vector_steps", "gpsimd_steps"))
        by = {"act": AC, "dve": DV_}
        x_in, c_in, lb_in, pos_in = sem("x_loaded"), sem("const_loaded"), sem("lb_loaded"), sem("positions_loaded")
        par_in = sem("params_loaded")
        landed = [sem(f"weights_landed{r}") for r in range(RING)]
        fin_in, out_done = sem("final_gain_loaded"), sem("out_stored")
        chain = sem("prologue_chain")
        lb_T, shifted, lb_exp, trig = sem("lb_turned"), sem("exponents_ready"), sem("lb_exponentials"), sem("trig_ready")
        rows_0 = sem("rows_cleared")
        fin_ms, fin_r, fin_rows = sem("final_squares"), sem("final_inverse"), sem("final_rows")
        PARS = (7 * 16, 8 * 16)

        def par_at(layer):
            block, l = layer
            return par_in, l * PARS[block] + (DEPTH * PARS[0] if block else 0) + PARS[block]

        def landed_at(layer, s, j=None):
            block, l = layer
            per = [16 * o.loads(o.slots - RING + s % RING) for o in ORD]
            v = l * per[block] + (DEPTH * per[0] if block else 0) + 16 * ORD[block].loads(s)
            return landed[s % RING], v if j is None else v + j * (16 * 5)

        def slot_at(eng, layer, what, s, j=None):
            o = ORD[layer[0]]
            if s < 0:
                return eng.before(layer, f"{what}-{-s}")
            r = s - (o.ffn0 + LOOP_AT) - (0 if what == "used" else LOOK)
            if j is None and 0 <= r < LOOP_SLOTS * LOOP_TIMES:
                semaphore, v = eng.at(layer, f"{what}{s - r + r % LOOP_SLOTS}")
                return semaphore, v + (r // LOOP_SLOTS) * eng.body(layer[0])
            return eng.at(layer, f"{what}{s}", j)

        def slot_name(layer, what, s):
            o = ORD[layer[0]]
            return f"{what}{s}" if s < o.slots - RING else f"{what}-{o.slots - s}"

        def name_at(eng, layer, what, s, j=None):
            o = ORD[layer[0]]
            if s >= o.slots - RING:
                return eng.at(layer, f"{what}-{o.slots - s}", j)
            return slot_at(eng, layer, what, s, j)

        def bc(ap, shape):
            return ap.to_broadcast(shape)

        block_ = ctx.enter_context(nc.Block())

        @block_.sync
        def _(sp):
            sp.dma_start(x[:, :, :], A["x"].rearrange("(t p) d -> p t d", p=P)).then_inc(x_in, 16)
            sp.dma_start(const[:, :], A["const"]).then_inc(c_in, 16)
            sp.dma_start(carve(0, 8, P), A["masks"]).then_inc(c_in, 16)
            sp.wait_ge(rows_0, 1)
            sp.dma_start(rows[0:8, :], A["hg_lb_logits"].rearrange("l (h k) -> (l h) k", k=DK)).then_inc(lb_in, 16)
            sp.dma_start(posi[:, :], A["positions_2"].rearrange("(t p) -> p t", p=P),
                         allow_slow_non_contiguous=True).then_inc(pos_in, 16)

            def row(name, l, n):
                return A[name][bass.ds(l, 1), :].to_broadcast([P, n])

            def params(layer):
                block, l = layer
                sp.wait_ge(*DV_.before(layer, "f0"))
                for i, name in enumerate(("norm_mix", "norm_ffn")):
                    src = A[name + ("_2" if block else "")][bass.ds(l, 1), :]
                    sp.dma_start(gcol[:, i, :], src.rearrange("a (k p) -> p (a k)", p=P),
                                 allow_slow_non_contiguous=True).then_inc(par_in, 16)
                if block == 0:
                    for name, at, n in (("mla_norm_cq", G_CQ, QL), ("mla_norm_ckv", G_CKV, KVL), ("mla_q_norm", G_QK, DQK), ("mla_k_norm", G_QK + DQK, DQK), ("hg_out_norm", G_HG, DK)):
                        sp.dma_start(gains[:, at:at + n], row(name, l, n)).then_inc(par_in, 16)
                else:
                    sp.dma_start(gains[:, G_SSM:G_SSM + SI], row("ssm_norm_2", l, SI)).then_inc(par_in, 16)
                    for i, name in enumerate(("dt_bias_2", "a_log_2", "d_skip_2")):
                        sp.dma_start(prm[:, 16 * i:16 * i + 16], row(name, l, SH)).then_inc(par_in, 16)
                    sp.dma_start(rows[0:48, :], A["conv_w_2"][bass.ds(l * 48, 48), :]).then_inc(par_in, 16)
                    sp.dma_start(rows[48:60, :], A["conv_b_2"][bass.ds(l * 12, 12), :]).then_inc(par_in, 16)

            def ffn_load(layer, s, kind, i, q, j=None):
                block, l = layer
                suffix = "_2" if block else ""
                sp.wait_ge(*name_at(DV_, layer, "lo", s - RING, j))
                place = w_raw[:, s % RING, :]
                if kind == "gu":
                    dst = place.rearrange("p (k u n) -> p k u n", k=2, u=2)
                    for u, name in enumerate(("w_gate", "w_up")):
                        src = A[name + suffix][bass.ds(l * D + 2 * q * P, 2 * P), bass.ds(i * FW, FW)]
                        sp.dma_start(dst[:, :, u, :], src.rearrange("(k p) n -> p k n", p=P))\
                            .then_inc(landed[s % RING], 16)
                else:
                    src = A["w_down" + suffix][bass.ds(l * FF + i * FW + q * P, P), :]
                    sp.dma_start(place, src).then_inc(landed[s % RING], 16)

            def layer_loads(layer):
                block, l = layer
                o = ORD[block]
                params(layer)
                for s, (name, i) in enumerate(o.slot_of):
                    c = o.chunks[name]
                    k0, nk = c.slots[i]
                    sp.wait_ge(*name_at(DV_, layer, "lo", s - RING))
                    src = A[c.weight][bass.ds(l * c.rows + k0 * P, nk * P), c.col:c.col + c.ncols]
                    dst = w_raw[:, s % RING, 0:nk * c.ncols].rearrange("p (k n) -> p k n", k=nk)
                    sp.dma_start(dst, src.rearrange("(k p) n -> p k n", p=P)).then_inc(landed[s % RING], 16)
                s = o.ffn0

                def gate_up(s, i, j=None):
                    for q in range(4):
                        ffn_load(layer, s + q, "gu", i, q, j)

                def down(s, i, j=None):
                    for q in range(2):
                        ffn_load(layer, s + q, "dn", i, q, j)

                gate_up(s, 0)
                gate_up(s + 4, 1)
                down(s + 8, 0)
                s += LOOP_AT
                with sp.Fori(0, LOOP_TIMES) as j:
                    gate_up(s, 2 * j + 2, j)
                    down(s + 4, 2 * j + 1, j)
                    gate_up(s + 6, 2 * j + 3, j)
                    down(s + 10, 2 * j + 2, j)
                s += LOOP_SLOTS * LOOP_TIMES
                gate_up(s, 10)
                down(s + 4, 9)
                down(s + 6, 10)

            for block in range(2):
                with sp.Fori(0, DEPTH) as l:
                    layer_loads((block, l))
            sp.wait_ge(*DV_.final("f0"))
            sp.dma_start(gains[:, 0:D], A["final_norm_2"].rearrange("(a n) -> a n", a=1).to_broadcast([P, D]))\
                .then_inc(fin_in, 16)
            for t in range(NT):
                sp.wait_ge(fin_rows, t + 1)
                sp.dma_start(out[t * P:(t + 1) * P, :], hrow[:, t, :]).then_inc(out_done, 16)
            sp.wait_ge(out_done, 16 * NT)

        @block_.tensor
        def _(pe):
            def product(dst, st, k, t, rhs_hi, rhs_lo, first, last):
                hi, lo = st
                cols = slice(t * P, (t + 1) * P)
                pe.matmul(dst, hi[:, k, cols], rhs_hi, start=first, stop=False)
                pe.matmul(dst, hi[:, k, cols], rhs_lo, start=False, stop=False)
                return pe.matmul(dst, lo[:, k, cols], rhs_hi, start=False, stop=last)

            pe.wait_ge(c_in, 32)
            pe.wait_ge(lb_in, 16)
            pe.wait_ge(rows_0, 1)
            pe.transpose(misc[3][:, 0:P], rows[:, :], ident).then_inc(lb_T, 1)

            def run_slot(layer, name, i):
                block = layer[0]
                o = ORD[block]
                c, s = o.chunks[name], o.slot_no[name, i]
                k0, nk = c.slots[i]
                if i == 0:
                    for pr in ((0, 1) if c.wide else (o.pair[name],)):
                        n = o.pair_turn[name, pr]
                        if n == 0:
                            pe.wait_ge(*DV_.before(layer, f"x_ffn{2 * pr + 1}"))
                        else:
                            prior = [m for (m, q), v in o.pair_turn.items() if q == pr and v == n - 1][0]
                            who, step = (READ_A, READ_B)[block][prior]
                            pe.wait_ge(*by[who].at(layer, step))
                if (name, i) in NEEDS[block]:
                    pe.wait_ge(*DV_.at(layer, NEEDS[block][name, i]))
                pe.wait_ge(*name_at(DV_, layer, "lo", s))
                for kk in range(nk):
                    k = k0 + kk
                    if c.stat == "mix":
                        st, tile = (stat["st"], k) if k < 4 else (stat["h"], k - 4)
                    else:
                        st, tile = stat[c.stat], c.tile0 + k
                    for t in range(NT):
                        for half in range(2 if c.wide else 1):
                            n = 512 if c.wide else c.ncols
                            at = kk * c.ncols + half * 512
                            bank = 2 * (half if c.wide else o.pair[name]) + t
                            mm = product(acc[bank][:, 0:n], st, tile, t, w_hi[:, s % RING, at:at + n],
                                         w_lo[:, s % RING, at:at + n], k == 0, k == c.ktiles - 1)
                mm.then_inc(*PE.mark(slot_name(layer, "used", s)))

            def bank_of(layer, name):
                block = layer[0]
                o = ORD[block]
                u = o.turn[name]
                if u >= 4:
                    prior = [m for m, v in o.turn.items() if v == u - 4][0]
                    who, step = reader(block, prior)
                    pe.wait_ge(*by[who].at(layer, step))
                else:
                    pe.wait_ge(*DV_.before(layer, "fT10"))
                return misc[u % 4]

            def transposes(layer, name, blocks, n=P):
                b = bank_of(layer, name)
                for i, src in enumerate(blocks):
                    tr = pe.transpose(b[0:n, i * P:(i + 1) * P], src, ident)
                tr.then_inc(*PE.mark(name))

            def scores(layer, g):
                block = layer[0]
                d, group = (DQK, 1) if block == 0 else (DB, HB // HKV)
                b = bank_of(layer, f"S{g}")
                qk = qkT[block]
                heads, nq, keys = (range(4 * g, 4 * g + 4), 0, P) if g < 2 else (range(2 * g - 4, 2 * g - 2), 1, T)
                for i, hd in enumerate(heads):
                    mm = pe.matmul(b[:, i * keys:(i + 1) * keys], qk[0:d, hd, nq * P:(nq + 1) * P],
                                   qk[0:d, HB + hd // group, 0:keys], start=True, stop=True)
                mm.then_inc(*PE.mark(f"S{g}"))

            def weigh(layer, g):
                block = layer[0]
                group = 1 if block == 0 else HB // HKV
                pe.wait_ge(*AC.at(layer, f"PT{g}"))
                b = bank_of(layer, f"O{g}")
                pt = PTx[block][:, g % 2, :]
                heads, nk = (range(4 * g, 4 * g + 4), 1) if g < 2 else (range(2 * g - 4, 2 * g - 2), 2)
                for i, hd in enumerate(heads):
                    for k in range(nk):
                        at = (i * nk + k) * P
                        mm = pe.matmul(b[:, i * 64:(i + 1) * 64], pt[:, at:at + P],
                                       va[block][:, k, hd // group, :], start=(k == 0), stop=(k == nk - 1))
                mm.then_inc(*PE.mark(f"O{g}"))

            def shared(layer, name):
                block = layer[0]
                kind, num = name.rstrip("0123456789"), name[len(name.rstrip("0123456789")):]
                i = int(num) if num else 0
                if kind in ("nT", "mT"):
                    if kind == "nT":
                        pe.wait_ge(*DV_.before(layer, f"x_ffn{2 * (i // 2) + 1}"))
                        pe.wait_ge(x_in, 16)
                    else:
                        pe.wait_ge(*DV_.at(layer, f"wo{i // 2}.t1"))
                    transposes(layer, name, [x[:, t, k * P:(k + 1) * P] for k in (2 * i, 2 * i + 1)
                                             for t in range(NT)])
                elif kind == "S":
                    if i == 0:
                        pe.wait_ge(*AC.at(layer, "qkT7" if block == 0 else "qkT4"))
                    scores(layer, i)
                elif kind == "PT":
                    pe.wait_ge(*AC.at(layer, f"p{i}"))
                    transposes(layer, name, [Sx[block][:, i % 2, k * P:(k + 1) * P] for k in range(4)])
                elif kind == "O":
                    weigh(layer, i)
                elif kind == "attT":
                    if i == 0:
                        pe.wait_ge(*DV_.at(layer, "O5"))
                    transposes(layer, name, [att[block][:, t, k * P:(k + 1) * P] for k in (2 * i, 2 * i + 1)
                                             for t in range(NT)])
                elif block == 0:
                    shared_a(layer, name, kind, i)
                else:
                    shared_b(layer, name, kind, i)

            def shared_a(layer, name, kind, i):
                if kind == "cT":
                    if i == 0:
                        pe.wait_ge(*DV_.at(layer, "cnorm"))
                    tiles = ((0, 1), (2, 3), (4,))[i]
                    transposes(layer, name, [zm[:, t, k * P:(k + 1) * P] for k in tiles for t in range(NT)])
                elif kind in ("hqT", "hfT"):
                    src = zq if kind == "hqT" else zf
                    if i == 0:
                        pe.wait_ge(*AC.at(layer, f"{kind[:2]}.t1"))
                    transposes(layer, name, [src[:, t, k * P:(k + 1) * P] for k in (2 * i, 2 * i + 1)
                                             for t in range(NT)])
                elif kind == "qkT":
                    if i == 0:
                        pe.wait_ge(*DV_.at(layer, "qk1"))
                    transposes(layer, name, [QK[:, t, hd, :] for hd in (2 * i, 2 * i + 1) for t in range(NT)], DQK)
                elif kind.startswith("G") and name != "GX":
                    lev, pr = int(name[1]), int(name[3])
                    if pr == 0:
                        pe.wait_ge(*DV_.at(layer, f"X{lev}"))
                    if lev == 0 and pr == 0:
                        pe.wait_ge(*AC.at(layer, "hqT1"))
                    b = bank_of(layer, name)
                    for n, (hd, t) in enumerate((hd, t) for hd in (2 * pr, 2 * pr + 1) for t in range(NT)):
                        cols = slice(hd * T + t * P, hd * T + (t + 1) * P)
                        keys = hK[:, cols] if lev == 0 else X[:, lev % 2, cols]
                        queries = hQ[:, cols] if lev == 0 else X[:, lev % 2, cols]
                        mm = pe.matmul(b[:, n * P:(n + 1) * P], keys, queries, start=True, stop=True)
                    mm.then_inc(*PE.mark(name))
                elif name == "GX":
                    pe.wait_ge(*DV_.at(layer, "X8"))
                    b = bank_of(layer, name)
                    for hd in range(HG):
                        mm = pe.matmul(b[:, hd * P:(hd + 1) * P], X[:, 0, hd * T:hd * T + P],
                                       X[:, 0, hd * T + P:hd * T + T], start=True, stop=True)
                    mm.then_inc(*PE.mark(name))
                elif kind == "oH":
                    if i == 0:
                        pe.wait_ge(*AC.at(layer, "GX"))
                        pe.wait_ge(*DV_.at(layer, "G7_1"))
                    b = bank_of(layer, name)
                    for hd in range(HG):
                        cols = slice(hd * P, (hd + 1) * P)
                        if i == 0:
                            mm = pe.matmul(b[:, cols], AT[:, hd, 0, :], vh[:, 0, cols], start=True, stop=True)
                        else:
                            pe.matmul(b[:, cols], AT[:, hd, 2, :], vh[:, 0, cols], start=True, stop=False)
                            mm = pe.matmul(b[:, cols], AT[:, hd, 1, :], vh[:, 1, cols], start=False, stop=True)
                    mm.then_inc(*PE.mark(name))
                elif kind == "hgT":
                    if i == 0:
                        pe.wait_ge(*DV_.at(layer, "oh1"))
                    transposes(layer, name, [oh[:, t, k * P:(k + 1) * P] for k in (2 * i, 2 * i + 1)
                                             for t in range(NT)])
                elif kind == "yT":
                    pe.wait_ge(*DV_.at(layer, f"y{i // 2}"))
                    transposes(layer, name, [gate[:, t, k * P:(k + 1) * P] for k in (2 * i, 2 * i + 1)
                                             for t in range(NT)])
                else:
                    raise ValueError(name)

            def shared_b(layer, name, kind, i):
                if kind == "cvT":
                    pe.wait_ge(*par_at(layer))
                    b = bank_of(layer, name)
                    pe.transpose(b[:, 0:P], rows[:, :], ident).then_inc(*PE.mark(name))
                elif kind == "qkT":
                    if i == 0:
                        pe.wait_ge(*DV_.at(layer, "qk"))
                    transposes(layer, name, [zqkv[:, t, hd * DB:hd * DB + DQK] for hd in (2 * i, 2 * i + 1)
                                             for t in range(NT)], DQK)
                elif kind == "xT":
                    if i == 0:
                        pe.wait_ge(*AC.at(layer, "xd3.t1"))
                    transposes(layer, name, [xd[:, t, k * P:(k + 1) * P] for k in (2 * i, 2 * i + 1)
                                             for t in range(NT)])
                elif kind == "xsT":
                    if i == 0:
                        pe.wait_ge(*AC.at(layer, "conv_silu"))
                    t, half = i // 2, i % 2
                    transposes(layer, name, [cv[:, 4 * half + k, t * P:(t + 1) * P] for k in range(4)])
                elif kind == "cb":
                    b = bank_of(layer, name)
                    pe.matmul(b[:, 0:T], cv[:, 8 + i, 0:P], cv[:, 10 + i, :], start=True, stop=True)
                    pe.matmul(b[:, T:T + P], cv[:, 8 + i, P:T], cv[:, 10 + i, P:T], start=True, stop=True)\
                        .then_inc(*PE.mark(name))
                elif name == "cs":
                    pe.wait_ge(*DV_.at(layer, "dt_a"))
                    b = bank_of(layer, name)
                    pe.matmul(b[:, 0:16], tri, dt_a[:, 0:16], start=True, stop=True)
                    pe.matmul(b[:, 16:32], tri, dt_a[:, 16:32], start=True, stop=True)
                    pe.matmul(b[:, 32:48], bc(tri[:, P - 1:P], [P, P]), dt_a[:, 0:16], start=True, stop=True)\
                        .then_inc(*PE.mark(name))
                elif kind == "cr":
                    b = bank_of(layer, name)
                    for n, (hd, t) in enumerate((hd, t) for hd in (2 * i, 2 * i + 1) for t in range(NT)):
                        a = dt_a[:, 16 * t + hd:16 * t + hd + 1]
                        mm = pe.matmul(b[:, n * P:(n + 1) * P], bc(a, [P, P]), tri, start=True, stop=True)
                    mm.then_inc(*PE.mark(name))
                elif kind == "y":
                    pe.wait_ge(*DV_.at(layer, f"M{i}"))
                    b = bank_of(layer, name)
                    for u in range(2):
                        hd = 2 * i + u
                        E = Ex[:, i % 2, u, :]
                        cols = slice(hd * SP, (hd + 1) * SP)
                        pe.matmul(b[:, u * SP:(u + 1) * SP], E[:, 0:P], xdt[:, 0, cols], start=True, stop=True)
                        at = P + u * SP
                        pe.matmul(b[:, at:at + SP], E[:, P:2 * P], xdt[:, 0, cols], start=True, stop=False)
                        mm = pe.matmul(b[:, at:at + SP], E[:, 2 * P:3 * P], xdt[:, 1, cols], start=False, stop=True)
                    mm.then_inc(*PE.mark(name))
                elif kind == "ssT":
                    if i == 0:
                        pe.wait_ge(*DV_.at(layer, "ys"))
                    transposes(layer, name, [ys[:, t, k * P:(k + 1) * P] for k in (2 * i, 2 * i + 1)
                                             for t in range(NT)])
                else:
                    raise ValueError(name)

            def feed_forward(layer):
                o = ORD[layer[0]]

                def gate_up(s, i, j=None, behind=None):
                    pe.wait_ge(*DV_.at(layer, behind, j))
                    first = i == 0
                    banks = acc[0:2] if first else misc[2:4]
                    for q in range(4):
                        if first:
                            pe.wait_ge(*DV_.at(layer, f"mT{q}"))
                        pe.wait_ge(*name_at(DV_, layer, "lo", s + q, j))
                        for kk in range(2):
                            for t in range(NT):
                                at = kk * 512
                                mm = product(banks[t][:, :], stat["h"], 2 * q + kk, t,
                                             w_hi[:, (s + q) % RING, at:at + 512],
                                             w_lo[:, (s + q) % RING, at:at + 512],
                                             q == 0 and kk == 0, q == 3 and kk == 1)
                        mm.then_inc(*PE.mark(slot_name(layer, "used", s + q)))

                def turn(step, j=None):
                    pe.wait_ge(*DV_.at(layer, f"f{step}", j))
                    for kk in range(2):
                        for t in range(NT):
                            at = kk * T + t * P
                            tr = pe.transpose(misc[0][:, at:at + P], f_act[:, t, kk * P:(kk + 1) * P], ident)
                    tr.then_inc(*PE.mark(f"fT{step}"))

                def down(s, step, first=False, last=False, j=None):
                    pe.wait_ge(*DV_.at(layer, f"fT{step}", j))
                    for q in range(2):
                        pe.wait_ge(*name_at(DV_, layer, "lo", s + q, j))
                        for half in range(2):
                            for t in range(NT):
                                at = half * 512
                                mm = product(acc[2 * half + t][:, :], stat["st"], q, t,
                                             w_hi[:, (s + q) % RING, at:at + 512],
                                             w_lo[:, (s + q) % RING, at:at + 512],
                                             first and q == 0, last and q == 1)
                            if last and q == 1 and half == 0:
                                mm.then_inc(*PE.mark("x_half"))
                        mm.then_inc(*PE.mark(slot_name(layer, "used", s + q)))

                s = o.ffn0
                gate_up(s, 0, behind="wo0.t1")
                turn("0")
                gate_up(s + 4, 1, behind="mT3")
                pe.wait_ge(*DV_.at(layer, "wo1.t1"))
                pe.wait_ge(*DV_.at(layer, "f0"))
                down(s + 8, "0", first=True)
                turn("1")
                s += LOOP_AT
                PE.loop(None)
                with pe.Fori(0, LOOP_TIMES) as j:
                    gate_up(s, 2, j, behind="f1")
                    down(s + 4, "1", j=j)
                    turn("2", j)
                    gate_up(s + 6, 3, j, behind="f2")
                    down(s + 10, "2", j=j)
                    turn("3", j)
                PE.loop(LOOP_TIMES)
                s += LOOP_SLOTS * LOOP_TIMES
                gate_up(s, 10, behind="f3@last")
                down(s + 4, "3@last")
                turn("10")
                down(s + 6, "10", last=True)

            pe.wait_ge(shifted, 1)
            for block in range(2):
                with pe.Fori(0, DEPTH) as l:
                    layer = (block, l)
                    for item in ORD[block].plan:
                        if item[0] == "slot":
                            run_slot(layer, item[1], item[2])
                        else:
                            shared(layer, item[1])
                    feed_forward(layer)
                PE.end()

        @block_.scalar
        def _(act):
            split = [0]

            def split_until(layer, n, j=None):
                o = ORD[layer[0]]
                for s in range(split[0], min(n, o.slots)):
                    act.wait_ge(*landed_at(layer, s, j))
                    act.wait_ge(*name_at(PE, layer, "used", s - RING, j))
                    w = o.words(s)
                    act.activation(w_hi[:, s % RING, 0:w], w_raw[:, s % RING, 0:w], ACT.Copy)\
                        .then_inc(*AC.mark(slot_name(layer, "hi", s)))
                split[0] = max(split[0], min(n, o.slots))

            def wait_bank(layer, name):
                split_until(layer, ORD[layer[0]].before["misc", name] + LOOK)
                act.wait_ge(*PE.at(layer, name))
                return misc[ORD[layer[0]].turn[name] % 4]

            def wait_product(layer, name):
                o = ORD[layer[0]]
                end = o.chunk_end(name)
                split_until(layer, end + LOOK)
                act.wait_ge(*name_at(PE, layer, "used", end - 1))
                pair = o.pair[name]
                return acc[2 * pair], acc[2 * pair + 1]

            def operand(layer, name):
                where, tile, n, scale = OPERANDS[layer[0]][name]
                b = wait_bank(layer, name)
                dst = stat[where][0][:, tile:tile + n, :].rearrange("p k t -> p (k t)")
                act.activation(dst, b[:, 0:n * T], ACT.Copy, scale=scale).then_inc(*AC.mark(f"hi.{name}"))

            def norm_operand(layer, name):
                kind, i = name[:2], int(name[2])
                b = wait_bank(layer, name)
                if kind == "mT":
                    act.wait_ge(*name_at(PE, layer, "used", ORD[layer[0]].chunk_end("wo1") - 1))
                for k in range(2):
                    act.activation(h_hi[:, 2 * i + k, :], b[:, k * T:(k + 1) * T], ACT.Copy,
                                   scale=gcol[:, kind == "mT", 2 * i + k:2 * i + k + 1])\
                        .then_inc(*AC.mark(f"hi.{name}"))

            def inv(layer, kind, t):
                c = {"x": RS + M_X, "x/2": RS + M_H, "y": RS + M_Y}[kind] + t
                return small[:, c:c + 1]

            def squares(layer, kind):
                col = M_X if kind == "nT" else M_Y
                for t in range(NT):
                    act.activation(hrow[:, t, :], x[:, t, :], ACT.Square, scale=D ** -0.5, accum_out=small[:, col + t:col + t + 1])\
                        .then_inc(*AC.mark(f"ms.{kind}"))

            def softmax(layer, g, scale):
                block = layer[0]
                split_until(layer, ORD[block].before["misc", f"S{g}"] + LOOK)
                act.wait_ge(*DV_.at(layer, f"S{g}"))
                n, keys = (4, P) if g < 2 else (2, T)
                for i in range(n):
                    v = Sx[block][:, g % 2, i * keys:(i + 1) * keys]
                    c = (g % 4) * 4 + i
                    e = act.activation(v, v, ACT.Exp, scale=scale, bias=small[:, 144 + c:145 + c],
                                       accum_out=small[:, 160 + c:161 + c])
                    e.then_inc(*AC.mark(f"p{g}"))

            def turned_weights(layer, g):
                b = wait_bank(layer, f"PT{g}")
                if g >= 2:
                    act.wait_ge(*PE.at(layer, f"O{g - 2}"))
                act.activation(PTx[layer[0]][:, g % 2, :], b[:, :], ACT.Copy).then_inc(*AC.mark(f"PT{g}"))

            def feed_forward(layer):
                o = ORD[layer[0]]

                def silu(s_end, step, used_s, j=None):
                    split_until(layer, s_end + LOOK, j)
                    act.wait_ge(*name_at(PE, layer, "used", used_s, j))
                    if step == "0":
                        act.wait_ge(*PO.at(layer, "r.mT"))
                    for t in range(NT):
                        b = acc[t] if step == "0" else misc[2 + t]
                        act.activation(f_silu[:, t, :], b[:, 0:FW], ACT.Silu, scale=inv(layer, "y", t))\
                            .then_inc(*AC.mark(f"f{step}.t{t}"))

                def turned(s_end, step, j=None):
                    split_until(layer, s_end + LOOK, j)
                    act.wait_ge(*PE.at(layer, f"fT{step}", j))
                    act.activation(st_hi[:, 0:2, :].rearrange("p k t -> p (k t)"), misc[0][:, :], ACT.Copy)\
                        .then_inc(*AC.mark(f"fT{step}"))

                s = o.ffn0
                silu(s + 2, "0", s + 3)
                turned(s + 4, "0")
                silu(s + 8, "1", s + 7)
                turned(s + 10, "1")
                s += LOOP_AT
                AC.loop(None)
                with act.Fori(0, LOOP_TIMES) as j:
                    silu(s + 4, "2", s + 3, j)
                    turned(s + 6, "2", j)
                    silu(s + 10, "3", s + 9, j)
                    turned(s + 12, "3", j)
                AC.loop(LOOP_TIMES)
                split[0] += LOOP_SLOTS * (LOOP_TIMES - 1)
                s += LOOP_SLOTS * LOOP_TIMES
                silu(s + 4, "10", s + 3)
                turned(s + 6, "10")
                split_until(layer, o.slots)
                split[0] = 0

            def copy_product(layer, name, dst, func=ACT.Copy, rms=None):
                banks = wait_product(layer, name)
                n = ORD[layer[0]].chunks[name].ncols
                for t in range(NT):
                    scale = 1.0 if rms is None else inv(layer, rms, t)
                    act.activation(dst(t), banks[t][:, 0:n], func, scale=scale).then_inc(*AC.mark(f"{name}.t{t}"))

            def body_a(layer):
                sc = float(DQK) ** -0.5
                act.wait_ge(x_in, 16)
                act.wait_ge(*par_at(layer))
                act.wait_ge(*DV_.before(layer, "x_ffn3"))
                for i in range(4):
                    norm_operand(layer, f"nT{i}")
                squares(layer, "nT")
                act.wait_ge(*PO.at(layer, "r.nT"))
                for i in range(2):
                    copy_product(layer, f"mla{i}", lambda t: zm[:, t, 336 * i:336 * i + 336], rms="x")
                act.wait_ge(*AC.now(layer))
                for t in range(NT):
                    act.activation(sq[:, 0, 0:4, :].rearrange("p a b -> p (a b)"), zm[:, t, 0:QL], ACT.Square, scale=QL ** -0.5,
                                   accum_out=small[:, M_CQ + t:M_CQ + t + 1]).then_inc(*AC.mark())
                    act.activation(sq[:, 1, 0:4, 0:64], zm[:, t, QL:QL + KVL].rearrange("p (a b) -> p a b", a=4),
                                   ACT.Square, scale=KVL ** -0.5, accum_out=small[:, M_CKV + t:M_CKV + t + 1])\
                        .then_inc(*AC.mark("ms.c"))
                    act.wait_ge(*AC.now(layer))
                copy_product(layer, "hq", lambda t: zq[:, t, :], rms="x")
                copy_product(layer, "hf", lambda t: zf[:, t, :], rms="x")
                for i in range(3):
                    operand(layer, f"cT{i}")
                copy_product(layer, "hi", lambda t: vh[:, t, :], rms="x")
                for i in range(2):
                    b = wait_bank(layer, f"hqT{i}")
                    act.activation(hQ[:, 512 * i:512 * i + 512], b[:, :], ACT.Copy).then_inc(*AC.mark(f"hqT{i}"))
                for i in range(2):
                    b = wait_bank(layer, f"hfT{i}")
                    act.activation(hP[:, 512 * i:512 * i + 512], b[:, :], ACT.Sigmoid).then_inc(*AC.mark())
                    act.activation(hK[:, 512 * i:512 * i + 512], b[:, :], ACT.Sigmoid, scale=-1.0)\
                        .then_inc(*AC.mark(f"hfT{i}"))
                banks = wait_product(layer, "hg")
                for t in range(NT):
                    act.activation(zq[:, t, :], banks[t][:, :], ACT.Copy, scale=inv(layer, "x", t))\
                        .then_inc(*AC.mark())
                    act.activation(sg[:, t, :], banks[t][:, :], ACT.Tanh, scale=inv(layer, "x/2", t))\
                        .then_inc(*AC.mark(f"hg.t{t}"))
                for i in range(2):
                    copy_product(layer, f"uq{i}",
                                 lambda t: QK[:, t, 4 * i:4 * i + 4, :].rearrange("p a b -> p (a b)"))
                for i in range(2):
                    banks = wait_product(layer, f"ukv{i}")
                    for t in range(NT):
                        kv = banks[t][:, :].rearrange("p (h e) -> p h e", h=4)
                        act.activation(QK[:, t, 8 + 4 * i:12 + 4 * i, 0:NOPE], kv[:, :, 0:NOPE], ACT.Copy)\
                            .then_inc(*AC.mark())
                        act.activation(va[0][:, t, 4 * i:4 * i + 4, :], kv[:, :, NOPE:NOPE + DV], ACT.Copy)\
                            .then_inc(*AC.mark(f"ukv{i}.t{t}"))
                for t in range(NT):
                    src = zm[:, t, QL + KVL:].rearrange("p (a d) -> p a d", a=1)
                    act.activation(QK[:, t, 8:16, NOPE:DQK], bc(src, [P, 8, RA]), ACT.Copy).then_inc(*AC.mark("kpe"))
                act.wait_ge(*AC.now(layer))
                for t in range(NT):
                    act.activation(sq[:, t, :, :], QK[:, t, :, :], ACT.Square, scale=DQK ** -0.5).then_inc(*AC.mark(f"sq{t}"))
                for i in range(2):
                    copy_product(layer, f"gate{i}", lambda t: gate[:, t, 512 * i:512 * i + 512], ACT.Tanh, "x/2")
                for i in range(8):
                    b = wait_bank(layer, f"qkT{i}")
                    act.activation(qkT[0][0:DQK, 2 * i:2 * i + 2, :].rearrange("p h t -> p (h t)"), b[0:DQK, :],
                                   ACT.Copy).then_inc(*AC.mark(f"qkT{i}"))
                for i in range(8):
                    if 1 <= i < 7:
                        turned_weights(layer, i - 1)
                    if i == 0:
                        softmax(layer, 0, sc)
                        softmax(layer, 1, sc)
                    elif i < 5:
                        softmax(layer, i + 1, sc)
                    if i == 4 or i == 7:
                        n = 2 + (i == 7)
                        copy_product(layer, f"gate{n}", lambda t: gate[:, t, 512 * n:512 * n + 512], ACT.Tanh,
                                     "x/2")
                b = wait_bank(layer, "GX")
                act.activation(AT[:, :, 2, :], b[:, :].rearrange("p (h q) -> p h q", h=HG), ACT.Copy)\
                    .then_inc(*AC.mark("GX"))
                operand(layer, "attT0")
                operand(layer, "attT1")
                for t in range(NT):
                    b = wait_bank(layer, f"oH{t}")
                    for hd in range(HG):
                        c = M_HG + 4 * t + hd
                        act.activation(hdump[:, t, hd, :], b[:, hd * P:(hd + 1) * P], ACT.Square, scale=DK ** -0.5,
                                       accum_out=small[:, c:c + 1]).then_inc(*AC.mark(f"ms.h{t}"))
                operand(layer, "hgT0")
                operand(layer, "hgT1")
                for i in range(4):
                    operand(layer, f"yT{i}")
                for i in range(4):
                    norm_operand(layer, f"mT{i}")
                squares(layer, "mT")
                feed_forward(layer)

            def body_b(layer):
                sc = float(DB) ** -0.5
                act.wait_ge(*par_at(layer))
                act.wait_ge(*DV_.before(layer, "x_ffn3"))
                for i in range(4):
                    norm_operand(layer, f"nT{i}")
                squares(layer, "nT")
                act.wait_ge(*PO.at(layer, "r.nT"))
                for i in range(3):
                    copy_product(layer, f"qkv{i}", lambda t: zqkv[:, t, 256 * i:256 * i + 256], rms="x")
                for i in range(4):
                    copy_product(layer, f"xd{i}", lambda t: xd[:, t, 388 * i:388 * i + 388], rms="x")
                for i in range(5):
                    b = wait_bank(layer, f"qkT{i}")
                    act.activation(qkT[1][0:DB, 2 * i:2 * i + 2, :].rearrange("p h t -> p (h t)"), b[0:DB, :],
                                   ACT.Copy).then_inc(*AC.mark(f"qkT{i}"))
                softmax(layer, 0, sc)
                softmax(layer, 1, sc)
                act.wait_ge(*DV_.at(layer, "pad"))

                def channels(i):
                    b = wait_bank(layer, f"xT{i}")
                    act.activation(xc[:, 2 * i:2 * i + 2, TAPS - 1:], b[:, :].rearrange("p (k t) -> p k t", k=2),
                                   ACT.Copy).then_inc(*AC.mark(f"xT{i}"))

                channels(0)
                channels(1)
                turned_weights(layer, 0)
                softmax(layer, 2, sc)
                channels(2)
                channels(3)
                turned_weights(layer, 1)
                softmax(layer, 3, sc)
                channels(4)
                channels(5)
                turned_weights(layer, 2)
                softmax(layer, 4, sc)
                turned_weights(layer, 3)
                softmax(layer, 5, sc)
                act.wait_ge(*DV_.at(layer, "dt_u"))
                act.activation(dt_v, dt_v, ACT.Exp).then_inc(*AC.mark())
                act.activation(ea, prm[:, 16:32], ACT.Exp).then_inc(*AC.mark())
                act.wait_ge(*AC.now(layer))
                act.activation(dt_v, dt_v, ACT.Ln, bias=1.0).then_inc(*AC.mark("dt_ln"))
                turned_weights(layer, 4)
                turned_weights(layer, 5)
                act.wait_ge(*DV_.at(layer, "conv"))
                for i in range(3):
                    act.activation(cv[:, 4 * i:4 * i + 4, :], cv[:, 4 * i:4 * i + 4, :], ACT.Silu)\
                        .then_inc(*AC.mark("conv_silu"))
                copy_product(layer, "z0", lambda t: zs[:, t, 0:512], ACT.Silu, "x")
                operand(layer, "attT0")
                operand(layer, "attT1")
                for i in range(4):
                    t, half = i // 2, i % 2
                    b = wait_bank(layer, f"xsT{i}")
                    act.activation(xs[:, t, 512 * half:512 * half + 512], b[:, :], ACT.Copy)\
                        .then_inc(*AC.mark(f"xs{i}"))
                for hp in range(SH // 2):
                    if hp == 1:
                        copy_product(layer, "z1", lambda t: zs[:, t, 512:1024], ACT.Silu, "x")
                    b = wait_bank(layer, f"cr{hp}")
                    act.wait_ge(*DV_.at(layer, f"cr{hp}"))
                    E = Ex[:, hp % 2, :, :]
                    for u in range(2):
                        act.activation(E[:, u, P:2 * P], b[:, (2 * u + 1) * P:(2 * u + 2) * P], ACT.Exp,
                                       bias=ncx[:, 2 * hp + u:2 * hp + u + 1]).then_inc(*AC.mark(f"cr{hp}"))
                    both = E.rearrange("p u (b t) -> p u b t", b=3)
                    for c in (0, 2):
                        act.activation(both[:, :, c, :], both[:, :, c, :], ACT.Exp).then_inc(*AC.mark(f"ex{hp}"))
                act.wait_ge(*DV_.at(layer, "ysz"))
                for t in range(NT):
                    for g in range(2):
                        c = M_HG + 2 * t + g
                        act.activation(zs[:, t, 512 * g:512 * g + 512], ys[:, t, 512 * g:512 * g + 512], ACT.Square,
                                       scale=(SI // 2) ** -0.5,
                                       accum_out=small[:, c:c + 1]).then_inc(*AC.mark("ms.s"))
                for i in range(4):
                    operand(layer, f"ssT{i}")
                for i in range(4):
                    norm_operand(layer, f"mT{i}")
                squares(layer, "mT")
                feed_forward(layer)

            act.wait_ge(shifted, 1)
            act.activation(sinb, angs, ACT.Sin).then_inc(trig, 1)
            act.activation(cosb, wrap, ACT.Sin).then_inc(trig, 1)
            act.activation(lbw[:, 0:8], lbw[:, 0:8], ACT.Exp).then_inc(lb_exp, 1)
            for block, body in enumerate((body_a, body_b)):
                with act.Fori(0, DEPTH) as l:
                    body((block, l))
                AC.end()
            act.wait_ge(*DV_.final("x_ffn3"))
            for t in range(NT):
                act.activation(hrow[:, t, :], x[:, t, :], ACT.Square, scale=D ** -0.5, accum_out=small[:, t:t + 1])\
                    .then_inc(fin_ms, 1)

        @block_.vector
        def _(dve):
            split = [0]

            def split_until(layer, n, j=None):
                o = ORD[layer[0]]
                for s in range(split[0], min(n, o.slots)):
                    dve.wait_ge(*name_at(AC, layer, "hi", s, j))
                    w = o.words(s)
                    dve.tensor_tensor(w_lo[:, s % RING, 0:w], w_raw[:, s % RING, 0:w],
                                      w_hi[:, s % RING, 0:w].bitcast(F32), ALU.subtract)\
                        .then_inc(*DV_.mark(slot_name(layer, "lo", s)))
                split[0] = max(split[0], min(n, o.slots))

            def wait_bank(layer, name):
                split_until(layer, ORD[layer[0]].before["misc", name] + LOOK)
                dve.wait_ge(*PE.at(layer, name))
                return misc[ORD[layer[0]].turn[name] % 4]

            def wait_product(layer, name):
                o = ORD[layer[0]]
                end = o.chunk_end(name)
                split_until(layer, end + LOOK)
                dve.wait_ge(*name_at(PE, layer, "used", end - 1))
                pair = o.pair[name]
                return acc if o.chunks[name].wide else acc[2 * pair:2 * pair + 2]

            def operand(layer, name):
                where, tile, n, scale = OPERANDS[layer[0]][name]
                split_until(layer, ORD[layer[0]].before["misc", name] + LOOK)
                dve.wait_ge(*AC.at(layer, f"hi.{name}"))
                b = misc[ORD[layer[0]].turn[name] % 4]
                hi, lo = (s[:, tile:tile + n, :].rearrange("p k t -> p (k t)") for s in stat[where])
                dve.scalar_tensor_tensor(out=lo, in0=b[:, 0:n * T], scalar=scale, in1=hi.bitcast(F32),
                                         op0=ALU.mult, op1=ALU.subtract).then_inc(*DV_.mark(name))

            def norm_operand(layer, name):
                kind, i = name[:2], int(name[2])
                split_until(layer, ORD[layer[0]].before["misc", name] + LOOK)
                b = misc[ORD[layer[0]].turn[name] % 4]
                dve.wait_ge(*AC.at(layer, f"hi.{name}"))
                for k in range(2):
                    dve.scalar_tensor_tensor(out=h_lo[:, 2 * i + k, :], in0=b[:, k * T:(k + 1) * T],
                                             scalar=gcol[:, kind == "mT", 2 * i + k:2 * i + k + 1],
                                             in1=h_hi[:, 2 * i + k, :].bitcast(F32), op0=ALU.mult,
                                             op1=ALU.subtract).then_inc(*DV_.mark(name))

            def row_max(layer, g, scale):
                block = layer[0]
                b = wait_bank(layer, f"S{g}")
                if g >= 2:
                    dve.wait_ge(*PE.at(layer, f"PT{g - 2}"))
                n, keys, off = (4, P, 0) if g < 2 else (2, T, P)
                base = (C_BIASA, C_BIASB)[block] + off
                v = Sx[block][:, g % 2, :].rearrange("p (h k) -> p h k", h=n)
                bias = const[:, base:base + keys].rearrange("p (a k) -> p a k", a=1)
                dve.tensor_tensor(v, b[:, :].rearrange("p (h k) -> p h k", h=n), bc(bias, [P, n, keys]), ALU.add)\
                    .then_inc(*DV_.mark(f"Sread{g}"))
                c = (g % 4) * 4
                dve.wait_ge(*DV_.now(layer))
                dve.tensor_reduce(small[:, 128 + c:128 + c + n], v, AX.X, ALU.max).then_inc(*DV_.mark())
                dve.wait_ge(*DV_.now(layer))
                dve.tensor_scalar(small[:, 144 + c:144 + c + n], small[:, 128 + c:128 + c + n], -scale, None,
                                  ALU.mult).then_inc(*DV_.mark(f"S{g}"))

            def weighed(layer, g):
                block = layer[0]
                n, c = (4 if g < 2 else 2), (g % 4) * 4
                dve.wait_ge(*AC.at(layer, f"p{g}"))
                dve.reciprocal(small[:, 176 + c:176 + c + n], small[:, 160 + c:160 + c + n]).then_inc(*DV_.mark())
                b = wait_bank(layer, f"O{g}")
                dve.wait_ge(*DV_.now(layer))
                t, h0 = (0, 4 * g) if g < 2 else (1, 2 * g - 4)
                dst = att[block][:, t, h0 * 64:(h0 + n) * 64].rearrange("p (h d) -> p h d", h=n)
                r = small[:, 176 + c:176 + c + n].rearrange("p (h a) -> p h a", a=1)
                dve.tensor_tensor(dst, b[:, 0:n * 64].rearrange("p (h d) -> p h d", h=n), bc(r, [P, n, 64]), ALU.mult)\
                    .then_inc(*DV_.mark(f"O{g}"))

            def rotate(layer, x1, x2, cos, sin, scratch, name):
                a, b_, c, d = scratch
                for dst, u, v in ((a, x1, cos), (b_, x2, sin), (c, x1, sin), (d, x2, cos)):
                    dve.tensor_tensor(dst, u, v, ALU.mult).then_inc(*DV_.mark())
                dve.wait_ge(*DV_.now(layer))
                dve.tensor_tensor(x1, a, b_, ALU.subtract).then_inc(*DV_.mark())
                dve.tensor_tensor(x2, c, d, ALU.add).then_inc(*DV_.mark(name))

            def residual(layer, banks, names):
                for (half, t, b), name in zip(banks, names):
                    v = x[:, t, half * 512:half * 512 + 512]
                    dve.tensor_tensor(v, v, b[:, :], ALU.add).then_inc(*DV_.mark(name))

            def feed_forward(layer):
                o = ORD[layer[0]]

                def gated(s_end, step, j=None):
                    split_until(layer, s_end + LOOK, j)
                    for t in range(NT):
                        dve.wait_ge(*AC.at(layer, f"f{step}.t{t}", j))
                        b = acc[t] if step == "0" else misc[2 + t]
                        c = RS + M_Y + t
                        dve.scalar_tensor_tensor(out=f_act[:, t, :], in0=b[:, FW:2 * FW], scalar=small[:, c:c + 1],
                                                 in1=f_silu[:, t, :], op0=ALU.mult, op1=ALU.mult)\
                            .then_inc(*DV_.mark(f"f{step}"))

                def turned(s_end, step, j=None):
                    split_until(layer, s_end + LOOK, j)
                    dve.wait_ge(*AC.at(layer, f"fT{step}", j))
                    hi, lo = (s[:, 0:2, :].rearrange("p k t -> p (k t)") for s in stat["st"])
                    dve.tensor_tensor(lo, misc[0][:, :], hi.bitcast(F32), ALU.subtract)\
                        .then_inc(*DV_.mark(f"fT{step}"))

                s = o.ffn0
                gated(s + 2, "0")
                turned(s + 4, "0")
                gated(s + 8, "1")
                turned(s + 10, "1")
                s += LOOP_AT
                DV_.loop(None)
                with dve.Fori(0, LOOP_TIMES) as j:
                    gated(s + 4, "2", j)
                    turned(s + 6, "2", j)
                    gated(s + 10, "3", j)
                    turned(s + 12, "3", j)
                DV_.loop(LOOP_TIMES)
                split[0] += LOOP_SLOTS * (LOOP_TIMES - 1)
                s += LOOP_SLOTS * LOOP_TIMES
                gated(s + 4, "10")
                turned(s + 6, "10")
                split_until(layer, o.slots)
                split[0] = 0
                for half, step in enumerate(("x_half", "used-1")):
                    dve.wait_ge(*PE.at(layer, step))
                    residual(layer, [(half, t, acc[2 * half + t]) for t in range(NT)],
                             [f"x_ffn{2 * half + t}" for t in range(NT)])

            def level(layer, i):
                h = 1 << (i - 1)
                Q, K, D1, R, Y = (v.rearrange("p (b u h) -> p b u h", u=2, h=h)
                                  for v in (hQ, hK, hP, hR, X[:, i % 2, :]))
                n = 1024 // (2 * h)
                if i >= 3:
                    dve.wait_ge(*PE.at(layer, f"G{i - 2}_1"))
                dve.tensor_tensor(Y[:, :, 1, :], Q[:, :, 1, :], D1[:, :, 1, :], ALU.mult).then_inc(*DV_.mark())
                dve.tensor_tensor(Y[:, :, 0, :], K[:, :, 0, :], R[:, :, 0, :], ALU.mult).then_inc(*DV_.mark(f"X{i}"))
                if i < 8:
                    dve.wait_ge(*DV_.now(layer))
                    dve.tensor_tensor(R[:, :, 0, :], R[:, :, 0, :], bc(D1[:, :, 1, h - 1:h], [P, n, h]), ALU.mult)\
                        .then_inc(*DV_.mark())
                    dve.wait_ge(*DV_.now(layer))
                    dve.tensor_tensor(D1[:, :, 1, :], D1[:, :, 1, :], bc(D1[:, :, 0, h - 1:h], [P, n, h]), ALU.mult)\
                        .then_inc(*DV_.mark())
                    dve.wait_ge(*DV_.now(layer))

            def body_a(layer):
                sc = float(DQK) ** -0.5
                l = layer[1]
                dve.wait_ge(c_in, 32)
                dve.wait_ge(*par_at(layer))
                dve.tensor_copy(lbc[:, 0, :], lbs[:, bass.ds(l, 1), :].rearrange("p a h -> p (a h)"))\
                    .then_inc(*DV_.mark())
                dve.wait_ge(*DV_.now(layer))
                dve.tensor_scalar(lbc[:, 1, :], lbc[:, 0, :], -1.0, 1.0, ALU.mult, ALU.add).then_inc(*DV_.mark())
                for i in range(4):
                    norm_operand(layer, f"nT{i}")
                split_until(layer, ORD[0].chunk_end("mla1") + LOOK)
                dve.wait_ge(*PO.at(layer, "r.c"))
                for t in range(NT):
                    for col, a, n, g in ((M_CQ, 0, QL, G_CQ), (M_CKV, QL, KVL, G_CKV)):
                        v = zm[:, t, a:a + n]
                        dve.scalar_tensor_tensor(out=v, in0=v, scalar=small[:, RS + col + t:RS + col + t + 1],
                                                 in1=gains[:, g:g + n], op0=ALU.mult, op1=ALU.mult)\
                            .then_inc(*DV_.mark("cnorm"))
                for i in range(3):
                    operand(layer, f"cT{i}")
                split_until(layer, ORD[0].before["misc", "hfT1"] + LOOK)
                dve.wait_ge(*AC.at(layer, "hfT1"))
                for hd in range(HG):
                    cols = slice(hd * T, (hd + 1) * T)
                    lb, om = lbc[:, 0, hd:hd + 1], lbc[:, 1, hd:hd + 1]
                    dve.tensor_scalar(hP[:, cols], hP[:, cols], om, lb, ALU.mult, ALU.add).then_inc(*DV_.mark())
                    dve.tensor_scalar(hK[:, cols], hK[:, cols], om, None, ALU.mult).then_inc(*DV_.mark())
                dve.memset(hR[:, :], 1.0).then_inc(*DV_.mark("X0"))
                split_until(layer, ORD[0].chunk_end("hg") + LOOK)
                for t in range(NT):
                    dve.wait_ge(*AC.at(layer, f"hg.t{t}"))
                    dve.scalar_tensor_tensor(out=sg[:, t, :], in0=sg[:, t, :], scalar=1.0, in1=zq[:, t, :],
                                             op0=ALU.add, op1=ALU.mult).then_inc(*DV_.mark(f"hg.t{t}"))
                split_until(layer, ORD[0].chunk_end("ukv1") + LOOK)
                dve.wait_ge(*AC.at(layer, "kpe"))
                level(layer, 1)
                for t in range(NT):
                    split_until(layer, ORD[0].chunk_end(f"gate{t}") + LOOK - 4)
                    dve.wait_ge(*AC.at(layer, f"sq{t}"))
                    c = M_QK + 16 * t
                    dve.tensor_reduce(small[:, c:c + 16], sq[:, t, :, :], AX.X, ALU.add)\
                        .then_inc(*DV_.mark(f"ms.qk{t}"))
                for t in range(NT):
                    split_until(layer, ORD[0].chunk_end(f"gate{t}") + LOOK)
                    c = RS + M_QK + 16 * t
                    dve.wait_ge(*PO.at(layer, f"r.qk{t}"))
                    r = small[:, c:c + 16].rearrange("p (h a) -> p h a", a=1)
                    dve.tensor_tensor(QK[:, t, :, :], QK[:, t, :, :], bc(r, [P, 16, DQK]), ALU.mult)\
                        .then_inc(*DV_.mark())
                    dve.wait_ge(*DV_.now(layer))
                    for u in range(2):
                        v = QK[:, t, 8 * u:8 * u + 8, :]
                        g = gains[:, G_QK + DQK * u:G_QK + DQK * (u + 1)].rearrange("p (a d) -> p a d", a=1)
                        dve.tensor_tensor(v, v, bc(g, [P, 8, DQK]), ALU.mult).then_inc(*DV_.mark())
                    dve.wait_ge(*DV_.now(layer))
                    cos, sin = (bc(const[:, c0 + 16 * t:c0 + 16 * t + 16].rearrange("p (a d) -> p a d", a=1),
                                   [P, 16, 16]) for c0 in (C_COS, C_SIN))
                    rotate(layer, QK[:, t, :, NOPE:NOPE + 16], QK[:, t, :, NOPE + 16:DQK], cos, sin,
                           [rope[0][:, i, :, :] for i in range(4)], f"qk{t}")
                    dve.wait_ge(*DV_.now(layer))
                for i in range(8):
                    if i + 1 >= 2:
                        split_until(layer, ORD[0].before["misc", f"G{i}_0"] + LOOK)
                        level(layer, i + 1)
                    if 2 <= i < 8:
                        weighed(layer, i - 2)
                    if i == 0:
                        row_max(layer, 0, sc)
                        row_max(layer, 1, sc)
                    elif i < 5:
                        row_max(layer, i + 1, sc)
                    for pr in range(2):
                        split_until(layer, ORD[0].before["misc", f"G{i}_{pr}"] + LOOK)
                        b = wait_bank(layer, f"G{i}_{pr}")
                        dst = AT[:, 2 * pr:2 * pr + 2, 0:2, :]
                        src = b[:, :].rearrange("p (a b q) -> p a b q", a=2, b=2)
                        if i == 0:
                            for u in range(2):
                                dve.tensor_tensor(dst[:, u, :, :], src[:, u, :, :],
                                                  bc(ident.rearrange("p (b q) -> p b q", b=1), [P, 2, P]), ALU.mult)\
                                    .then_inc(*DV_.mark(f"G{i}_{pr}"))
                        else:
                            dve.tensor_copy(lbw[:, 0:1], b[:, 0:1]).then_inc(*DV_.mark())
                            m = masks[:, i, :].rearrange("p (a b q) -> p a b q", a=1, b=1)
                            dve.copy_predicated(out=dst, mask=bc(m, [P, 2, 2, P]), data=src)\
                                .then_inc(*DV_.mark(f"G{i}_{pr}"))
                        dve.wait_ge(*DV_.now(layer))
                operand(layer, "attT0")
                operand(layer, "attT1")
                dve.wait_ge(*PO.at(layer, "sgg"))
                for t in range(NT):
                    b = wait_bank(layer, f"oH{t}")
                    c = RS + M_HG + 4 * t
                    dve.wait_ge(*PO.at(layer, f"r.h{t}"))
                    r = small[:, c:c + 4].rearrange("p (h a) -> p h a", a=1)
                    dve.tensor_tensor(oh[:, t, :].rearrange("p (h d) -> p h d", h=HG),
                                      b[:, :].rearrange("p (h d) -> p h d", h=HG), bc(r, [P, HG, DK]), ALU.mult)\
                        .then_inc(*DV_.mark(f"oH{t}"))
                    dve.wait_ge(*DV_.now(layer))
                    dve.tensor_tensor(oh[:, t, :], oh[:, t, :], sg[:, t, :], ALU.mult).then_inc(*DV_.mark(f"oh{t}"))
                def gated_sum(name, i, off):
                    banks = wait_product(layer, f"{name}{i}")
                    for t in range(NT):
                        v = gate[:, t, off + 512 * i:off + 512 * i + 512]
                        dve.scalar_tensor_tensor(out=v, in0=v, scalar=1.0, in1=banks[t][:, :],
                                                 op0=ALU.add, op1=ALU.mult).then_inc(*DV_.mark(f"{name}{i}.t{t}"))
                dve.wait_ge(*AC.at(layer, "gate3.t1"))
                gated_sum("pa", 0, 0)
                gated_sum("pa", 1, 0)
                operand(layer, "hgT0")
                operand(layer, "hgT1")
                for i in range(2):
                    gated_sum("pb", i, D)
                    dve.wait_ge(*DV_.now(layer))
                    for t in range(NT):
                        v = gate[:, t, 512 * i:512 * i + 512]
                        dve.tensor_tensor(v, v, gate[:, t, D + 512 * i:D + 512 * i + 512], ALU.add)\
                            .then_inc(*DV_.mark(f"y{i}"))
                for i in range(4):
                    operand(layer, f"yT{i}")
                for i in range(2):
                    banks = wait_product(layer, f"wo{i}")
                    residual(layer, [(i, t, banks[t]) for t in range(NT)], [f"wo{i}.t{t}" for t in range(NT)])
                for i in range(4):
                    norm_operand(layer, f"mT{i}")
                feed_forward(layer)

            def body_b(layer):
                sc = float(DB) ** -0.5
                dve.wait_ge(*par_at(layer))
                for i in range(4):
                    norm_operand(layer, f"nT{i}")
                dve.memset(xc[:, :, 0:TAPS - 1], 0.0).then_inc(*DV_.mark("pad"))
                b = wait_bank(layer, "cvT0")
                dve.tensor_copy(conv[:, 0:48], b[:, 0:48]).then_inc(*DV_.mark("cvT0"))
                b = wait_bank(layer, "cvT1")
                dve.tensor_copy(conv[:, 48:60], b[:, 48:60]).then_inc(*DV_.mark("cvT1"))
                split_until(layer, ORD[1].chunk_end("qkv2") + LOOK)
                dve.wait_ge(*AC.at(layer, "qkv2.t1"))
                qk = zqkv[:, :, 0:640].rearrange("p t (h d) -> p t h d", h=10)
                cos, sin = (bc(v.rearrange("p (t a d) -> p t a d", t=NT, a=1), [P, NT, 10, 8]) for v in (cosb, sinb))
                dve.wait_ge(trig, 2)
                rotate(layer, qk[:, :, :, 0:8], qk[:, :, :, 8:16], cos, sin,
                       [rope[1][:, i, :, :].rearrange("p (t h) d -> p t h d", t=NT) for i in range(4)], "qk")
                split_until(layer, ORD[1].chunk_end("xd3") + LOOK)
                dve.wait_ge(*AC.at(layer, "xd3.t1"))
                v3 = [v.rearrange("p (t h) -> p t h", t=NT) for v in (dt_u, dt_m, dt_v, dt_a)]
                one_row = prm[:, 0:16].rearrange("p (a h) -> p a h", a=1)
                dve.tensor_tensor(v3[0], xd[:, :, XBC:XD], bc(one_row, [P, NT, 16]), ALU.add).then_inc(*DV_.mark())
                dve.wait_ge(*DV_.now(layer))
                dve.tensor_scalar(dt_m, dt_u, 0.0, None, ALU.max).then_inc(*DV_.mark())
                dve.tensor_scalar(dt_a, dt_u, -1.0, None, ALU.mult).then_inc(*DV_.mark())
                dve.wait_ge(*DV_.now(layer))
                dve.tensor_tensor(dt_v, dt_u, dt_a, ALU.min).then_inc(*DV_.mark("dt_u"))

                def convolve(g):
                    for i in (2 * g, 2 * g + 1):
                        split_until(layer, ORD[1].before["misc", f"xT{i}"] + LOOK)
                        dve.wait_ge(*AC.at(layer, f"xT{i}"))
                        for k in (2 * i, 2 * i + 1):
                            dve.tensor_scalar(cv[:, k, :], xc[:, k, 3:3 + T], conv[:, 36 + k:37 + k],
                                              conv[:, 48 + k:49 + k], ALU.mult, ALU.add).then_inc(*DV_.mark())
                    for tap in range(3):
                        dve.wait_ge(*DV_.now(layer))
                        for k in range(4 * g, 4 * g + 4):
                            dve.scalar_tensor_tensor(out=cv[:, k, :], in0=xc[:, k, tap:tap + T],
                                                     scalar=conv[:, 12 * tap + k:12 * tap + k + 1],
                                                     in1=cv[:, k, :], op0=ALU.mult, op1=ALU.add)\
                                .then_inc(*DV_.mark("conv"))

                row_max(layer, 0, sc)
                row_max(layer, 1, sc)
                row_max(layer, 2, sc)
                convolve(0)
                weighed(layer, 0)
                row_max(layer, 3, sc)
                convolve(1)
                weighed(layer, 1)
                row_max(layer, 4, sc)
                weighed(layer, 2)
                row_max(layer, 5, sc)
                convolve(2)
                weighed(layer, 3)
                dve.wait_ge(*AC.at(layer, "dt_ln"))
                dve.tensor_tensor(dt_m, dt_m, dt_v, ALU.add).then_inc(*DV_.mark("dt"))
                dve.wait_ge(*DV_.now(layer))
                ea3 = bc(ea.rearrange("p (a h) -> p a h", a=1), [P, NT, 16])
                dve.scalar_tensor_tensor(out=v3[3], in0=v3[1], scalar=-1.0, in1=ea3, op0=ALU.mult, op1=ALU.mult)\
                    .then_inc(*DV_.mark("dt_a"))
                weighed(layer, 4)
                weighed(layer, 5)
                operand(layer, "attT0")
                operand(layer, "attT1")
                for i in range(4):
                    t, half = i // 2, i % 2
                    dve.wait_ge(*AC.at(layer, f"xs{i}"))
                    b = misc[ORD[1].turn[f"xsT{i}"] % 4]
                    r = dt_m[:, 16 * t + 8 * half:16 * t + 8 * half + 8].rearrange("p (h a) -> p h a", a=1)
                    dve.tensor_tensor(xdt[:, t, 512 * half:512 * half + 512].rearrange("p (h d) -> p h d", h=8),
                                      b[:, :].rearrange("p (h d) -> p h d", h=8), bc(r, [P, 8, SP]), ALU.mult)\
                        .then_inc(*DV_.mark(f"xsT{i}"))
                for g in range(2):
                    b = wait_bank(layer, f"cb{g}")
                    dve.tensor_tensor(cbm[:, g, 0:P], b[:, 0:P], tri, ALU.mult).then_inc(*DV_.mark())
                    dve.tensor_copy(cbm[:, g, P:2 * P], b[:, P:2 * P]).then_inc(*DV_.mark())
                    dve.tensor_tensor(cbm[:, g, 2 * P:3 * P], b[:, 2 * P:3 * P], tri, ALU.mult)\
                        .then_inc(*DV_.mark(f"cb{g}"))
                b = wait_bank(layer, "cs")
                dve.tensor_copy(cs, b[:, 0:48]).then_inc(*DV_.mark("cs"))
                dve.wait_ge(*DV_.now(layer))
                dve.tensor_tensor(ncx, cs[:, 32:48], cs[:, 0:16], ALU.subtract).then_inc(*DV_.mark())

                def head_pair_out(hp):
                    b = wait_bank(layer, f"y{hp}")
                    cols = slice(2 * hp * SP, (2 * hp + 2) * SP)
                    dve.tensor_tensor(ys[:, :, cols], b[:, 0:T].rearrange("p (t c) -> p t c", t=NT), xs[:, :, cols],
                                      ALU.add).then_inc(*DV_.mark(f"y{hp}"))

                dve.wait_ge(*PO.at(layer, "xsd"))
                for hp in range(SH // 2):
                    b = wait_bank(layer, f"cr{hp}")
                    if hp >= 2:
                        dve.wait_ge(*PE.at(layer, f"y{hp - 2}"))
                    E = Ex[:, hp % 2, :, :]
                    for u in range(2):
                        hd = 2 * hp + u
                        for t in range(NT):
                            dve.tensor_scalar(E[:, u, 2 * t * P:(2 * t + 1) * P],
                                              b[:, (2 * u + t) * P:(2 * u + t + 1) * P],
                                              cs[:, 16 * t + hd:16 * t + hd + 1], 0.0, ALU.subtract, ALU.min)\
                                .then_inc(*DV_.mark(f"cr{hp}"))
                    if hp >= 1:
                        head_pair_out(hp - 1)
                    dve.wait_ge(*AC.at(layer, f"ex{hp}"))
                    g = cbm[:, hp // 4, :].rearrange("p (a k) -> p a k", a=1)
                    dve.tensor_tensor(E, E, bc(g, [P, 2, 384]), ALU.mult).then_inc(*DV_.mark(f"M{hp}"))
                head_pair_out(SH // 2 - 1)
                dve.wait_ge(*DV_.now(layer))
                dve.wait_ge(*AC.at(layer, "z1.t1"))
                for t in range(NT):
                    dve.tensor_tensor(ys[:, t, :], ys[:, t, :], zs[:, t, :], ALU.mult).then_inc(*DV_.mark("ysz"))
                dve.wait_ge(*PO.at(layer, "r.s"))
                for t in range(NT):
                    for g in range(2):
                        c = RS + M_HG + 2 * t + g
                        v = ys[:, t, 512 * g:512 * g + 512]
                        dve.scalar_tensor_tensor(out=v, in0=v, scalar=small[:, c:c + 1],
                                                 in1=gains[:, G_SSM + 512 * g:G_SSM + 512 * g + 512],
                                                 op0=ALU.mult, op1=ALU.mult).then_inc(*DV_.mark("ys"))
                for i in range(4):
                    operand(layer, f"ssT{i}")
                for i in range(2):
                    banks = wait_product(layer, f"wo{i}")
                    residual(layer, [(i, t, banks[t]) for t in range(NT)], [f"wo{i}.t{t}" for t in range(NT)])
                for i in range(4):
                    norm_operand(layer, f"mT{i}")
                feed_forward(layer)

            dve.memset(small[:, 192:193], -0.5).then_inc(DV_.sem, DV_.seed())
            dve.memset(small[:, 193:194], -0.5).then_inc(PE.sem, PE.seed())
            dve.memset(small[:, 194:195], -0.5).then_inc(AC.sem, AC.seed())
            dve.memset(small[:, 195:208], -0.5).then_inc(PO.sem, PO.seed())
            dve.memset(rows[:, :], 0.0).then_inc(rows_0, 1)
            dve.memset(halves[:, :], 0.5).then_inc(rows_0, 1)
            dve.memset(epsilons[:, 0:16], EPS_A).then_inc(chain, 1)
            dve.memset(epsilons[:, 16:32], EPS_B).then_inc(chain, 1)
            dve.wait_ge(pos_in, 16)
            dve.wait_ge(c_in, 32)
            n = [2]

            def link(ins):
                ins.then_inc(chain, 1)
                n[0] += 1
                dve.wait_ge(chain, n[0])

            link(dve.tensor_copy(masks[:, :, :], carve(0, 8, P)))
            link(dve.tensor_copy(posf, posi[:, :]))
            for t in range(NT):
                link(dve.tensor_scalar(dt_u[:, 8 * t:8 * t + 8], const[:, C_INV:C_INV + 8], posf[:, t:t + 1], None,
                                       ALU.mult))
            ang = dt_u[:, 0:16]
            magic = 1.5 * 2.0 ** 23
            tau_parts = (6.28125, 0.0019350051879882812, 3.019916050561733e-07)
            for dst, quarter in ((angs, 0.0), (wrap, 0.25)):
                link(dve.tensor_scalar(turns_, ang, 1.0 / (2.0 * math.pi), quarter, ALU.mult, ALU.add))
                link(dve.tensor_scalar(turns_, turns_, magic, None, ALU.add))
                link(dve.tensor_scalar(turns_, turns_, -magic, None, ALU.add))
                link(dve.tensor_copy(dst, ang))
                for part in tau_parts:
                    link(dve.scalar_tensor_tensor(out=dst, in0=turns_, scalar=-part, in1=dst, op0=ALU.mult,
                                                  op1=ALU.add))
                if quarter:
                    link(dve.tensor_scalar(dst, dst, math.pi / 2, None, ALU.add))
                link(dve.tensor_scalar(dst, dst, 3.1415925, -3.1415925, ALU.min, ALU.max))
            dve.wait_ge(lb_T, 1)
            link(dve.tensor_copy(lbw[:, 0:8], misc[3][:, 0:8]))
            link(dve.tensor_tensor(lbw[:, 8:12], lbw[:, 0:4], lbw[:, 4:8], ALU.max))
            link(dve.tensor_tensor(lbw[:, 0:4], lbw[:, 0:4], lbw[:, 8:12], ALU.subtract))
            dve.tensor_tensor(lbw[:, 4:8], lbw[:, 4:8], lbw[:, 8:12], ALU.subtract).then_inc(shifted, 1)
            dve.wait_ge(lb_exp, 1)
            link(dve.tensor_tensor(lbw[:, 8:12], lbw[:, 0:4], lbw[:, 4:8], ALU.add))
            link(dve.reciprocal(lbw[:, 8:12], lbw[:, 8:12]))
            link(dve.tensor_tensor(lbw[:, 0:4], lbw[:, 0:4], lbw[:, 8:12], ALU.mult))
            link(dve.tensor_tensor(lbw[:, 4:8], lbw[:, 4:8], lbw[:, 8:12], ALU.mult))
            link(dve.tensor_tensor(lbs[:, 0, :], lbw[:, 0:4], lbw[:, 0:4], ALU.subtract))
            link(dve.tensor_tensor(lbw[:, 12:16], lbw[:, 0:4], lbw[:, 4:8], ALU.add))
            link(dve.tensor_tensor(lbw[:, 12:16], lbw[:, 12:16], lbw[:, 0:4], ALU.subtract))
            link(dve.tensor_scalar(lbs[:, 1, :], lbw[:, 12:16], 0.0, None, ALU.max))
            for block, body in enumerate((body_a, body_b)):
                with dve.Fori(0, DEPTH) as l:
                    body((block, l))
                DV_.end()
            dve.wait_ge(fin_in, 16)
            dve.wait_ge(fin_r, 1)
            for t in range(NT):
                dve.scalar_tensor_tensor(out=hrow[:, t, :], in0=x[:, t, :], scalar=small[:, RS + t:RS + t + 1],
                                         in1=gains[:, 0:D], op0=ALU.mult, op1=ALU.mult).then_inc(fin_rows, 1)

        @block_.gpsimd
        def _(pool):
            def inverse_rms(layer, col, n, name, eps):
                pool.tensor_tensor(small[:, RS + col:RS + col + n], small[:, col:col + n],
                                   epsilons[:, 16 * eps:16 * eps + n], ALU.add).then_inc(*PO.mark())
                pool.wait_ge(*PO.now(layer))
                pool.tensor_tensor(small[:, RS + col:RS + col + n], small[:, RS + col:RS + col + n],
                                   small[:, 192:192 + n], ALU.pow).then_inc(*PO.mark(name))

            def body_a(layer):
                pool.wait_ge(*AC.at(layer, "ms.nT"))
                inverse_rms(layer, M_X, 2, None, 0)
                pool.wait_ge(*PO.now(layer))
                pool.tensor_tensor(small[:, RS + M_H:RS + M_H + 2], small[:, RS + M_X:RS + M_X + 2],
                                   halves[:, 0:2], ALU.mult).then_inc(*PO.mark("r.nT"))
                pool.wait_ge(*AC.at(layer, "ms.c"))
                inverse_rms(layer, M_CQ, 4, "r.c", 0)
                pool.wait_ge(*par_at(layer))
                for t in range(NT):
                    pool.wait_ge(*DV_.at(layer, f"hg.t{t}"))
                    v = sg[:, t, :].rearrange("p (h d) -> p h d", h=HG)
                    g = gains[:, G_HG:G_HG + DK].rearrange("p (a d) -> p a d", a=1)
                    pool.tensor_tensor(v, v, bc(g, [P, HG, DK]), ALU.mult).then_inc(*PO.mark("sgg"))
                for t in range(NT):
                    pool.wait_ge(*DV_.at(layer, f"ms.qk{t}"))
                    c = M_QK + 16 * t
                    inverse_rms(layer, c, 16, f"r.qk{t}", 0)
                for t in range(NT):
                    pool.wait_ge(*AC.at(layer, f"ms.h{t}"))
                    c = M_HG + 4 * t
                    inverse_rms(layer, c, 4, f"r.h{t}", 0)
                pool.wait_ge(*AC.at(layer, "ms.mT"))
                inverse_rms(layer, M_Y, 2, "r.mT", 0)

            def body_b(layer):
                pool.wait_ge(*AC.at(layer, "ms.nT"))
                inverse_rms(layer, M_X, 2, "r.nT", 1)
                pool.wait_ge(*par_at(layer))
                for i in range(4):
                    t, half = i // 2, i % 2
                    pool.wait_ge(*AC.at(layer, f"xs{i}"))
                    v = xs[:, t, 512 * half:512 * half + 512].rearrange("p (h d) -> p h d", h=8)
                    dsk = prm[:, 32 + 8 * half:40 + 8 * half].rearrange("p (h a) -> p h a", a=1)
                    pool.tensor_tensor(v, v, bc(dsk, [P, 8, SP]), ALU.mult).then_inc(*PO.mark("xsd"))
                pool.wait_ge(*AC.at(layer, "ms.s"))
                inverse_rms(layer, M_HG, 4, "r.s", 1)
                pool.wait_ge(*AC.at(layer, "ms.mT"))
                inverse_rms(layer, M_Y, 2, "r.mT", 1)

            for block, body in enumerate((body_a, body_b)):
                with pool.Fori(0, DEPTH) as l:
                    body((block, l))
                PO.end()
            pool.wait_ge(fin_ms, 2)
            pool.tensor_tensor(small[:, RS:RS + 2], small[:, 0:2], epsilons[:, 16:18], ALU.add).then_inc(fin_ms, 1)
            pool.wait_ge(fin_ms, 3)
            pool.tensor_tensor(small[:, RS:RS + 2], small[:, RS:RS + 2], small[:, 192:194], ALU.pow)\
                .then_inc(fin_r, 1)


def constants():
    q, k = np.arange(P)[None, :], np.arange(P)[:, None]
    const = np.zeros((P, C_END), np.float32)
    const[:, C_ID:C_ID + P] = np.eye(P)
    const[:, C_TRI:C_TRI + P] = k <= q
    rows, low = np.arange(P)[:, None], np.float32(-1e30)
    scale_b = float(DB) ** -0.5
    for tile, at, keys in ((0, 0, P), (1, P, T)):
        delta = (rows + tile * P) - np.arange(keys)[None, :]
        const[:, C_BIASA + at:C_BIASA + at + keys] = np.where(delta >= 0, 0.0, low)
        times = sum(((delta >= 0) & (delta <= w) & (delta % d == 0)).astype(int)
                    for w, d in ((128, 1), (512, 4), (2048, 16)))
        const[:, C_BIASB + at:C_BIASB + at + keys] = np.where(
            times > 0, np.log(np.maximum(times, 1)) / scale_b, low)
    inv = (1.0 / (np.float32(10000.0) ** (np.arange(0, RA, 2, dtype=np.float32) / RA))).astype(np.float32)
    ang = np.arange(T, dtype=np.float32)[:, None] * inv[None, :]
    for t in range(NT):
        const[:, C_COS + 16 * t:C_COS + 16 * t + 16] = np.cos(ang[t * P:(t + 1) * P])
        const[:, C_SIN + 16 * t:C_SIN + 16 * t + 16] = np.sin(ang[t * P:(t + 1) * P])
    const[:, C_INV:C_INV + 8] = np.float32(500000.0) ** (-np.arange(0, RB, 2, dtype=np.float32) / RB)
    masks = np.zeros((P, 8, P), np.float32)
    masks[:, 0, :] = np.eye(P)
    for i in range(1, 8):
        h = 1 << (i - 1)
        masks[:, i, :] = (k // (2 * h) == q // (2 * h)) & (k // h % 2 == 0) & (q // h % 2 == 1)
    return const, masks


FLAT = {"w_in": IN_A, "mla_w_uq": HA * DQK, "mla_w_ukv": HA * (NOPE + DV), "w_proj_a": D, "w_proj_b": D,
        "w_out": D, "w_gate": FF, "w_up": FF, "w_down": D, "w_in_2": IN_B, "w_out_2": D, "w_gate_2": FF,
        "w_up_2": FF, "w_down_2": D, "x": D, "conv_w_2": P, "conv_b_2": P}
NAMES = ["x", "norm_mix", "w_in", "mla_norm_cq", "mla_w_uq", "mla_norm_ckv", "mla_w_ukv", "mla_q_norm",
         "mla_k_norm", "hg_lb_logits", "hg_out_norm", "w_proj_a", "w_proj_b", "w_out", "norm_ffn", "w_gate",
         "w_up", "w_down", "positions_2", "norm_mix_2", "w_in_2", "conv_w_2", "conv_b_2", "dt_bias_2", "a_log_2",
         "d_skip_2", "ssm_norm_2", "w_out_2", "norm_ffn_2", "w_gate_2", "w_up_2", "w_down_2", "final_norm_2"]


def program(nc, arrays, table):
    A = {name: nc.dram_tensor(f"in_{name}", a.shape, mybir.dt.from_np(a.dtype), kind="ExternalInput").ap()
         for name, a in arrays.items()}
    out = nc.dram_tensor("out_0", (T, D), F32, kind="ExternalOutput").ap()
    build(nc, A, out, table)


def kernel(**inputs):
    import concourse.bacc as bacc
    from concourse.bass_utils import run_bass_kernel_spmd

    arrays = {}
    for name in NAMES:
        a = np.ascontiguousarray(inputs[name])
        if name in FLAT:
            a = a.reshape(-1, FLAT[name])
        elif name == "positions_2":
            a = a.reshape(-1)
        arrays[name] = a
    arrays["const"], arrays["masks"] = constants()
    table = {}
    for _ in range(2):
        nc = bacc.Bacc("TRN2", target_bir_lowering=False, num_devices=1)
        program(nc, arrays, table)
    r = run_bass_kernel_spmd(nc, [{f"in_{name}": a for name, a in arrays.items()}], core_ids=[0])
    return r.results[0]["out_0"].reshape(1, T, D)
```

```python
import math
from contextlib import ExitStack

import numpy as np
import concourse.bass as bass
from concourse import mybir

F32 = mybir.dt.float32
F32R = mybir.dt.float32r
I32 = mybir.dt.int32
U8 = mybir.dt.uint8
ALU = mybir.AluOpType
ACT = mybir.ActivationFunctionType
AX = mybir.AxisListType

P = 128
T = 256
NT = T // P
D = 1024
KD = D // P
DEPTH = 2
FF = 2816
FW = 256
FSTEPS = FF // FW
RING = 4
SLOT = 1024

QL, KVL, RA = 384, 256, 32
HA, NOPE, DQK, DV = 8, 64, 96, 64
HG, DK = 4, 128
IN_A = 4768
EPS_A = 1e-6
HB, HKV, DB = 8, 2, 64
RB = 16
SH, SP, SI, SN = 16, 64, 1024, 128
XBC = 1536
TAPS = 4
IN_B = 3344
XD = XBC + SH
EPS_B = 1e-5

C_ID, C_TRI, C_BIASA, C_BIASB = 0, 128, 256, 640
C_COS, C_SIN, C_INV, C_END = 1024, 1056, 1088, 1096
G_CQ, G_CKV, G_QK, G_HG = 0, QL, QL + KVL, QL + KVL + 2 * DQK
G_SSM = 0
M_X, M_CQ, M_CKV, M_QK, M_HG, M_Y, M_H, RS = 0, 2, 4, 8, 40, 48, 50, 64


class Progress:

    def __init__(self, nc, ctx, name, table):
        self.sem = ctx.enter_context(nc.semaphore(name))
        self.table, self.old = table.setdefault(name, {}), dict(table.setdefault(name, {}))
        self.k, self.block, self.inner = 0, 0, None

    def per(self, block):
        return self.old.get((block, "layer"), 1)

    def body(self, block):
        return self.old.get((block, "loop"), 1)

    def seed(self):
        return self.per(0)

    def mark(self, name=None):
        self.k += 1
        if name is not None:
            self.table[self.block, name] = self.k
        return self.sem, 1

    def at(self, layer, name, j=None):
        block, l = layer
        turns = 0
        if name is None:
            k = self.k
        elif self.old:
            if name.endswith("@last"):
                name, turns = name[:-5], LOOP_TIMES - 1
            k = self.old[block, name] + turns * self.body(block)
        else:
            k = 1
        base = self.seed() + (DEPTH * self.per(0) if block else 0) + k
        value = l * self.per(block) + base
        return self.sem, value if j is None else value + j * self.body(block)

    def now(self, layer, j=None):
        return self.at(layer, None, j)

    def before(self, layer, name):
        block, l = layer
        left = [self.per(b) - self.old.get((b, name), 1) for b in (0, 1)]
        assert not self.old or left[0] == left[1], (name, left)
        return self.sem, l * self.per(block) + (self.seed() + (DEPTH * self.per(0) if block else 0) - left[0])

    def final(self, name):
        return self.sem, self.seed() + DEPTH * self.per(0) + (DEPTH - 1) * self.per(1) + self.old.get((1, name), 1)

    def loop(self, times):
        if times is None:
            self.inner = self.k
        else:
            body = self.k - self.inner
            self.table[self.block, "loop"] = body
            self.k = self.inner + times * body

    def end(self):
        self.table[self.block, "layer"] = self.k
        self.k = 0
        self.block += 1


class Chunk:

    def __init__(self, name, weight, rows, col, ncols, nk, ktiles, stat, tile0, wide=False):
        self.name, self.weight, self.rows, self.col, self.ncols = name, weight, rows, col, ncols
        self.ktiles, self.stat, self.tile0, self.wide = ktiles, stat, tile0, wide
        self.slots = [(k, min(nk, ktiles - k)) for k in range(0, ktiles, nk)]


def plan_a():
    ch = {}

    def add(*args, **kw):
        ch[args[0]] = Chunk(*args, **kw)

    for i in range(2):
        add(f"mla{i}", "w_in", D, 336 * i, 336, 2, KD, "h", 0)
    for i, n in enumerate(("hq", "hf", "hi", "hg")):
        add(n, "w_in", D, 672 + 512 * i, 512, 2, KD, "h", 0)
    for i in range(4):
        add(f"gate{i}", "w_in", D, 2720 + 512 * i, 512, 2, KD, "h", 0)
    for i in range(2):
        add(f"uq{i}", "mla_w_uq", QL, 384 * i, 384, 2, 3, "st", 0)
        add(f"ukv{i}", "mla_w_ukv", KVL, 512 * i, 512, 2, 2, "st", 3)
        add(f"pa{i}", "w_proj_a", 512, 512 * i, 512, 2, 4, "st", 0)
        add(f"pb{i}", "w_proj_b", 512, 512 * i, 512, 2, 4, "h", 4)
        add(f"wo{i}", "w_out", D, 512 * i, 512, 2, KD, "h", 0)

    def whole(n):
        return [("slot", n, i) for i in range(len(ch[n].slots))]

    plan = [("misc", f"nT{i}") for i in range(4)]
    plan += whole("mla0") + whole("mla1") + whole("hq") + whole("hf")
    plan += [("misc", f"cT{i}") for i in range(3)]
    plan += whole("hi")
    plan += [("misc", n) for n in ("hqT0", "hqT1", "hfT0", "hfT1")]
    plan += whole("hg") + whole("uq0") + whole("uq1") + whole("ukv0") + whole("ukv1")
    ahead = whole("gate1")
    plan += whole("gate0") + ahead[:-1] + [("misc", f"qkT{i}") for i in range(8)] + ahead[-1:]
    spare = whole("gate2") + whole("gate3")
    for i in range(8):
        if 2 <= i < 8:
            plan.append(("misc", f"O{i - 2}"))
        if 1 <= i < 7:
            plan.append(("misc", f"PT{i - 1}"))
        if i == 0:
            plan += [("misc", "S0"), ("misc", "S1")]
        elif i < 5:
            plan.append(("misc", f"S{i + 1}"))
        plan += [("misc", f"G{i}_0"), ("misc", f"G{i}_1"), spare.pop(0)]
    plan += [("misc", "GX"), ("misc", "attT0"), ("misc", "attT1"), ("misc", "oH0"), ("misc", "oH1")]
    plan += whole("pa0") + [("misc", "hgT0"), ("misc", "hgT1")] + whole("pa1") + whole("pb0")
    halves, first, last = whole("pb1"), whole("wo0"), whole("wo1")
    plan += halves[:1] + [("misc", "yT0"), ("misc", "yT1")] + halves[1:]
    plan += first[:1] + [("misc", "yT2"), ("misc", "yT3")] + first[1:] + last[:-1] + [("misc", "mT0"), ("misc", "mT1"), last[-1], ("misc", "mT2"), ("misc", "mT3")]
    return ch, plan


def plan_b():
    ch = {}

    def add(*args, **kw):
        ch[args[0]] = Chunk(*args, **kw)

    for i in range(3):
        add(f"qkv{i}", "w_in_2", D, 256 * i, 256, 4, KD, "h", 0)
    for i in range(4):
        add(f"xd{i}", "w_in_2", D, 1792 + 388 * i, 388, 2, KD, "h", 0)
    for i in range(2):
        add(f"z{i}", "w_in_2", D, 768 + 512 * i, 512, 2, KD, "h", 0)
    for i in range(2):
        add(f"wo{i}", "w_out_2", 1536, 512 * i, 512, 2, 12, "mix", 0)

    def whole(n):
        return [("slot", n, i) for i in range(len(ch[n].slots))]

    order = """
        nT0 nT1 nT2 nT3 qkv0 qkv0 qkv1 qkv1 cvT0 cvT1 qkv2 qkv2 xd0 xd0 qkT0 qkT1 qkT2 qkT3 qkT4 xd0 S0 S1 xd0
        xd1 PT0 S2 xd1 xT0 O0 PT1 S3 xd1 O1 PT2 S4 xd1 xd2 O2 PT3 S5 xd2 xT1 O3 PT4 xd2 xT2 O4 PT5 xd2 O5
        xd3 attT0 attT1 xd3 xT3 xd3 xd3 z0 xT4 xT5 z0 z0 xsT0 xsT1 xsT2 xsT3 z0 z1 cb0 cb1 cs cr0 cr1
        z1 y0 cr2 z1 y1 cr3 z1 y2 cr4 wo0 y3 cr5 wo0 y4 cr6 wo1 y5 cr7 ssT0 ssT1 wo1 y6 y7 wo0 wo0 wo1
        ssT2 ssT3 wo1 wo0 wo0 wo1 mT0 mT1 wo1 mT2 mT3"""
    slots = {n: whole(n) for n in ch}
    plan = [slots[n].pop(0) if n in ch else ("misc", n) for n in order.split()]
    assert not any(slots.values())
    return ch, plan


class Order:

    def __init__(self, chunks, plan):
        self.chunks, self.plan = chunks, plan
        self.slot_no, self.turn, self.before, self.pair, self.pair_turn = {}, {}, {}, {}, {}
        self.slot_of = []
        n_pair = [0, 0]
        for item in plan:
            self.before[item] = len(self.slot_of)
            if item[0] == "slot":
                self.slot_no[item[1:]] = len(self.slot_of)
                self.slot_of.append(item[1:])
                if item[2] == 0:
                    c = chunks[item[1]]
                    self.pair[c.name] = 0 if c.wide else len(self.pair) % 2
                    for pr in ((0, 1) if c.wide else (self.pair[c.name],)):
                        self.pair_turn[c.name, pr] = n_pair[pr]
                        n_pair[pr] += 1
            else:
                self.turn[item[1]] = len(self.turn)
        self.ffn0 = len(self.slot_of)
        self.slots = self.ffn0 + 6 * FSTEPS
        self.turns = len(self.turn)
        self.pair_total = [n + 1 for n in n_pair]
        assert self.slots % RING == 0 and self.turns % 4 == 0, (self.slots, self.turns)

    def chunk_end(self, name):
        return self.slot_no[name, len(self.chunks[name].slots) - 1] + 1

    def words(self, s):
        if s >= self.ffn0:
            return SLOT
        name, i = self.slot_of[s]
        return self.chunks[name].slots[i][1] * self.chunks[name].ncols

    def is_gate_up(self, s):
        r = s - self.ffn0
        return r >= 0 and (r < 4 or (r < 64 and (r - 4) % 6 < 4))

    def loads(self, s):
        return sum(2 if self.is_gate_up(x) else 1 for x in range(s % RING, s + 1, RING))


CH_A, PLAN_A = plan_a()
CH_B, PLAN_B = plan_b()
ORD = (Order(CH_A, PLAN_A), Order(CH_B, PLAN_B))


READ_A = {"hq": ("act", "hq.t1"), "hf": ("act", "hf.t1"), "hi": ("act", "hi.t1"), "hg": ("act", "hg.t1")}
READ_A.update({f"{n}{i}": ("act", f"{n}{i}.t1") for n in ("mla", "uq", "ukv") for i in range(2)})
READ_A.update({f"gate{i}": ("act", f"gate{i}.t1") for i in range(4)})
READ_A.update({f"{n}{i}": ("dve", f"{n}{i}.t1") for n in ("pa", "pb", "wo") for i in range(2)})
READ_B = {f"qkv{i}": ("act", f"qkv{i}.t1") for i in range(3)}
READ_B.update({f"xd{i}": ("act", f"xd{i}.t1") for i in range(4)})
READ_B.update({f"z{i}": ("act", f"z{i}.t1") for i in range(2)})
READ_B.update({f"wo{i}": ("dve", f"wo{i}.t1") for i in range(2)})
ACT_READS = ("hqT", "hfT", "qkT", "PT", "GX", "xT", "cr")


def reader(block, name):
    if block == 0 and name.startswith("oH"):
        return "dve", name
    return ("act" if name.startswith(ACT_READS) else "dve"), name


OPERANDS = (
    {"cT0": ("st", 0, 2, 1.0), "cT1": ("st", 2, 2, 1.0), "cT2": ("st", 4, 1, 1.0),
     "attT0": ("st", 0, 2, 1.0), "attT1": ("st", 2, 2, 1.0),
     "hgT0": ("h", 4, 2, 0.5), "hgT1": ("h", 6, 2, 0.5),
     **{f"yT{i}": ("h", 2 * i, 2, 0.5) for i in range(4)}},
    {"attT0": ("st", 0, 2, 1.0), "attT1": ("st", 2, 2, 1.0),
     **{f"ssT{i}": ("h", 2 * i, 2, 1.0) for i in range(4)}},
)
NEEDS = (
    {**{("mla0", i): f"nT{i}" for i in range(4)}, ("uq0", 0): "cT1", ("ukv0", 0): "cT2", ("pa0", 0): "attT1",
     ("pb0", 0): "hgT1", **{("wo0", i): f"yT{i}" for i in range(4)}},
    {("wo0", 0): "attT1", ("wo0", 2): "ssT1",
     ("wo0", 4): "ssT3"},
)
POOL_LO = ({0, 1, 2, *range(ORD[0].slot_no["gate1", 1], ORD[0].slot_no["gate3", 3] + 1, 2)},
           {0, 1, 2, *range(ORD[1].slot_no["xd0", 0], ORD[1].slot_no["wo1", 1] + 1, 2)})
LOOK = 3
LOOP_AT, LOOP_SLOTS, LOOP_TIMES = 10, 12, 4


def build(nc, A, out, table):
    ctx = ExitStack()
    with ctx:
        def sb(name, shape, dt=F32):
            return ctx.enter_context(nc.sbuf_tensor(name, shape, dt))

        def sem(name):
            return ctx.enter_context(nc.semaphore(name))

        x = sb("x", [P, NT, D])
        h_hi = sb("h_hi", [P, KD, T], F32R)
        h_lo = sb("h_lo", [P, KD, T], F32R)
        st_hi = sb("st_hi", [P, 5, T], F32R)
        st_lo = sb("st_lo", [P, 5, T], F32R)
        w_raw = sb("w_raw", [P, RING, SLOT])
        w_hi = sb("w_hi", [P, RING, SLOT], F32R)
        w_lo = sb("w_lo", [P, RING, SLOT], F32R)
        gains = sb("gains", [P, D])
        gcol = sb("gcol", [P, 2, KD])
        gqk = sb("gqk", [P, 2])
        const = sb("const", [P, C_END])
        masks = sb("masks", [P, 8, P], U8)
        lbs = sb("lbs", [P, 2, HG])
        lbw = sb("lbw", [P, 16])
        lbc = sb("lbc", [P, 2, HG])
        small = sb("small", [P, 208])
        halves = sb("halves", [P, 2])
        epsilons = sb("epsilons", [P, 32])
        ssm = sb("ssm", [P, 352])
        rows = sb("rows", [P, P])
        conv = sb("conv", [P, 60])
        arena = sb("arena", [P, 26112])
        acc = [ctx.enter_context(nc.psum_tensor(f"acc{i}", [P, 512], F32)) for i in range(4)]
        misc = [ctx.enter_context(nc.psum_tensor(f"misc{i}", [P, 512], F32)) for i in range(4)]
        ident = const[:, C_ID:C_ID + P]
        tri = const[:, C_TRI:C_TRI + P]
        stat = {"h": (h_hi, h_lo), "st": (st_hi, st_lo)}

        def carve(at, *shape):
            v = arena[:, at:at + int(np.prod(shape))]
            names = "abcd"[:len(shape)]
            if len(shape) == 1:
                return v
            return v.rearrange(f"p ({' '.join(names)}) -> p {' '.join(names)}",
                               **{c: s for c, s in zip(names[1:], shape[1:])})

        hrow = carve(0, NT, D)
        f_silu = carve(4096, NT, FW)
        f_act = carve(4608, NT, FW)
        gate = carve(0, NT, 2048)
        zm = carve(4096, NT, 672)
        X = carve(4096, 2, 1024)
        zq = carve(6144, NT, 512)
        zf = carve(7168, NT, 512)
        vh = carve(8192, NT, 512)
        sg = carve(9216, NT, 512)
        QK = carve(10240, NT, 16, DQK)
        hQ, hK, hP, hR = (carve(18432 + 1024 * i, 1024) for i in range(4))
        AT = carve(22528, HG, 3, P)
        sq = carve(14336, 2, 16, DQK)
        hdump = carve(14336, NT, HG, DK)
        zqkv = carve(4096, NT, 768)
        xd = carve(5632, NT, XD)
        xs = carve(5632, NT, SI)
        zs = carve(8736, NT, SI)
        xc = carve(13344, 12, T + TAPS - 1)
        xdt = carve(13344, NT, SI)
        cv = carve(16452, 12, T)
        cbm = carve(19524, 2, 384)
        Ex = (carve(20292, 2, 384), carve(21060, 2, 384), carve(22852, 2, 384))
        ys = carve(2048, NT, SI)
        qkT = (carve(14336, 16, T), carve(10784, HB + HKV, T))
        va = (carve(13312, NT, HA, DV), zqkv[:, :, 640:768].rearrange("p t (h d) -> p t h d", h=HKV))
        Sx = (carve(24064, 2, 512), carve(22852, 2, 512))
        PTx = (carve(25088, 2, 512), carve(23876, 2, 512))
        att = (carve(6144, NT, 512), carve(21828, NT, 512))
        oh = carve(7168, NT, 512)
        rope = (carve(24064, 4, 16, 16), carve(24900, 4, NT * 10, 8))
        prm = ssm[:, 0:48]
        dt_u, dt_m, dt_v, dt_a = (ssm[:, 48 + 32 * i:80 + 32 * i] for i in range(4))
        ea = ssm[:, 176:192]
        cs = ssm[:, 192:240]
        ncx = ssm[:, 240:256]
        cosb, sinb, angs = ssm[:, 256:272], ssm[:, 272:288], ssm[:, 288:304]
        turns_, wrap = ssm[:, 304:320], ssm[:, 320:336]
        posf = ssm[:, 336:338]
        posi = sb("posi", [P, NT], I32)

        PE, AC, DV_, PO = (Progress(nc, ctx, n, table) for n in
                           ("tensor_steps", "scalar_steps", "vector_steps", "gpsimd_steps"))
        by = {"act": AC, "dve": DV_}
        x_in, c_in, lb_in, pos_in = sem("x_loaded"), sem("const_loaded"), sem("lb_loaded"), sem("positions_loaded")
        par_in = sem("params_loaded")
        landed = [sem(f"weights_landed{r}") for r in range(RING)]
        fin_in, out_done = sem("final_gain_loaded"), sem("out_stored")
        chain = sem("prologue_chain")
        lb_T, shifted, lb_exp, trig = sem("lb_turned"), sem("exponents_ready"), sem("lb_exponentials"), sem("trig_ready")
        rows_0, angles_in = sem("rows_cleared"), sem("angles_ready")
        fin_ms, fin_r, fin_rows = sem("final_squares"), sem("final_inverse"), sem("final_rows")
        PARS = (9 * 16, 8 * 16)

        def par_at(layer):
            block, l = layer
            return par_in, l * PARS[block] + (DEPTH * PARS[0] if block else 0) + PARS[block]

        def landed_at(layer, s, j=None):
            block, l = layer
            per = [16 * o.loads(o.slots - RING + s % RING) for o in ORD]
            v = l * per[block] + (DEPTH * per[0] if block else 0) + 16 * ORD[block].loads(s)
            return landed[s % RING], v if j is None else v + j * (16 * 5)

        def slot_at(eng, layer, what, s, j=None):
            o = ORD[layer[0]]
            if s < 0:
                return eng.before(layer, f"{what}-{-s}")
            r = s - (o.ffn0 + LOOP_AT) - (0 if what == "used" else LOOK)
            if j is None and 0 <= r < LOOP_SLOTS * LOOP_TIMES:
                semaphore, v = eng.at(layer, f"{what}{s - r + r % LOOP_SLOTS}")
                return semaphore, v + (r // LOOP_SLOTS) * eng.body(layer[0])
            return eng.at(layer, f"{what}{s}", j)

        def slot_name(layer, what, s):
            o = ORD[layer[0]]
            return f"{what}{s}" if s < o.slots - RING else f"{what}-{o.slots - s}"

        def name_at(eng, layer, what, s, j=None):
            o = ORD[layer[0]]
            if s >= o.slots - RING:
                return eng.at(layer, f"{what}-{o.slots - s}", j)
            return slot_at(eng, layer, what, s, j)

        def lo_at(layer, s, j=None):
            return name_at(PO if s in POOL_LO[layer[0]] else DV_, layer, "lo", s, j)

        def bc(ap, shape):
            return ap.to_broadcast(shape)

        block_ = ctx.enter_context(nc.Block())

        @block_.sync
        def _(sp):
            sp.dma_start(x[:, :, :], A["x"].rearrange("(t p) d -> p t d", p=P)).then_inc(x_in, 16)
            sp.dma_start(const[:, :], A["const"]).then_inc(c_in, 16)
            sp.dma_start(carve(0, 8, P), A["masks"]).then_inc(c_in, 16)
            sp.wait_ge(rows_0, 1)
            sp.dma_start(rows[0:8, :], A["hg_lb_logits"].rearrange("l (h k) -> (l h) k", k=DK)).then_inc(lb_in, 16)
            sp.dma_start(posi[:, :], A["positions_2"].rearrange("(t p) -> p t", p=P),
                         allow_slow_non_contiguous=True).then_inc(pos_in, 16)

            def row(name, l, n):
                return A[name][bass.ds(l, 1), :].to_broadcast([P, n])

            def params(layer):
                block, l = layer
                sp.wait_ge(*DV_.before(layer, "f0"))
                for i, name in enumerate(("norm_mix", "norm_ffn")):
                    src = A[name + ("_2" if block else "")][bass.ds(l, 1), :]
                    sp.dma_start(gcol[:, i, :], src.rearrange("a (k p) -> p (a k)", p=P),
                                 allow_slow_non_contiguous=True).then_inc(par_in, 16)
                if block == 0:
                    for i, name in enumerate(("mla_q_norm", "mla_k_norm")):
                        src = A[name][bass.ds(l, 1), 0:NOPE]
                        sp.dma_start(gqk[0:NOPE, i:i + 1], src.rearrange("a d -> d a"),
                                     allow_slow_non_contiguous=True).then_inc(par_in, 16)
                    for name, at, n in (("mla_norm_cq", G_CQ, QL), ("mla_norm_ckv", G_CKV, KVL), ("mla_q_norm", G_QK, DQK), ("mla_k_norm", G_QK + DQK, DQK), ("hg_out_norm", G_HG, DK)):
                        sp.dma_start(gains[:, at:at + n], row(name, l, n)).then_inc(par_in, 16)
                else:
                    sp.dma_start(gains[:, G_SSM:G_SSM + SI], row("ssm_norm_2", l, SI)).then_inc(par_in, 16)
                    for i, name in enumerate(("dt_bias_2", "a_log_2", "d_skip_2")):
                        sp.dma_start(prm[:, 16 * i:16 * i + 16], row(name, l, SH)).then_inc(par_in, 16)
                    sp.dma_start(rows[0:48, :], A["conv_w_2"][bass.ds(l * 48, 48), :]).then_inc(par_in, 16)
                    sp.dma_start(rows[48:60, :], A["conv_b_2"][bass.ds(l * 12, 12), :]).then_inc(par_in, 16)

            def ffn_load(layer, s, kind, i, q, j=None):
                block, l = layer
                suffix = "_2" if block else ""
                sp.wait_ge(*lo_at(layer, s - RING, j))
                place = w_raw[:, s % RING, :]
                if kind == "gu":
                    dst = place.rearrange("p (k u n) -> p k u n", k=2, u=2)
                    for u, name in enumerate(("w_gate", "w_up")):
                        src = A[name + suffix][bass.ds(l * D + 2 * q * P, 2 * P), bass.ds(i * FW, FW)]
                        sp.dma_start(dst[:, :, u, :], src.rearrange("(k p) n -> p k n", p=P))\
                            .then_inc(landed[s % RING], 16)
                else:
                    src = A["w_down" + suffix][bass.ds(l * FF + i * FW + q * P, P), :]
                    sp.dma_start(place, src).then_inc(landed[s % RING], 16)

            def layer_loads(layer):
                block, l = layer
                o = ORD[block]
                params(layer)
                for s, (name, i) in enumerate(o.slot_of):
                    c = o.chunks[name]
                    k0, nk = c.slots[i]
                    sp.wait_ge(*lo_at(layer, s - RING))
                    src = A[c.weight][bass.ds(l * c.rows + k0 * P, nk * P), c.col:c.col + c.ncols]
                    dst = w_raw[:, s % RING, 0:nk * c.ncols].rearrange("p (k n) -> p k n", k=nk)
                    sp.dma_start(dst, src.rearrange("(k p) n -> p k n", p=P)).then_inc(landed[s % RING], 16)
                s = o.ffn0

                def gate_up(s, i, j=None):
                    for q in range(4):
                        ffn_load(layer, s + q, "gu", i, q, j)

                def down(s, i, j=None):
                    for q in range(2):
                        ffn_load(layer, s + q, "dn", i, q, j)

                gate_up(s, 0)
                gate_up(s + 4, 1)
                down(s + 8, 0)
                s += LOOP_AT
                with sp.Fori(0, LOOP_TIMES) as j:
                    gate_up(s, 2 * j + 2, j)
                    down(s + 4, 2 * j + 1, j)
                    gate_up(s + 6, 2 * j + 3, j)
                    down(s + 10, 2 * j + 2, j)
                s += LOOP_SLOTS * LOOP_TIMES
                gate_up(s, 10)
                down(s + 4, 9)
                down(s + 6, 10)

            for block in range(2):
                with sp.Fori(0, DEPTH) as l:
                    layer_loads((block, l))
            sp.wait_ge(*DV_.final("f0"))
            sp.dma_start(gains[:, 0:D], A["final_norm_2"].rearrange("(a n) -> a n", a=1).to_broadcast([P, D]))\
                .then_inc(fin_in, 16)
            for t in range(NT):
                sp.wait_ge(fin_rows, t + 1)
                sp.dma_start(out[t * P:(t + 1) * P, :], hrow[:, t, :]).then_inc(out_done, 16)
            sp.wait_ge(out_done, 16 * NT)

        @block_.tensor
        def _(pe):
            def product(dst, st, k, t, rhs_hi, rhs_lo, first, last):
                hi, lo = st
                cols = slice(t * P, (t + 1) * P)
                pe.matmul(dst, hi[:, k, cols], rhs_hi, start=first, stop=False)
                pe.matmul(dst, hi[:, k, cols], rhs_lo, start=False, stop=False)
                return pe.matmul(dst, lo[:, k, cols], rhs_hi, start=False, stop=last)

            pe.wait_ge(c_in, 32)
            pe.wait_ge(lb_in, 16)
            pe.wait_ge(rows_0, 1)
            pe.transpose(misc[3][:, 0:P], rows[:, :], ident).then_inc(lb_T, 1)

            def run_slot(layer, name, i):
                block = layer[0]
                o = ORD[block]
                c, s = o.chunks[name], o.slot_no[name, i]
                k0, nk = c.slots[i]
                if i == 0:
                    for pr in ((0, 1) if c.wide else (o.pair[name],)):
                        n = o.pair_turn[name, pr]
                        if n == 0:
                            pe.wait_ge(*DV_.before(layer, f"x_ffn{2 * pr + 1}"))
                        else:
                            prior = [m for (m, q), v in o.pair_turn.items() if q == pr and v == n - 1][0]
                            who, step = (READ_A, READ_B)[block][prior]
                            pe.wait_ge(*by[who].at(layer, step))
                if (name, i) in NEEDS[block]:
                    pe.wait_ge(*DV_.at(layer, NEEDS[block][name, i]))
                pe.wait_ge(*lo_at(layer, s))
                for kk in range(nk):
                    k = k0 + kk
                    if name == "qkv0" and k % 2 == 0:
                        pe.wait_ge(*DV_.at(layer, f"nT{k // 2}"))
                    if c.stat == "mix":
                        st, tile = (stat["st"], k) if k < 4 else (stat["h"], k - 4)
                    else:
                        st, tile = stat[c.stat], c.tile0 + k
                    for t in range(NT):
                        for half in range(2 if c.wide else 1):
                            n = 512 if c.wide else c.ncols
                            at = kk * c.ncols + half * 512
                            bank = 2 * (half if c.wide else o.pair[name]) + t
                            mm = product(acc[bank][:, 0:n], st, tile, t, w_hi[:, s % RING, at:at + n],
                                         w_lo[:, s % RING, at:at + n], k == 0, k == c.ktiles - 1)
                mm.then_inc(*PE.mark(slot_name(layer, "used", s)))

            def bank_of(layer, name):
                block = layer[0]
                o = ORD[block]
                u = o.turn[name]
                if u >= 4:
                    prior = [m for m, v in o.turn.items() if v == u - 4][0]
                    who, step = reader(block, prior)
                    pe.wait_ge(*by[who].at(layer, step))
                else:
                    pe.wait_ge(*DV_.before(layer, "fT10"))
                return misc[u % 4]

            def transposes(layer, name, blocks, n=P):
                b = bank_of(layer, name)
                for i, src in enumerate(blocks):
                    tr = pe.transpose(b[0:n, i * P:(i + 1) * P], src, ident)
                tr.then_inc(*PE.mark(name))

            def scores(layer, g):
                block = layer[0]
                d, group = (DQK, 1) if block == 0 else (DB, HB // HKV)
                b = bank_of(layer, f"S{g}")
                qk = qkT[block]
                heads, nq, keys = (range(4 * g, 4 * g + 4), 0, P) if g < 2 else (range(2 * g - 4, 2 * g - 2), 1, T)
                for i, hd in enumerate(heads):
                    mm = pe.matmul(b[:, i * keys:(i + 1) * keys], qk[0:d, hd, nq * P:(nq + 1) * P],
                                   qk[0:d, HB + hd // group, 0:keys], start=True, stop=True)
                mm.then_inc(*PE.mark(f"S{g}"))

            def weigh(layer, g):
                block = layer[0]
                group = 1 if block == 0 else HB // HKV
                pe.wait_ge(*AC.at(layer, f"PT{g}"))
                b = bank_of(layer, f"O{g}")
                pt = PTx[block][:, g % 2, :]
                heads, nk = (range(4 * g, 4 * g + 4), 1) if g < 2 else (range(2 * g - 4, 2 * g - 2), 2)
                for i, hd in enumerate(heads):
                    for k in range(nk):
                        at = (i * nk + k) * P
                        mm = pe.matmul(b[:, i * 64:(i + 1) * 64], pt[:, at:at + P],
                                       va[block][:, k, hd // group, :], start=(k == 0), stop=(k == nk - 1))
                mm.then_inc(*PE.mark(f"O{g}"))

            def shared(layer, name):
                block = layer[0]
                kind, num = name.rstrip("0123456789"), name[len(name.rstrip("0123456789")):]
                i = int(num) if num else 0
                if kind in ("nT", "mT"):
                    if kind == "nT":
                        pe.wait_ge(x_in, 16)
                    b = misc[ORD[block].turn[name] % 4]
                    for t in range(NT):
                        pe.wait_ge(*(DV_.before(layer, f"x_ffn{2 * (i // 2) + t}") if kind == "nT" else
                                     DV_.at(layer, f"wo{i // 2}.t{t}")))
                        for kk in range(2):
                            at, k = kk * T + t * P, 2 * i + kk
                            tr = pe.transpose(b[:, at:at + P], x[:, t, k * P:(k + 1) * P], ident)
                    tr.then_inc(*PE.mark(name))
                elif kind == "S":
                    if i == 0:
                        pe.wait_ge(*AC.at(layer, "qkT7" if block == 0 else "qkT4"))
                    scores(layer, i)
                elif kind == "PT":
                    pe.wait_ge(*AC.at(layer, f"p{i}"))
                    transposes(layer, name, [Sx[block][:, i % 2, k * P:(k + 1) * P] for k in range(4)])
                elif kind == "O":
                    weigh(layer, i)
                elif kind == "attT":
                    if i == 0:
                        pe.wait_ge(*DV_.at(layer, "O5"))
                    transposes(layer, name, [att[block][:, t, k * P:(k + 1) * P] for k in (2 * i, 2 * i + 1)
                                             for t in range(NT)])
                elif block == 0:
                    shared_a(layer, name, kind, i)
                else:
                    shared_b(layer, name, kind, i)

            def shared_a(layer, name, kind, i):
                if kind == "cT":
                    if i == 0:
                        pe.wait_ge(*DV_.at(layer, "cnorm"))
                    tiles = ((0, 1), (2, 3), (4,))[i]
                    transposes(layer, name, [zm[:, t, k * P:(k + 1) * P] for k in tiles for t in range(NT)])
                elif kind in ("hqT", "hfT"):
                    src = zq if kind == "hqT" else zf
                    if i == 0:
                        pe.wait_ge(*AC.at(layer, f"{kind[:2]}.t1"))
                    transposes(layer, name, [src[:, t, k * P:(k + 1) * P] for k in (2 * i, 2 * i + 1)
                                             for t in range(NT)])
                elif kind == "qkT":
                    if i == 0:
                        pe.wait_ge(*DV_.at(layer, "qk1"))
                    transposes(layer, name, [QK[:, t, hd, :] for hd in (2 * i, 2 * i + 1) for t in range(NT)], DQK)
                elif kind.startswith("G") and name != "GX":
                    lev, pr = int(name[1]), int(name[3])
                    if pr == 0:
                        pe.wait_ge(*DV_.at(layer, f"X{lev}"))
                    if lev == 0 and pr == 0:
                        pe.wait_ge(*AC.at(layer, "hqT1"))
                    b = bank_of(layer, name)
                    for n, (hd, t) in enumerate((hd, t) for hd in (2 * pr, 2 * pr + 1) for t in range(NT)):
                        cols = slice(hd * T + t * P, hd * T + (t + 1) * P)
                        keys = hK[:, cols] if lev == 0 else X[:, lev % 2, cols]
                        queries = hQ[:, cols] if lev == 0 else X[:, lev % 2, cols]
                        mm = pe.matmul(b[:, n * P:(n + 1) * P], keys, queries, start=True, stop=True)
                    mm.then_inc(*PE.mark(name))
                elif name == "GX":
                    pe.wait_ge(*DV_.at(layer, "X8"))
                    b = bank_of(layer, name)
                    for hd in range(HG):
                        mm = pe.matmul(b[:, hd * P:(hd + 1) * P], X[:, 0, hd * T:hd * T + P],
                                       X[:, 0, hd * T + P:hd * T + T], start=True, stop=True)
                    mm.then_inc(*PE.mark(name))
                elif kind == "oH":
                    if i == 0:
                        pe.wait_ge(*AC.at(layer, "GX"))
                        pe.wait_ge(*DV_.at(layer, "G7_1"))
                    b = bank_of(layer, name)
                    for hd in range(HG):
                        cols = slice(hd * P, (hd + 1) * P)
                        if i == 0:
                            mm = pe.matmul(b[:, cols], AT[:, hd, 0, :], vh[:, 0, cols], start=True, stop=True)
                        else:
                            pe.matmul(b[:, cols], AT[:, hd, 2, :], vh[:, 0, cols], start=True, stop=False)
                            mm = pe.matmul(b[:, cols], AT[:, hd, 1, :], vh[:, 1, cols], start=False, stop=True)
                    mm.then_inc(*PE.mark(name))
                elif kind == "hgT":
                    if i == 0:
                        pe.wait_ge(*DV_.at(layer, "oh1"))
                    transposes(layer, name, [oh[:, t, k * P:(k + 1) * P] for k in (2 * i, 2 * i + 1)
                                             for t in range(NT)])
                elif kind == "yT":
                    pe.wait_ge(*DV_.at(layer, f"y{i // 2}"))
                    transposes(layer, name, [gate[:, t, k * P:(k + 1) * P] for k in (2 * i, 2 * i + 1)
                                             for t in range(NT)])
                else:
                    raise ValueError(name)

            def shared_b(layer, name, kind, i):
                if kind == "cvT":
                    pe.wait_ge(*par_at(layer))
                    b = bank_of(layer, name)
                    pe.transpose(b[:, 0:P], rows[:, :], ident).then_inc(*PE.mark(name))
                elif kind == "qkT":
                    if i == 0:
                        pe.wait_ge(*DV_.at(layer, "qk"))
                    transposes(layer, name, [zqkv[:, t, hd * DB:hd * DB + DQK] for hd in (2 * i, 2 * i + 1)
                                             for t in range(NT)], DQK)
                elif kind == "xT":
                    if i != 2:
                        pe.wait_ge(*AC.at(layer, f"xd{(0, 1, 1, 2, 3, 3)[i]}.t1"))
                    transposes(layer, name, [xd[:, t, k * P:(k + 1) * P] for k in (2 * i, 2 * i + 1)
                                             for t in range(NT)])
                elif kind == "xsT":
                    pe.wait_ge(*AC.at(layer, f"conv_silu{i % 2}"))
                    t, half = i // 2, i % 2
                    transposes(layer, name, [cv[:, 4 * half + k, t * P:(t + 1) * P] for k in range(4)])
                elif kind == "cb":
                    pe.wait_ge(*AC.at(layer, "conv_silu2"))
                    b = bank_of(layer, name)
                    pe.matmul(b[:, 0:T], cv[:, 8 + i, 0:P], cv[:, 10 + i, :], start=True, stop=True)
                    pe.matmul(b[:, T:T + P], cv[:, 8 + i, P:T], cv[:, 10 + i, P:T], start=True, stop=True)\
                        .then_inc(*PE.mark(name))
                elif name == "cs":
                    pe.wait_ge(*DV_.at(layer, "dt_a"))
                    b = bank_of(layer, name)
                    pe.matmul(b[:, 0:16], tri, dt_a[:, 0:16], start=True, stop=True)
                    pe.matmul(b[:, 16:32], tri, dt_a[:, 16:32], start=True, stop=True)
                    pe.matmul(b[:, 32:48], bc(tri[:, P - 1:P], [P, P]), dt_a[:, 0:16], start=True, stop=True)\
                        .then_inc(*PE.mark(name))
                elif kind == "cr":
                    b = bank_of(layer, name)
                    for n, (hd, t) in enumerate((hd, t) for hd in (2 * i, 2 * i + 1) for t in range(NT)):
                        a = dt_a[:, 16 * t + hd:16 * t + hd + 1]
                        mm = pe.matmul(b[:, n * P:(n + 1) * P], bc(a, [P, P]), tri, start=True, stop=True)
                    mm.then_inc(*PE.mark(name))
                elif kind == "y":
                    pe.wait_ge(*DV_.at(layer, f"M{i}"))
                    b = bank_of(layer, name)
                    for u in range(2):
                        hd = 2 * i + u
                        E = Ex[i % 3][:, u, :]
                        cols = slice(hd * SP, (hd + 1) * SP)
                        pe.matmul(b[:, u * SP:(u + 1) * SP], E[:, 0:P], xdt[:, 0, cols], start=True, stop=True)
                        at = P + u * SP
                        pe.matmul(b[:, at:at + SP], E[:, P:2 * P], xdt[:, 0, cols], start=True, stop=False)
                        mm = pe.matmul(b[:, at:at + SP], E[:, 2 * P:3 * P], xdt[:, 1, cols], start=False, stop=True)
                    mm.then_inc(*PE.mark(name))
                elif kind == "ssT":
                    pe.wait_ge(*DV_.at(layer, f"ys{i // 2}"))
                    transposes(layer, name, [ys[:, t, k * P:(k + 1) * P] for k in (2 * i, 2 * i + 1)
                                             for t in range(NT)])
                else:
                    raise ValueError(name)

            def feed_forward(layer):
                o = ORD[layer[0]]

                def gate_up(s, i, j=None, behind=None, between=None):
                    pe.wait_ge(*DV_.at(layer, behind, j))
                    first = i == 0
                    banks = acc[0:2] if first else misc[2:4]
                    for q in range(4):
                        if between and q == 2:
                            turn(between)
                        if first:
                            pe.wait_ge(*DV_.at(layer, f"mT{q}"))
                        pe.wait_ge(*lo_at(layer, s + q, j))
                        for kk in range(2):
                            for t in range(NT):
                                at = kk * 512
                                mm = product(banks[t][:, :], stat["h"], 2 * q + kk, t,
                                             w_hi[:, (s + q) % RING, at:at + 512],
                                             w_lo[:, (s + q) % RING, at:at + 512],
                                             q == 0 and kk == 0, q == 3 and kk == 1)
                        mm.then_inc(*PE.mark(slot_name(layer, "used", s + q)))

                def turn(step, j=None):
                    pe.wait_ge(*DV_.at(layer, f"f{step}", j))
                    for kk in range(2):
                        for t in range(NT):
                            at = kk * T + t * P
                            tr = pe.transpose(misc[0][:, at:at + P], f_act[:, t, kk * P:(kk + 1) * P], ident)
                    tr.then_inc(*PE.mark(f"fT{step}"))

                def down(s, step, first=False, last=False, j=None, between=None):
                    pe.wait_ge(*DV_.at(layer, f"fT{step}", j))
                    for q in range(2):
                        if between and q == 1:
                            turn(between)
                        pe.wait_ge(*lo_at(layer, s + q, j))
                        for half in range(2):
                            for t in range(NT):
                                at = half * 512
                                mm = product(acc[2 * half + t][:, :], stat["st"], q + (2 if last else 0), t,
                                             w_hi[:, (s + q) % RING, at:at + 512],
                                             w_lo[:, (s + q) % RING, at:at + 512],
                                             first and q == 0, last and q == 1)
                            if last and q == 1 and half == 0:
                                mm.then_inc(*PE.mark("x_half"))
                        mm.then_inc(*PE.mark(slot_name(layer, "used", s + q)))

                s = o.ffn0
                gate_up(s, 0, behind="wo0.t1")
                gate_up(s + 4, 1, behind="mT3", between="0")
                pe.wait_ge(*DV_.at(layer, "wo1.t1"))
                pe.wait_ge(*DV_.at(layer, "f0"))
                down(s + 8, "0", first=True)
                turn("1")
                s += LOOP_AT
                PE.loop(None)
                with pe.Fori(0, LOOP_TIMES) as j:
                    gate_up(s, 2, j, behind="f1")
                    down(s + 4, "1", j=j)
                    turn("2", j)
                    gate_up(s + 6, 3, j, behind="f2")
                    down(s + 10, "2", j=j)
                    turn("3", j)
                PE.loop(LOOP_TIMES)
                s += LOOP_SLOTS * LOOP_TIMES
                gate_up(s, 10, behind="f3@last")
                down(s + 4, "3@last", between="10")
                down(s + 6, "10", last=True)

            pe.wait_ge(shifted, 1)
            for block in range(2):
                with pe.Fori(0, DEPTH) as l:
                    layer = (block, l)
                    for item in ORD[block].plan:
                        if item[0] == "slot":
                            run_slot(layer, item[1], item[2])
                        else:
                            shared(layer, item[1])
                    feed_forward(layer)
                PE.end()

        @block_.scalar
        def _(act):
            split = [0]

            def split_until(layer, n, j=None):
                o = ORD[layer[0]]
                for s in range(split[0], min(n, o.slots)):
                    act.wait_ge(*landed_at(layer, s, j))
                    act.wait_ge(*name_at(PE, layer, "used", s - RING, j))
                    w = o.words(s)
                    act.activation(w_hi[:, s % RING, 0:w], w_raw[:, s % RING, 0:w], ACT.Copy)\
                        .then_inc(*AC.mark(slot_name(layer, "hi", s)))
                split[0] = max(split[0], min(n, o.slots))

            def wait_bank(layer, name):
                split_until(layer, ORD[layer[0]].before["misc", name] + LOOK)
                act.wait_ge(*PE.at(layer, name))
                return misc[ORD[layer[0]].turn[name] % 4]

            def wait_product(layer, name):
                o = ORD[layer[0]]
                end = o.chunk_end(name)
                split_until(layer, end + LOOK)
                act.wait_ge(*name_at(PE, layer, "used", end - 1))
                pair = o.pair[name]
                return acc[2 * pair], acc[2 * pair + 1]

            def operand(layer, name):
                where, tile, n, scale = OPERANDS[layer[0]][name]
                b = wait_bank(layer, name)
                dst = stat[where][0][:, tile:tile + n, :].rearrange("p k t -> p (k t)")
                act.activation(dst, b[:, 0:n * T], ACT.Copy, scale=scale).then_inc(*AC.mark(f"hi.{name}"))

            def norm_operand(layer, name):
                kind, i = name[:2], int(name[2])
                if name == "mT0":
                    split_until(layer, ORD[layer[0]].chunk_end("wo1") + LOOK)
                b = wait_bank(layer, name)
                if kind == "mT":
                    act.wait_ge(*name_at(PE, layer, "used", ORD[layer[0]].chunk_end("wo1") - 1))
                for k in range(2):
                    act.activation(h_hi[:, 2 * i + k, :], b[:, k * T:(k + 1) * T], ACT.Copy,
                                   scale=gcol[:, kind == "mT", 2 * i + k:2 * i + k + 1])\
                        .then_inc(*AC.mark(f"hi.{name}"))

            def inv(layer, kind, t):
                c = {"x": RS + M_X, "x/2": RS + M_H, "y": RS + M_Y}[kind] + t
                return small[:, c:c + 1]

            def squares(layer, kind):
                col = M_X if kind == "nT" else M_Y
                for t in range(NT):
                    act.activation(hrow[:, t, :], x[:, t, :], ACT.Square, scale=D ** -0.5, accum_out=small[:, col + t:col + t + 1])\
                        .then_inc(*AC.mark(f"ms.{kind}"))

            def softmax(layer, g, scale):
                block = layer[0]
                split_until(layer, ORD[block].before["misc", f"S{g}"] + LOOK)
                act.wait_ge(*DV_.at(layer, f"S{g}"))
                n, keys = (4, P) if g < 2 else (2, T)
                for i in range(n):
                    v = Sx[block][:, g % 2, i * keys:(i + 1) * keys]
                    c = (g % 4) * 4 + i
                    e = act.activation(v, v, ACT.Exp, scale=scale, bias=small[:, 144 + c:145 + c],
                                       accum_out=small[:, 160 + c:161 + c])
                    e.then_inc(*AC.mark(f"p{g}"))

            def turned_weights(layer, g):
                b = wait_bank(layer, f"PT{g}")
                if g >= 2:
                    act.wait_ge(*PE.at(layer, f"O{g - 2}"))
                act.activation(PTx[layer[0]][:, g % 2, :], b[:, :], ACT.Copy).then_inc(*AC.mark(f"PT{g}"))

            def feed_forward(layer):
                o = ORD[layer[0]]

                def silu(s_end, step, used_s, j=None):
                    split_until(layer, s_end + LOOK, j)
                    act.wait_ge(*name_at(PE, layer, "used", used_s, j))
                    if step == "0":
                        act.wait_ge(*PO.at(layer, "r.mT"))
                    for t in range(NT):
                        b = acc[t] if step == "0" else misc[2 + t]
                        act.activation(f_silu[:, t, :], b[:, 0:FW], ACT.Silu, scale=inv(layer, "y", t))\
                            .then_inc(*AC.mark(f"f{step}.t{t}"))

                def turned(s_end, step, j=None):
                    split_until(layer, s_end + LOOK, j)
                    act.wait_ge(*PE.at(layer, f"fT{step}", j))
                    at = 2 if step == "10" else 0
                    act.activation(st_hi[:, at:at + 2, :].rearrange("p k t -> p (k t)"), misc[0][:, :], ACT.Copy)\
                        .then_inc(*AC.mark(f"fT{step}"))

                s = o.ffn0
                silu(s + 3, "0", s + 3)
                turned(s + 4, "0")
                silu(s + 8, "1", s + 7)
                turned(s + 10, "1")
                s += LOOP_AT
                AC.loop(None)
                with act.Fori(0, LOOP_TIMES) as j:
                    silu(s + 4, "2", s + 3, j)
                    turned(s + 6, "2", j)
                    silu(s + 10, "3", s + 9, j)
                    turned(s + 12, "3", j)
                AC.loop(LOOP_TIMES)
                split[0] += LOOP_SLOTS * (LOOP_TIMES - 1)
                s += LOOP_SLOTS * LOOP_TIMES
                silu(s + 4, "10", s + 3)
                turned(s + 6, "10")
                split_until(layer, o.slots)
                split[0] = 0

            def copy_product(layer, name, dst, func=ACT.Copy, rms=None):
                banks = wait_product(layer, name)
                n = ORD[layer[0]].chunks[name].ncols
                for t in range(NT):
                    scale = 1.0 if rms is None else inv(layer, rms, t)
                    act.activation(dst(t), banks[t][:, 0:n], func, scale=scale).then_inc(*AC.mark(f"{name}.t{t}"))

            def body_a(layer):
                sc = float(DQK) ** -0.5
                act.wait_ge(x_in, 16)
                act.wait_ge(*par_at(layer))
                split_until(layer, RING)
                act.wait_ge(*DV_.before(layer, "x_ffn3"))
                for i in range(4):
                    norm_operand(layer, f"nT{i}")
                squares(layer, "nT")
                split_until(layer, RING + 1)
                act.wait_ge(*PO.at(layer, "r.nT"))
                for i in range(2):
                    copy_product(layer, f"mla{i}", lambda t: zm[:, t, 336 * i:336 * i + 336], rms="x")
                act.wait_ge(*AC.now(layer))
                for t in range(NT):
                    act.activation(sq[:, 0, 0:4, :].rearrange("p a b -> p (a b)"), zm[:, t, 0:QL], ACT.Square, scale=QL ** -0.5,
                                   accum_out=small[:, M_CQ + t:M_CQ + t + 1]).then_inc(*AC.mark())
                    act.activation(sq[:, 1, 0:4, 0:64], zm[:, t, QL:QL + KVL].rearrange("p (a b) -> p a b", a=4),
                                   ACT.Square, scale=KVL ** -0.5, accum_out=small[:, M_CKV + t:M_CKV + t + 1])\
                        .then_inc(*AC.mark("ms.c"))
                    act.wait_ge(*AC.now(layer))
                copy_product(layer, "hq", lambda t: zq[:, t, :], rms="x")
                copy_product(layer, "hf", lambda t: zf[:, t, :], rms="x")
                for i in range(3):
                    operand(layer, f"cT{i}")
                copy_product(layer, "hi", lambda t: vh[:, t, :], rms="x")
                for i in range(2):
                    b = wait_bank(layer, f"hqT{i}")
                    act.activation(hQ[:, 512 * i:512 * i + 512], b[:, :], ACT.Copy).then_inc(*AC.mark(f"hqT{i}"))
                for i in range(2):
                    b = wait_bank(layer, f"hfT{i}")
                    act.activation(hP[:, 512 * i:512 * i + 512], b[:, :], ACT.Sigmoid).then_inc(*AC.mark())
                    act.activation(hK[:, 512 * i:512 * i + 512], b[:, :], ACT.Sigmoid, scale=-1.0)\
                        .then_inc(*AC.mark(f"hfT{i}"))
                banks = wait_product(layer, "hg")
                for t in range(NT):
                    act.activation(zq[:, t, :], banks[t][:, :], ACT.Copy, scale=inv(layer, "x", t))\
                        .then_inc(*AC.mark())
                    act.activation(sg[:, t, :], banks[t][:, :], ACT.Tanh, scale=inv(layer, "x/2", t))\
                        .then_inc(*AC.mark(f"hg.t{t}"))
                for i in range(2):
                    copy_product(layer, f"uq{i}",
                                 lambda t: QK[:, t, 4 * i:4 * i + 4, :].rearrange("p a b -> p (a b)"))
                for i in range(2):
                    banks = wait_product(layer, f"ukv{i}")
                    for t in range(NT):
                        kv = banks[t][:, :].rearrange("p (h e) -> p h e", h=4)
                        act.activation(QK[:, t, 8 + 4 * i:12 + 4 * i, 0:NOPE], kv[:, :, 0:NOPE], ACT.Copy)\
                            .then_inc(*AC.mark())
                        act.activation(va[0][:, t, 4 * i:4 * i + 4, :], kv[:, :, NOPE:NOPE + DV], ACT.Copy)\
                            .then_inc(*AC.mark(f"ukv{i}.t{t}"))
                for t in range(NT):
                    src = zm[:, t, QL + KVL:].rearrange("p (a d) -> p a d", a=1)
                    act.activation(QK[:, t, 8:16, NOPE:DQK], bc(src, [P, 8, RA]), ACT.Copy).then_inc(*AC.mark("kpe"))
                act.wait_ge(*AC.now(layer))
                for t in range(NT):
                    split_until(layer, ORD[0].chunk_end("ukv1") + LOOK - 1 + t)
                    act.activation(sq[:, t, :, :], QK[:, t, :, :], ACT.Square, scale=DQK ** -0.5).then_inc(*AC.mark(f"sq{t}"))
                copy_product(layer, "gate0", lambda t: gate[:, t, 0:512], ACT.Tanh, "x/2")
                for i in range(8):
                    b = wait_bank(layer, f"qkT{i}")
                    act.activation(qkT[0][0:DQK, 2 * i:2 * i + 2, :].rearrange("p h t -> p (h t)"), b[0:DQK, :],
                                   ACT.Copy, scale=gqk[0:DQK, i // 4:i // 4 + 1]).then_inc(*AC.mark(f"qkT{i}"))
                copy_product(layer, "gate1", lambda t: gate[:, t, 512:1024], ACT.Tanh, "x/2")
                for i in range(8):
                    if 1 <= i < 7:
                        turned_weights(layer, i - 1)
                    if i == 0:
                        softmax(layer, 0, sc)
                        softmax(layer, 1, sc)
                    elif i < 5:
                        softmax(layer, i + 1, sc)
                    if i == 4 or i == 7:
                        n = 2 + (i == 7)
                        copy_product(layer, f"gate{n}", lambda t: gate[:, t, 512 * n:512 * n + 512], ACT.Tanh,
                                     "x/2")
                b = wait_bank(layer, "GX")
                act.activation(AT[:, :, 2, :], b[:, :].rearrange("p (h q) -> p h q", h=HG), ACT.Copy)\
                    .then_inc(*AC.mark("GX"))
                operand(layer, "attT0")
                operand(layer, "attT1")
                for t in range(NT):
                    b = wait_bank(layer, f"oH{t}")
                    for hd in range(HG):
                        c = M_HG + 4 * t + hd
                        act.activation(hdump[:, t, hd, :], b[:, hd * P:(hd + 1) * P], ACT.Square, scale=DK ** -0.5,
                                       accum_out=small[:, c:c + 1]).then_inc(*AC.mark(f"ms.h{t}"))
                operand(layer, "hgT0")
                operand(layer, "hgT1")
                for i in range(4):
                    operand(layer, f"yT{i}")
                for i in range(4):
                    norm_operand(layer, f"mT{i}")
                squares(layer, "mT")
                feed_forward(layer)

            def body_b(layer):
                sc = float(DB) ** -0.5
                act.wait_ge(*par_at(layer))
                split_until(layer, RING)
                act.wait_ge(*DV_.before(layer, "x_ffn3"))
                for i in range(4):
                    norm_operand(layer, f"nT{i}")
                squares(layer, "nT")
                split_until(layer, RING + 1)
                act.wait_ge(*PO.at(layer, "r.nT"))
                for i in range(3):
                    copy_product(layer, f"qkv{i}", lambda t: zqkv[:, t, 256 * i:256 * i + 256], rms="x")
                for i in range(5):
                    b = wait_bank(layer, f"qkT{i}")
                    act.activation(qkT[1][0:DB, 2 * i:2 * i + 2, :].rearrange("p h t -> p (h t)"), b[0:DB, :],
                                   ACT.Copy).then_inc(*AC.mark(f"qkT{i}"))

                def mixed(i):
                    copy_product(layer, f"xd{i}", lambda t: xd[:, t, 388 * i:388 * i + 388], rms="x")

                def channels(i):
                    b = wait_bank(layer, f"xT{i}")
                    act.activation(xc[:, 2 * i:2 * i + 2, TAPS - 1:], b[:, :].rearrange("p (k t) -> p k t", k=2),
                                   ACT.Copy).then_inc(*AC.mark(f"xT{i}"))

                def conv_silu(g):
                    act.wait_ge(*DV_.at(layer, f"conv{2 * g + 1}"))
                    act.activation(cv[:, 4 * g:4 * g + 4, :], cv[:, 4 * g:4 * g + 4, :], ACT.Silu)\
                        .then_inc(*AC.mark(f"conv_silu{g}"))

                softmax(layer, 0, sc)
                softmax(layer, 1, sc)
                mixed(0)
                act.wait_ge(*DV_.at(layer, "pad"))
                turned_weights(layer, 0)
                softmax(layer, 2, sc)
                channels(0)
                turned_weights(layer, 1)
                softmax(layer, 3, sc)
                turned_weights(layer, 2)
                softmax(layer, 4, sc)
                mixed(1)
                turned_weights(layer, 3)
                softmax(layer, 5, sc)
                channels(1)
                turned_weights(layer, 4)
                channels(2)
                turned_weights(layer, 5)
                mixed(2)
                operand(layer, "attT0")
                operand(layer, "attT1")
                channels(3)
                mixed(3)
                channels(4)
                channels(5)
                act.wait_ge(*DV_.at(layer, "dt_u"))
                act.activation(dt_v, dt_v, ACT.Exp).then_inc(*AC.mark())
                act.activation(ea, prm[:, 16:32], ACT.Exp).then_inc(*AC.mark())
                act.wait_ge(*AC.now(layer))
                act.activation(dt_v, dt_v, ACT.Ln, bias=1.0).then_inc(*AC.mark("dt_ln"))
                conv_silu(0)
                conv_silu(1)
                for i in range(4):
                    t, half = i // 2, i % 2
                    b = wait_bank(layer, f"xsT{i}")
                    act.activation(xs[:, t, 512 * half:512 * half + 512], b[:, :], ACT.Copy)\
                        .then_inc(*AC.mark(f"xs{i}"))
                conv_silu(2)
                copy_product(layer, "z0", lambda t: zs[:, t, 0:512], ACT.Silu, "x")

                def group_squares(g):
                    act.wait_ge(*DV_.at(layer, f"ysz{g}"))
                    for t in range(NT):
                        c = M_HG + 2 * g + t
                        act.activation(zs[:, t, 512 * g:512 * g + 512], ys[:, t, 512 * g:512 * g + 512], ACT.Square,
                                       scale=(SI // 2) ** -0.5,
                                       accum_out=small[:, c:c + 1]).then_inc(*AC.mark(f"ms.s{g}"))

                for hp in range(SH // 2):
                    if hp == 4:
                        copy_product(layer, "z1", lambda t: zs[:, t, 512:1024], rms="x")
                    b = wait_bank(layer, f"cr{hp}")
                    act.wait_ge(*DV_.at(layer, f"cr{hp}"))
                    E = Ex[hp % 3]
                    for u in range(2):
                        act.activation(E[:, u, P:2 * P], b[:, (2 * u + 1) * P:(2 * u + 2) * P], ACT.Exp,
                                       bias=ncx[:, 2 * hp + u:2 * hp + u + 1]).then_inc(*AC.mark(f"cr{hp}"))
                    both = E.rearrange("p u (b t) -> p u b t", b=3)
                    for c in (0, 2):
                        act.activation(both[:, :, c, :], both[:, :, c, :], ACT.Exp).then_inc(*AC.mark(f"ex{hp}"))
                    if hp == 5:
                        split_until(layer, ORD[1].before["misc", "cr6"] + LOOK)
                        group_squares(0)
                operand(layer, "ssT0")
                operand(layer, "ssT1")
                split_until(layer, ORD[1].before["misc", f"y{SH // 2 - 1}"] + LOOK)
                act.wait_ge(*AC.at(layer, "z1.t1"))
                for t in range(NT):
                    act.activation(zs[:, t, 512:1024], zs[:, t, 512:1024], ACT.Silu).then_inc(*AC.mark("z1_silu"))
                group_squares(1)
                operand(layer, "ssT2")
                operand(layer, "ssT3")
                for i in range(4):
                    norm_operand(layer, f"mT{i}")
                squares(layer, "mT")
                feed_forward(layer)

            act.wait_ge(shifted, 1)
            act.activation(lbw[:, 0:8], lbw[:, 0:8], ACT.Exp).then_inc(lb_exp, 1)
            for block, body in enumerate((body_a, body_b)):
                if block == 1:
                    act.wait_ge(angles_in, 1)
                    act.activation(sinb, angs, ACT.Sin).then_inc(trig, 1)
                    act.activation(cosb, wrap, ACT.Sin).then_inc(trig, 1)
                with act.Fori(0, DEPTH) as l:
                    body((block, l))
                AC.end()
            for t in range(NT):
                act.wait_ge(*DV_.final(f"x_ffn{2 + t}"))
                act.activation(hrow[:, t, :], x[:, t, :], ACT.Square, scale=D ** -0.5, accum_out=small[:, t:t + 1])\
                    .then_inc(fin_ms, 1)

        @block_.vector
        def _(dve):
            split = [0]

            def split_until(layer, n, j=None):
                o = ORD[layer[0]]
                for s in range(split[0], min(n, o.slots)):
                    if s in POOL_LO[layer[0]]:
                        continue
                    dve.wait_ge(*name_at(AC, layer, "hi", s, j))
                    w = o.words(s)
                    dve.tensor_tensor(w_lo[:, s % RING, 0:w], w_raw[:, s % RING, 0:w],
                                      w_hi[:, s % RING, 0:w].bitcast(F32), ALU.subtract)\
                        .then_inc(*DV_.mark(slot_name(layer, "lo", s)))
                split[0] = max(split[0], min(n, o.slots))

            def wait_bank(layer, name):
                split_until(layer, ORD[layer[0]].before["misc", name] + LOOK)
                dve.wait_ge(*PE.at(layer, name))
                return misc[ORD[layer[0]].turn[name] % 4]

            def wait_product(layer, name):
                o = ORD[layer[0]]
                end = o.chunk_end(name)
                split_until(layer, end + LOOK)
                dve.wait_ge(*name_at(PE, layer, "used", end - 1))
                pair = o.pair[name]
                return acc if o.chunks[name].wide else acc[2 * pair:2 * pair + 2]

            def operand(layer, name):
                where, tile, n, scale = OPERANDS[layer[0]][name]
                split_until(layer, ORD[layer[0]].before["misc", name] + LOOK)
                dve.wait_ge(*AC.at(layer, f"hi.{name}"))
                b = misc[ORD[layer[0]].turn[name] % 4]
                hi, lo = (s[:, tile:tile + n, :].rearrange("p k t -> p (k t)") for s in stat[where])
                dve.scalar_tensor_tensor(out=lo, in0=b[:, 0:n * T], scalar=scale, in1=hi.bitcast(F32),
                                         op0=ALU.mult, op1=ALU.subtract).then_inc(*DV_.mark(name))

            def norm_operand(layer, name):
                kind, i = name[:2], int(name[2])
                split_until(layer, ORD[layer[0]].before["misc", name] + LOOK)
                b = misc[ORD[layer[0]].turn[name] % 4]
                dve.wait_ge(*AC.at(layer, f"hi.{name}"))
                for k in range(2):
                    dve.scalar_tensor_tensor(out=h_lo[:, 2 * i + k, :], in0=b[:, k * T:(k + 1) * T],
                                             scalar=gcol[:, kind == "mT", 2 * i + k:2 * i + k + 1],
                                             in1=h_hi[:, 2 * i + k, :].bitcast(F32), op0=ALU.mult,
                                             op1=ALU.subtract).then_inc(*DV_.mark(name))

            def row_max(layer, g, scale):
                block = layer[0]
                b = wait_bank(layer, f"S{g}")
                if g >= 2:
                    dve.wait_ge(*PE.at(layer, f"PT{g - 2}"))
                n, keys, off = (4, P, 0) if g < 2 else (2, T, P)
                base = (C_BIASA, C_BIASB)[block] + off
                v = Sx[block][:, g % 2, :].rearrange("p (h k) -> p h k", h=n)
                bias = const[:, base:base + keys].rearrange("p (a k) -> p a k", a=1)
                dve.tensor_tensor(v, b[:, :].rearrange("p (h k) -> p h k", h=n), bc(bias, [P, n, keys]), ALU.add)\
                    .then_inc(*DV_.mark(f"Sread{g}"))
                c = (g % 4) * 4
                dve.wait_ge(*DV_.now(layer))
                dve.tensor_reduce(small[:, 128 + c:128 + c + n], v, AX.X, ALU.max).then_inc(*DV_.mark())
                dve.wait_ge(*DV_.now(layer))
                dve.tensor_scalar(small[:, 144 + c:144 + c + n], small[:, 128 + c:128 + c + n], -scale, None,
                                  ALU.mult).then_inc(*DV_.mark(f"S{g}"))

            def weighed(layer, g):
                block = layer[0]
                n, c = (4 if g < 2 else 2), (g % 4) * 4
                dve.wait_ge(*AC.at(layer, f"p{g}"))
                dve.reciprocal(small[:, 176 + c:176 + c + n], small[:, 160 + c:160 + c + n]).then_inc(*DV_.mark())
                b = wait_bank(layer, f"O{g}")
                dve.wait_ge(*DV_.now(layer))
                t, h0 = (0, 4 * g) if g < 2 else (1, 2 * g - 4)
                dst = att[block][:, t, h0 * 64:(h0 + n) * 64].rearrange("p (h d) -> p h d", h=n)
                r = small[:, 176 + c:176 + c + n].rearrange("p (h a) -> p h a", a=1)
                dve.tensor_tensor(dst, b[:, 0:n * 64].rearrange("p (h d) -> p h d", h=n), bc(r, [P, n, 64]), ALU.mult)\
                    .then_inc(*DV_.mark(f"O{g}"))

            def rotate(layer, x1, x2, cos, sin, scratch, name):
                a, b_, c, d = scratch
                for dst, u, v in ((a, x1, cos), (b_, x2, sin), (c, x1, sin), (d, x2, cos)):
                    dve.tensor_tensor(dst, u, v, ALU.mult).then_inc(*DV_.mark())
                dve.wait_ge(*DV_.now(layer))
                dve.tensor_tensor(x1, a, b_, ALU.subtract).then_inc(*DV_.mark())
                dve.tensor_tensor(x2, c, d, ALU.add).then_inc(*DV_.mark(name))

            def residual(layer, banks, names):
                for (half, t, b), name in zip(banks, names):
                    v = x[:, t, half * 512:half * 512 + 512]
                    dve.tensor_tensor(v, v, b[:, :], ALU.add).then_inc(*DV_.mark(name))

            def feed_forward(layer):
                o = ORD[layer[0]]

                def gated(s_end, step, j=None):
                    split_until(layer, s_end + LOOK, j)
                    for t in range(NT):
                        dve.wait_ge(*AC.at(layer, f"f{step}.t{t}", j))
                        b = acc[t] if step == "0" else misc[2 + t]
                        c = RS + M_Y + t
                        dve.scalar_tensor_tensor(out=f_act[:, t, :], in0=b[:, FW:2 * FW], scalar=small[:, c:c + 1],
                                                 in1=f_silu[:, t, :], op0=ALU.mult, op1=ALU.mult)\
                            .then_inc(*DV_.mark(f"f{step}"))

                def turned(s_end, step, j=None):
                    split_until(layer, s_end + LOOK, j)
                    dve.wait_ge(*AC.at(layer, f"fT{step}", j))
                    at = 2 if step == "10" else 0
                    hi, lo = (s[:, at:at + 2, :].rearrange("p k t -> p (k t)") for s in stat["st"])
                    dve.tensor_tensor(lo, misc[0][:, :], hi.bitcast(F32), ALU.subtract)\
                        .then_inc(*DV_.mark(f"fT{step}"))

                s = o.ffn0
                gated(s + 3, "0")
                turned(s + 4, "0")
                gated(s + 8, "1")
                turned(s + 10, "1")
                s += LOOP_AT
                DV_.loop(None)
                with dve.Fori(0, LOOP_TIMES) as j:
                    gated(s + 4, "2", j)
                    turned(s + 6, "2", j)
                    gated(s + 10, "3", j)
                    turned(s + 12, "3", j)
                DV_.loop(LOOP_TIMES)
                split[0] += LOOP_SLOTS * (LOOP_TIMES - 1)
                s += LOOP_SLOTS * LOOP_TIMES
                gated(s + 4, "10")
                turned(s + 6, "10")
                split_until(layer, o.slots)
                split[0] = 0
                for half, step in enumerate(("x_half", "used-1")):
                    dve.wait_ge(*PE.at(layer, step))
                    residual(layer, [(half, t, acc[2 * half + t]) for t in range(NT)],
                             [f"x_ffn{2 * half + t}" for t in range(NT)])

            def level(layer, i):
                h = 1 << (i - 1)
                Q, K, D1, R, Y = (v.rearrange("p (b u h) -> p b u h", u=2, h=h)
                                  for v in (hQ, hK, hP, hR, X[:, i % 2, :]))
                if i >= 2:
                    dve.wait_ge(*PO.at(layer, f"D{i - 1}"))
                if i >= 3:
                    dve.wait_ge(*PE.at(layer, f"G{i - 2}_1"))
                dve.tensor_tensor(Y[:, :, 1, :], Q[:, :, 1, :], D1[:, :, 1, :], ALU.mult).then_inc(*DV_.mark())
                dve.tensor_tensor(Y[:, :, 0, :], K[:, :, 0, :], R[:, :, 0, :], ALU.mult).then_inc(*DV_.mark(f"X{i}"))

            def body_a(layer):
                sc = float(DQK) ** -0.5
                l = layer[1]
                dve.wait_ge(c_in, 32)
                dve.wait_ge(*par_at(layer))
                dve.tensor_copy(lbc[:, 0, :], lbs[:, bass.ds(l, 1), :].rearrange("p a h -> p (a h)"))\
                    .then_inc(*DV_.mark())
                dve.wait_ge(*DV_.now(layer))
                dve.tensor_scalar(lbc[:, 1, :], lbc[:, 0, :], -1.0, 1.0, ALU.mult, ALU.add).then_inc(*DV_.mark())
                for i in range(4):
                    norm_operand(layer, f"nT{i}")
                split_until(layer, ORD[0].chunk_end("mla1") + LOOK)
                dve.wait_ge(*PO.at(layer, "r.c"))
                for t in range(NT):
                    for col, a, n, g in ((M_CQ, 0, QL, G_CQ), (M_CKV, QL, KVL, G_CKV)):
                        v = zm[:, t, a:a + n]
                        dve.scalar_tensor_tensor(out=v, in0=v, scalar=small[:, RS + col + t:RS + col + t + 1],
                                                 in1=gains[:, g:g + n], op0=ALU.mult, op1=ALU.mult)\
                            .then_inc(*DV_.mark("cnorm"))
                for i in range(3):
                    operand(layer, f"cT{i}")
                split_until(layer, ORD[0].before["misc", "hfT1"] + LOOK)
                dve.wait_ge(*AC.at(layer, "hfT1"))
                for hd in range(HG):
                    cols = slice(hd * T, (hd + 1) * T)
                    lb, om = lbc[:, 0, hd:hd + 1], lbc[:, 1, hd:hd + 1]
                    dve.tensor_scalar(hP[:, cols], hP[:, cols], om, lb, ALU.mult, ALU.add).then_inc(*DV_.mark())
                    dve.tensor_scalar(hK[:, cols], hK[:, cols], om, None, ALU.mult).then_inc(*DV_.mark())
                dve.memset(hR[:, :], 1.0).then_inc(*DV_.mark("X0"))
                split_until(layer, ORD[0].chunk_end("hg") + LOOK)
                for t in range(NT):
                    dve.wait_ge(*AC.at(layer, f"hg.t{t}"))
                    dve.scalar_tensor_tensor(out=sg[:, t, :], in0=sg[:, t, :], scalar=1.0, in1=zq[:, t, :],
                                             op0=ALU.add, op1=ALU.mult).then_inc(*DV_.mark(f"hg.t{t}"))
                split_until(layer, ORD[0].chunk_end("ukv1") + LOOK)
                dve.wait_ge(*AC.at(layer, "kpe"))
                level(layer, 1)
                end = ORD[0].chunk_end("ukv1") + LOOK
                for t in range(NT):
                    split_until(layer, end - 1 + t)
                    dve.wait_ge(*AC.at(layer, f"sq{t}"))
                    c = M_QK + 16 * t
                    dve.tensor_reduce(small[:, c:c + 16], sq[:, t, :, :], AX.X, ALU.add)\
                        .then_inc(*DV_.mark(f"ms.qk{t}"))
                for t in range(NT):
                    split_until(layer, end + 1 + 2 * t)
                    for u in range(2):
                        v = QK[:, t, 8 * u:8 * u + 8, NOPE:DQK]
                        g = gains[:, G_QK + DQK * u + NOPE:G_QK + DQK * (u + 1)].rearrange("p (a d) -> p a d", a=1)
                        dve.tensor_tensor(v, v, bc(g, [P, 8, DQK - NOPE]), ALU.mult).then_inc(*DV_.mark())
                    dve.wait_ge(*DV_.now(layer))
                    cos, sin = (bc(const[:, c0 + 16 * t:c0 + 16 * t + 16].rearrange("p (a d) -> p a d", a=1),
                                   [P, 16, 16]) for c0 in (C_COS, C_SIN))
                    rotate(layer, QK[:, t, :, NOPE:NOPE + 16], QK[:, t, :, NOPE + 16:DQK], cos, sin,
                           [rope[0][:, i, :, :] for i in range(4)], None)
                    dve.wait_ge(*DV_.now(layer))
                split_until(layer, end + 5)
                for t in range(NT):
                    c = RS + M_QK + 16 * t
                    dve.wait_ge(*PO.at(layer, f"r.qk{t}"))
                    r = small[:, c:c + 16].rearrange("p (h a) -> p h a", a=1)
                    dve.tensor_tensor(QK[:, t, :, :], QK[:, t, :, :], bc(r, [P, 16, DQK]), ALU.mult)\
                        .then_inc(*DV_.mark(f"qk{t}"))
                for i in range(8):
                    if i + 1 >= 2:
                        split_until(layer, ORD[0].before["misc", f"G{i}_0"] + LOOK)
                        level(layer, i + 1)
                    if 2 <= i < 8:
                        weighed(layer, i - 2)
                    if i == 0:
                        row_max(layer, 0, sc)
                        row_max(layer, 1, sc)
                    elif i < 5:
                        row_max(layer, i + 1, sc)
                    for pr in range(2):
                        split_until(layer, ORD[0].before["misc", f"G{i}_{pr}"] + LOOK)
                        b = wait_bank(layer, f"G{i}_{pr}")
                        dst = AT[:, 2 * pr:2 * pr + 2, 0:2, :]
                        src = b[:, :].rearrange("p (a b q) -> p a b q", a=2, b=2)
                        if i == 0:
                            for u in range(2):
                                dve.tensor_tensor(dst[:, u, :, :], src[:, u, :, :],
                                                  bc(ident.rearrange("p (b q) -> p b q", b=1), [P, 2, P]), ALU.mult)\
                                    .then_inc(*DV_.mark(f"G{i}_{pr}"))
                        else:
                            dve.tensor_copy(lbw[:, 0:1], b[:, 0:1]).then_inc(*DV_.mark())
                            m = masks[:, i, :].rearrange("p (a b q) -> p a b q", a=1, b=1)
                            dve.copy_predicated(out=dst, mask=bc(m, [P, 2, 2, P]), data=src)\
                                .then_inc(*DV_.mark(f"G{i}_{pr}"))
                        dve.wait_ge(*DV_.now(layer))
                operand(layer, "attT0")
                operand(layer, "attT1")
                dve.wait_ge(*PO.at(layer, "sgg"))
                for t in range(NT):
                    b = wait_bank(layer, f"oH{t}")
                    c = RS + M_HG + 4 * t
                    dve.wait_ge(*PO.at(layer, f"r.h{t}"))
                    r = small[:, c:c + 4].rearrange("p (h a) -> p h a", a=1)
                    dve.tensor_tensor(oh[:, t, :].rearrange("p (h d) -> p h d", h=HG),
                                      b[:, :].rearrange("p (h d) -> p h d", h=HG), bc(r, [P, HG, DK]), ALU.mult)\
                        .then_inc(*DV_.mark(f"oH{t}"))
                    dve.wait_ge(*DV_.now(layer))
                    dve.tensor_tensor(oh[:, t, :], oh[:, t, :], sg[:, t, :], ALU.mult).then_inc(*DV_.mark(f"oh{t}"))
                def gated_sum(name, i, off):
                    banks = wait_product(layer, f"{name}{i}")
                    for t in range(NT):
                        v = gate[:, t, off + 512 * i:off + 512 * i + 512]
                        dve.scalar_tensor_tensor(out=v, in0=v, scalar=1.0, in1=banks[t][:, :],
                                                 op0=ALU.add, op1=ALU.mult).then_inc(*DV_.mark(f"{name}{i}.t{t}"))
                dve.wait_ge(*AC.at(layer, "gate3.t1"))
                gated_sum("pa", 0, 0)
                operand(layer, "hgT0")
                operand(layer, "hgT1")
                gated_sum("pa", 1, 0)
                for i in range(2):
                    gated_sum("pb", i, D)
                    dve.wait_ge(*DV_.now(layer))
                    for t in range(NT):
                        v = gate[:, t, 512 * i:512 * i + 512]
                        dve.tensor_tensor(v, v, gate[:, t, D + 512 * i:D + 512 * i + 512], ALU.add)\
                            .then_inc(*DV_.mark(f"y{i}"))
                    operand(layer, f"yT{2 * i}")
                    operand(layer, f"yT{2 * i + 1}")
                for i in range(2):
                    banks = wait_product(layer, f"wo{i}")
                    residual(layer, [(i, t, banks[t]) for t in range(NT)], [f"wo{i}.t{t}" for t in range(NT)])
                for i in range(4):
                    norm_operand(layer, f"mT{i}")
                feed_forward(layer)

            def body_b(layer):
                sc = float(DB) ** -0.5
                dve.wait_ge(*par_at(layer))
                for i in range(4):
                    norm_operand(layer, f"nT{i}")
                dve.memset(xc[:, :, 0:TAPS - 1], 0.0).then_inc(*DV_.mark("pad"))
                b = wait_bank(layer, "cvT0")
                dve.tensor_copy(conv[:, 0:48], b[:, 0:48]).then_inc(*DV_.mark("cvT0"))
                b = wait_bank(layer, "cvT1")
                dve.tensor_copy(conv[:, 48:60], b[:, 48:60]).then_inc(*DV_.mark("cvT1"))
                split_until(layer, ORD[1].chunk_end("qkv2") + LOOK)
                dve.wait_ge(*AC.at(layer, "qkv2.t1"))
                qk = zqkv[:, :, 0:640].rearrange("p t (h d) -> p t h d", h=10)
                cos, sin = (bc(v.rearrange("p (t a d) -> p t a d", t=NT, a=1), [P, NT, 10, 8]) for v in (cosb, sinb))
                dve.wait_ge(trig, 2)
                rotate(layer, qk[:, :, :, 0:8], qk[:, :, :, 8:16], cos, sin,
                       [rope[1][:, i, :, :].rearrange("p (t h) d -> p t h d", t=NT) for i in range(4)], "qk")

                def convolve(i):
                    split_until(layer, ORD[1].before["misc", f"xT{i}"] + LOOK)
                    dve.wait_ge(*AC.at(layer, f"xT{i}"))
                    for k in (2 * i, 2 * i + 1):
                        dve.tensor_scalar(cv[:, k, :], xc[:, k, 3:3 + T], conv[:, 36 + k:37 + k],
                                          conv[:, 48 + k:49 + k], ALU.mult, ALU.add).then_inc(*DV_.mark())
                    for tap in range(3):
                        dve.wait_ge(*DV_.now(layer))
                        for k in (2 * i, 2 * i + 1):
                            dve.scalar_tensor_tensor(out=cv[:, k, :], in0=xc[:, k, tap:tap + T],
                                                     scalar=conv[:, 12 * tap + k:12 * tap + k + 1],
                                                     in1=cv[:, k, :], op0=ALU.mult, op1=ALU.add)\
                                .then_inc(*DV_.mark(f"conv{i}"))

                row_max(layer, 0, sc)
                row_max(layer, 1, sc)
                row_max(layer, 2, sc)
                weighed(layer, 0)
                row_max(layer, 3, sc)
                convolve(0)
                weighed(layer, 1)
                row_max(layer, 4, sc)
                weighed(layer, 2)
                row_max(layer, 5, sc)
                weighed(layer, 3)
                convolve(1)
                weighed(layer, 4)
                weighed(layer, 5)
                operand(layer, "attT0")
                operand(layer, "attT1")
                convolve(2)
                convolve(3)
                split_until(layer, ORD[1].chunk_end("xd3") + LOOK)
                dve.wait_ge(*AC.at(layer, "xd3.t1"))
                v3 = [v.rearrange("p (t h) -> p t h", t=NT) for v in (dt_u, dt_m, dt_v, dt_a)]
                one_row = prm[:, 0:16].rearrange("p (a h) -> p a h", a=1)
                dve.tensor_tensor(v3[0], xd[:, :, XBC:XD], bc(one_row, [P, NT, 16]), ALU.add).then_inc(*DV_.mark())
                dve.wait_ge(*DV_.now(layer))
                dve.tensor_scalar(dt_m, dt_u, 0.0, None, ALU.max).then_inc(*DV_.mark())
                dve.tensor_scalar(dt_a, dt_u, -1.0, None, ALU.mult).then_inc(*DV_.mark())
                dve.wait_ge(*DV_.now(layer))
                dve.tensor_tensor(dt_v, dt_u, dt_a, ALU.min).then_inc(*DV_.mark("dt_u"))
                convolve(4)
                dve.wait_ge(*AC.at(layer, "dt_ln"))
                dve.tensor_tensor(dt_m, dt_m, dt_v, ALU.add).then_inc(*DV_.mark("dt"))
                dve.wait_ge(*DV_.now(layer))
                ea3 = bc(ea.rearrange("p (a h) -> p a h", a=1), [P, NT, 16])
                dve.scalar_tensor_tensor(out=v3[3], in0=v3[1], scalar=-1.0, in1=ea3, op0=ALU.mult, op1=ALU.mult)\
                    .then_inc(*DV_.mark("dt_a"))
                convolve(5)
                for i in range(4):
                    t, half = i // 2, i % 2
                    split_until(layer, ORD[1].before["misc", f"xsT{i}"] + LOOK)
                    dve.wait_ge(*AC.at(layer, f"xs{i}"))
                    b = misc[ORD[1].turn[f"xsT{i}"] % 4]
                    r = dt_m[:, 16 * t + 8 * half:16 * t + 8 * half + 8].rearrange("p (h a) -> p h a", a=1)
                    dve.tensor_tensor(xdt[:, t, 512 * half:512 * half + 512].rearrange("p (h d) -> p h d", h=8),
                                      b[:, :].rearrange("p (h d) -> p h d", h=8), bc(r, [P, 8, SP]), ALU.mult)\
                        .then_inc(*DV_.mark(f"xsT{i}"))
                for g in range(2):
                    b = wait_bank(layer, f"cb{g}")
                    dve.tensor_tensor(cbm[:, g, 0:P], b[:, 0:P], tri, ALU.mult).then_inc(*DV_.mark())
                    dve.tensor_copy(cbm[:, g, P:2 * P], b[:, P:2 * P]).then_inc(*DV_.mark())
                    dve.tensor_tensor(cbm[:, g, 2 * P:3 * P], b[:, 2 * P:3 * P], tri, ALU.mult)\
                        .then_inc(*DV_.mark(f"cb{g}"))
                b = wait_bank(layer, "cs")
                dve.tensor_copy(cs, b[:, 0:48]).then_inc(*DV_.mark("cs"))
                dve.wait_ge(*DV_.now(layer))
                dve.tensor_tensor(ncx, cs[:, 32:48], cs[:, 0:16], ALU.subtract).then_inc(*DV_.mark())

                def head_pair_out(hp):
                    b = wait_bank(layer, f"y{hp}")
                    cols = slice(2 * hp * SP, (2 * hp + 2) * SP)
                    dve.tensor_tensor(ys[:, :, cols], b[:, 0:T].rearrange("p (t c) -> p t c", t=NT), xs[:, :, cols],
                                      ALU.add).then_inc(*DV_.mark(f"y{hp}"))

                def exponents(hp):
                    b = wait_bank(layer, f"cr{hp}")
                    if hp >= 3:
                        dve.wait_ge(*PE.at(layer, f"y{hp - 3}"))
                    for u in range(2):
                        hd = 2 * hp + u
                        for t in range(NT):
                            dve.tensor_scalar(Ex[hp % 3][:, u, 2 * t * P:(2 * t + 1) * P],
                                              b[:, (2 * u + t) * P:(2 * u + t + 1) * P],
                                              cs[:, 16 * t + hd:16 * t + hd + 1], 0.0, ALU.subtract, ALU.min)\
                                .then_inc(*DV_.mark(f"cr{hp}"))

                def times_silu(g):
                    dve.wait_ge(*DV_.now(layer))
                    dve.wait_ge(*AC.at(layer, ("z0.t1", "z1_silu")[g]))
                    v, z = (u[:, :, 512 * g:512 * g + 512] for u in (ys, zs))
                    dve.tensor_tensor(v, v, z, ALU.mult).then_inc(*DV_.mark(f"ysz{g}"))

                def normalised(g):
                    dve.wait_ge(*PO.at(layer, f"r.s{g}"))
                    for t in range(NT):
                        c = RS + M_HG + 2 * g + t
                        v = ys[:, t, 512 * g:512 * g + 512]
                        dve.scalar_tensor_tensor(out=v, in0=v, scalar=small[:, c:c + 1],
                                                 in1=gains[:, G_SSM + 512 * g:G_SSM + 512 * g + 512],
                                                 op0=ALU.mult, op1=ALU.mult).then_inc(*DV_.mark(f"ys{g}"))

                exponents(0)
                dve.wait_ge(*PO.at(layer, "xsd"))
                for hp in range(SH // 2):
                    if hp + 1 < SH // 2:
                        exponents(hp + 1)
                    dve.wait_ge(*AC.at(layer, f"ex{hp}"))
                    g = cbm[:, hp // 4, :].rearrange("p (a k) -> p a k", a=1)
                    dve.tensor_tensor(Ex[hp % 3], Ex[hp % 3], bc(g, [P, 2, 384]), ALU.mult)\
                        .then_inc(*DV_.mark(f"M{hp}"))
                    if hp >= 1 and hp < SH // 2 - 1:
                        head_pair_out(hp - 1)
                    if hp == 4:
                        times_silu(0)
                    if hp == 5:
                        normalised(0)
                operand(layer, "ssT0")
                operand(layer, "ssT1")
                head_pair_out(SH // 2 - 2)
                head_pair_out(SH // 2 - 1)
                times_silu(1)
                normalised(1)
                operand(layer, "ssT2")
                operand(layer, "ssT3")
                for i in range(2):
                    banks = wait_product(layer, f"wo{i}")
                    residual(layer, [(i, t, banks[t]) for t in range(NT)], [f"wo{i}.t{t}" for t in range(NT)])
                for i in range(4):
                    norm_operand(layer, f"mT{i}")
                feed_forward(layer)

            dve.memset(small[:, 192:193], -0.5).then_inc(DV_.sem, DV_.seed())
            dve.memset(small[:, 193:194], -0.5).then_inc(PE.sem, PE.seed())
            dve.memset(small[:, 194:195], -0.5).then_inc(AC.sem, AC.seed())
            dve.memset(small[:, 195:208], -0.5).then_inc(PO.sem, PO.seed())
            dve.memset(gqk[NOPE:DQK, :], 1.0).then_inc(chain, 1)
            dve.memset(rows[:, :], 0.0).then_inc(rows_0, 1)
            dve.memset(halves[:, :], 0.5).then_inc(rows_0, 1)
            dve.memset(epsilons[:, 0:16], EPS_A).then_inc(chain, 1)
            dve.memset(epsilons[:, 16:32], EPS_B).then_inc(chain, 1)
            dve.wait_ge(c_in, 32)
            n = [3]

            def link(ins):
                ins.then_inc(chain, 1)
                n[0] += 1
                dve.wait_ge(chain, n[0])

            link(dve.tensor_copy(masks[:, :, :], carve(0, 8, P)))
            dve.wait_ge(lb_T, 1)
            link(dve.tensor_copy(lbw[:, 0:8], misc[3][:, 0:8]))
            link(dve.tensor_tensor(lbw[:, 8:12], lbw[:, 0:4], lbw[:, 4:8], ALU.max))
            link(dve.tensor_tensor(lbw[:, 0:4], lbw[:, 0:4], lbw[:, 8:12], ALU.subtract))
            dve.tensor_tensor(lbw[:, 4:8], lbw[:, 4:8], lbw[:, 8:12], ALU.subtract).then_inc(shifted, 1)
            dve.wait_ge(pos_in, 16)
            link(dve.tensor_copy(posf, posi[:, :]))
            for t in range(NT):
                link(dve.tensor_scalar(dt_u[:, 8 * t:8 * t + 8], const[:, C_INV:C_INV + 8], posf[:, t:t + 1], None,
                                       ALU.mult))
            ang = dt_u[:, 0:16]
            magic = 1.5 * 2.0 ** 23
            tau_parts = (6.28125, 0.0019350051879882812, 3.019916050561733e-07)
            for dst, quarter in ((angs, 0.0), (wrap, 0.25)):
                link(dve.tensor_scalar(turns_, ang, 1.0 / (2.0 * math.pi), quarter, ALU.mult, ALU.add))
                link(dve.tensor_scalar(turns_, turns_, magic, None, ALU.add))
                link(dve.tensor_scalar(turns_, turns_, -magic, None, ALU.add))
                link(dve.tensor_copy(dst, ang))
                for part in tau_parts:
                    link(dve.scalar_tensor_tensor(out=dst, in0=turns_, scalar=-part, in1=dst, op0=ALU.mult,
                                                  op1=ALU.add))
                if quarter:
                    link(dve.tensor_scalar(dst, dst, math.pi / 2, None, ALU.add))
                last = dve.tensor_scalar(dst, dst, 3.1415925, -3.1415925, ALU.min, ALU.max)
                if quarter:
                    last.then_inc(angles_in, 1)
                else:
                    link(last)
            dve.wait_ge(lb_exp, 1)
            link(dve.tensor_tensor(lbw[:, 8:12], lbw[:, 0:4], lbw[:, 4:8], ALU.add))
            link(dve.reciprocal(lbw[:, 8:12], lbw[:, 8:12]))
            link(dve.tensor_tensor(lbw[:, 0:4], lbw[:, 0:4], lbw[:, 8:12], ALU.mult))
            link(dve.tensor_tensor(lbw[:, 4:8], lbw[:, 4:8], lbw[:, 8:12], ALU.mult))
            link(dve.tensor_tensor(lbs[:, 0, :], lbw[:, 0:4], lbw[:, 0:4], ALU.subtract))
            link(dve.tensor_tensor(lbw[:, 12:16], lbw[:, 0:4], lbw[:, 4:8], ALU.add))
            link(dve.tensor_tensor(lbw[:, 12:16], lbw[:, 12:16], lbw[:, 0:4], ALU.subtract))
            link(dve.tensor_scalar(lbs[:, 1, :], lbw[:, 12:16], 0.0, None, ALU.max))
            for block, body in enumerate((body_a, body_b)):
                with dve.Fori(0, DEPTH) as l:
                    body((block, l))
                DV_.end()
            dve.wait_ge(fin_in, 16)
            for t in range(NT):
                dve.wait_ge(fin_r, 2 * t + 2)
                dve.scalar_tensor_tensor(out=hrow[:, t, :], in0=x[:, t, :], scalar=small[:, RS + t:RS + t + 1],
                                         in1=gains[:, 0:D], op0=ALU.mult, op1=ALU.mult).then_inc(fin_rows, 1)

        @block_.gpsimd
        def _(pool):
            def inverse_rms(layer, col, n, name, eps):
                pool.tensor_tensor(small[:, RS + col:RS + col + n], small[:, col:col + n],
                                   epsilons[:, 16 * eps:16 * eps + n], ALU.add).then_inc(*PO.mark())
                pool.wait_ge(*PO.now(layer))
                pool.tensor_tensor(small[:, RS + col:RS + col + n], small[:, RS + col:RS + col + n],
                                   small[:, 192:192 + n], ALU.pow).then_inc(*PO.mark(name))

            split = [0]

            def split_until(layer, n):
                for s in range(split[0], n):
                    if s in POOL_LO[layer[0]]:
                        pool.wait_ge(*name_at(AC, layer, "hi", s))
                        w = ORD[layer[0]].words(s)
                        pool.tensor_tensor(w_lo[:, s % RING, 0:w], w_raw[:, s % RING, 0:w],
                                           w_hi[:, s % RING, 0:w].bitcast(F32), ALU.subtract)\
                            .then_inc(*PO.mark(slot_name(layer, "lo", s)))
                split[0] = max(split[0], n)

            def decay(layer, i):
                h = 1 << (i - 1)
                D1, R = (v.rearrange("p (b u h) -> p b u h", u=2, h=h) for v in (hP, hR))
                n = 1024 // (2 * h)
                pool.wait_ge(*DV_.at(layer, f"X{i}"))
                pool.tensor_tensor(R[:, :, 0, :], R[:, :, 0, :], bc(D1[:, :, 1, h - 1:h], [P, n, h]), ALU.mult)\
                    .then_inc(*PO.mark())
                pool.wait_ge(*PO.now(layer))
                pool.tensor_tensor(D1[:, :, 1, :], D1[:, :, 1, :], bc(D1[:, :, 0, h - 1:h], [P, n, h]), ALU.mult)\
                    .then_inc(*PO.mark(f"D{i}"))

            def body_a(layer):
                o = ORD[0]
                split[0] = 0
                split_until(layer, LOOK)
                pool.wait_ge(*AC.at(layer, "ms.nT"))
                inverse_rms(layer, M_X, 2, None, 0)
                pool.wait_ge(*PO.now(layer))
                pool.tensor_tensor(small[:, RS + M_H:RS + M_H + 2], small[:, RS + M_X:RS + M_X + 2],
                                   halves[:, 0:2], ALU.mult).then_inc(*PO.mark("r.nT"))
                split_until(layer, o.chunk_end("mla1") + LOOK)
                pool.wait_ge(*AC.at(layer, "ms.c"))
                inverse_rms(layer, M_CQ, 4, "r.c", 0)
                pool.wait_ge(*par_at(layer))
                for t in range(NT):
                    split_until(layer, o.chunk_end("hg") + LOOK)
                    pool.wait_ge(*DV_.at(layer, f"hg.t{t}"))
                    v = sg[:, t, :].rearrange("p (h d) -> p h d", h=HG)
                    g = gains[:, G_HG:G_HG + DK].rearrange("p (a d) -> p a d", a=1)
                    pool.tensor_tensor(v, v, bc(g, [P, HG, DK]), ALU.mult).then_inc(*PO.mark("sgg"))
                for t in range(NT):
                    split_until(layer, o.chunk_end("ukv1") + LOOK + t)
                    pool.wait_ge(*DV_.at(layer, f"ms.qk{t}"))
                    c = M_QK + 16 * t
                    inverse_rms(layer, c, 16, f"r.qk{t}", 0)
                for i in range(1, 8):
                    split_until(layer, o.before["misc", f"G{i - 1}_0"] + LOOK if i > 1 else
                                o.chunk_end("gate1") - 1)
                    decay(layer, i)
                for t in range(NT):
                    split_until(layer, o.before["misc", f"oH{t}"] + LOOK)
                    pool.wait_ge(*AC.at(layer, f"ms.h{t}"))
                    c = M_HG + 4 * t
                    inverse_rms(layer, c, 4, f"r.h{t}", 0)
                pool.wait_ge(*AC.at(layer, "ms.mT"))
                inverse_rms(layer, M_Y, 2, "r.mT", 0)

            def body_b(layer):
                o = ORD[1]
                split[0] = 0
                split_until(layer, LOOK)
                pool.wait_ge(*AC.at(layer, "ms.nT"))
                inverse_rms(layer, M_X, 2, "r.nT", 1)
                pool.wait_ge(*par_at(layer))
                for i in range(4):
                    t, half = i // 2, i % 2
                    split_until(layer, o.before["misc", f"xsT{i}"] + LOOK)
                    pool.wait_ge(*AC.at(layer, f"xs{i}"))
                    v = xs[:, t, 512 * half:512 * half + 512].rearrange("p (h d) -> p h d", h=8)
                    dsk = prm[:, 32 + 8 * half:40 + 8 * half].rearrange("p (h a) -> p h a", a=1)
                    pool.tensor_tensor(v, v, bc(dsk, [P, 8, SP]), ALU.mult).then_inc(*PO.mark("xsd"))
                for g in range(2):
                    split_until(layer, o.before["misc", ("cr5", "y7")[g]] + LOOK)
                    pool.wait_ge(*AC.at(layer, f"ms.s{g}"))
                    inverse_rms(layer, M_HG + 2 * g, 2, f"r.s{g}", 1)
                pool.wait_ge(*AC.at(layer, "ms.mT"))
                inverse_rms(layer, M_Y, 2, "r.mT", 1)

            for block, body in enumerate((body_a, body_b)):
                with pool.Fori(0, DEPTH) as l:
                    body((block, l))
                PO.end()
            for t in range(NT):
                r = small[:, RS + t:RS + t + 1]
                pool.wait_ge(fin_ms, t + 1)
                pool.tensor_tensor(r, small[:, t:t + 1], epsilons[:, 16:17], ALU.add).then_inc(fin_r, 1)
                pool.wait_ge(fin_r, 2 * t + 1)
                pool.tensor_tensor(r, r, small[:, 192:193], ALU.pow).then_inc(fin_r, 1)


def constants():
    q, k = np.arange(P)[None, :], np.arange(P)[:, None]
    const = np.zeros((P, C_END), np.float32)
    const[:, C_ID:C_ID + P] = np.eye(P)
    const[:, C_TRI:C_TRI + P] = k <= q
    rows, low = np.arange(P)[:, None], np.float32(-1e30)
    scale_b = float(DB) ** -0.5
    for tile, at, keys in ((0, 0, P), (1, P, T)):
        delta = (rows + tile * P) - np.arange(keys)[None, :]
        const[:, C_BIASA + at:C_BIASA + at + keys] = np.where(delta >= 0, 0.0, low)
        times = sum(((delta >= 0) & (delta <= w) & (delta % d == 0)).astype(int)
                    for w, d in ((128, 1), (512, 4), (2048, 16)))
        const[:, C_BIASB + at:C_BIASB + at + keys] = np.where(
            times > 0, np.log(np.maximum(times, 1)) / scale_b, low)
    inv = (1.0 / (np.float32(10000.0) ** (np.arange(0, RA, 2, dtype=np.float32) / RA))).astype(np.float32)
    ang = np.arange(T, dtype=np.float32)[:, None] * inv[None, :]
    for t in range(NT):
        const[:, C_COS + 16 * t:C_COS + 16 * t + 16] = np.cos(ang[t * P:(t + 1) * P])
        const[:, C_SIN + 16 * t:C_SIN + 16 * t + 16] = np.sin(ang[t * P:(t + 1) * P])
    const[:, C_INV:C_INV + 8] = np.float32(500000.0) ** (-np.arange(0, RB, 2, dtype=np.float32) / RB)
    masks = np.zeros((P, 8, P), np.float32)
    masks[:, 0, :] = np.eye(P)
    for i in range(1, 8):
        h = 1 << (i - 1)
        masks[:, i, :] = (k // (2 * h) == q // (2 * h)) & (k // h % 2 == 0) & (q // h % 2 == 1)
    return const, masks


FLAT = {"w_in": IN_A, "mla_w_uq": HA * DQK, "mla_w_ukv": HA * (NOPE + DV), "w_proj_a": D, "w_proj_b": D,
        "w_out": D, "w_gate": FF, "w_up": FF, "w_down": D, "w_in_2": IN_B, "w_out_2": D, "w_gate_2": FF,
        "w_up_2": FF, "w_down_2": D, "x": D, "conv_w_2": P, "conv_b_2": P}
NAMES = ["x", "norm_mix", "w_in", "mla_norm_cq", "mla_w_uq", "mla_norm_ckv", "mla_w_ukv", "mla_q_norm",
         "mla_k_norm", "hg_lb_logits", "hg_out_norm", "w_proj_a", "w_proj_b", "w_out", "norm_ffn", "w_gate",
         "w_up", "w_down", "positions_2", "norm_mix_2", "w_in_2", "conv_w_2", "conv_b_2", "dt_bias_2", "a_log_2",
         "d_skip_2", "ssm_norm_2", "w_out_2", "norm_ffn_2", "w_gate_2", "w_up_2", "w_down_2", "final_norm_2"]


def program(nc, arrays, table):
    A = {name: nc.dram_tensor(f"in_{name}", a.shape, mybir.dt.from_np(a.dtype), kind="ExternalInput").ap()
         for name, a in arrays.items()}
    out = nc.dram_tensor("out_0", (T, D), F32, kind="ExternalOutput").ap()
    build(nc, A, out, table)


def kernel(**inputs):
    import concourse.bacc as bacc
    from concourse.bass_utils import run_bass_kernel_spmd

    arrays = {}
    for name in NAMES:
        a = np.ascontiguousarray(inputs[name])
        if name in FLAT:
            a = a.reshape(-1, FLAT[name])
        elif name == "positions_2":
            a = a.reshape(-1)
        arrays[name] = a
    arrays["const"], arrays["masks"] = constants()
    table = {}
    for _ in range(2):
        nc = bacc.Bacc("TRN2", target_bir_lowering=False, num_devices=1)
        program(nc, arrays, table)
    r = run_bass_kernel_spmd(nc, [{f"in_{name}": a for name, a in arrays.items()}], core_ids=[0])
    return r.results[0]["out_0"].reshape(1, T, D)
```
